# Optimizing a Trainium2 kernel written in Bass

```python
import jax, jax.numpy as jnp
from jax import lax
import numpy as np

D_MODEL = 1024
BATCH = 1
SEQ = 512
DEPTH = 1

N_HEADS = 8
HEAD_DIM = 64
ATTN_WIDTH = N_HEADS * HEAD_DIM
IDX_HEADS = 4
IDX_DIM = 64
TOPK_MAX = 256
Q_BLOCK = 128
POOL_WINDOWS = (2, 4, 8, 16)
POOL_GROUPS = 4
POOL_GROUP_DIM = 128
POOL_WIDTH = POOL_GROUPS * POOL_GROUP_DIM
D_FF = 2816
CONV_WIDTH = 3
EPS = 1e-6
N_MOD = 6
IN_SIZES = (ATTN_WIDTH, ATTN_WIDTH, ATTN_WIDTH,
            IDX_HEADS * IDX_DIM, IDX_DIM, IDX_HEADS,
            POOL_WIDTH,
            D_MODEL, D_MODEL)
IN_TOTAL = sum(IN_SIZES)

kernel_name = "hybrid_dsa_pool_convffn_block"

def split_cols(a, sizes):
    outs = []
    off = 0
    for s in sizes:
        outs.append(a[..., off:off + s])
        off += s
    return outs

def rms_norm(x, g):
    xf = x.astype(jnp.float32)
    y = xf * lax.rsqrt(jnp.mean(xf * xf, axis=-1, keepdims=True) + EPS)
    return (y * g.astype(jnp.float32)).astype(x.dtype)

def modulate(x, g, shift, scale):
    return rms_norm(x, g) * (1.0 + scale[:, None, :]) + shift[:, None, :]

def alibi_slopes(n_heads):
    return 2.0 ** (-8.0 * jnp.arange(1, n_heads + 1, dtype=jnp.float32) / n_heads)

def dsa_sparse_attention(q, k, v, qi, ki, wi):
    B, S, H, Dh = q.shape
    topk = min(TOPK_MAX, S // 4)
    nb = S // Q_BLOCK
    slopes = alibi_slopes(H)
    key_pos = jnp.arange(S, dtype=jnp.int32)
    scale = HEAD_DIM ** -0.5

    def to_blocks(a):
        return a.reshape((B, nb, Q_BLOCK) + a.shape[2:]).swapaxes(0, 1)

    def block_fn(args):
        qb, qib, wib, bidx = args
        qpos = bidx * Q_BLOCK + jnp.arange(Q_BLOCK, dtype=jnp.int32)
        ilog = jnp.einsum('bqhd,bsd->bqhs', qib, ki).astype(jnp.float32)
        iscore = jnp.einsum('bqhs,bqh->bqs', jax.nn.relu(ilog), wib.astype(jnp.float32))
        causal = key_pos[None, :] <= qpos[:, None]
        iscore = jnp.where(causal[None], iscore, -jnp.inf)
        _, sel = lax.top_k(iscore, topk)
        kg = jax.vmap(lambda kk, ii: kk[ii])(k, sel)
        vg = jax.vmap(lambda vv, ii: vv[ii])(v, sel)
        s = jnp.einsum('bqhd,bqkhd->bhqk', qb, kg).astype(jnp.float32) * scale
        dist = (qpos[None, :, None] - sel).astype(jnp.float32)
        s = s - slopes[None, :, None, None] * dist[:, None]
        valid = sel <= qpos[None, :, None]
        s = jnp.where(valid[:, None], s, -jnp.inf)
        p = jax.nn.softmax(s, axis=-1).astype(vg.dtype)
        return jnp.einsum('bhqk,bqkhd->bqhd', p, vg)

    out = lax.map(block_fn, (to_blocks(q), to_blocks(qi), to_blocks(wi),
                             jnp.arange(nb, dtype=jnp.int32)))
    return out.swapaxes(0, 1).reshape(B, S, H, Dh)

def multiscale_pool(u, w_grp, pool_scale):
    B, S, P = u.shape
    uf = u.astype(jnp.float32)
    cs = jnp.pad(jnp.cumsum(uf, axis=1), ((0, 0), (1, 0), (0, 0)))
    t = jnp.arange(S, dtype=jnp.float32)
    groups = []
    for g, w in enumerate(POOL_WINDOWS):
        c_g = cs[:, :, g * POOL_GROUP_DIM:(g + 1) * POOL_GROUP_DIM]
        upper = c_g[:, 1:]
        lower = jnp.pad(c_g, ((0, 0), (w - 1, 0), (0, 0)))[:, :S]
        count = jnp.minimum(t + 1.0, float(w))[None, :, None]
        mean = (upper - lower) / count
        groups.append(mean - uf[:, :, g * POOL_GROUP_DIM:(g + 1) * POOL_GROUP_DIM])
    pooled = jnp.stack(groups, axis=2).astype(u.dtype)
    mixed = jnp.einsum('bsgc,gcd->bsgd', pooled, w_grp).reshape(B, S, P)
    return mixed * pool_scale

def conv_ffn(h, w_up, conv_w, conv_b, w_down):
    S = h.shape[1]
    up = h @ w_up
    padded = jnp.pad(up, ((0, 0), (CONV_WIDTH - 1, 0), (0, 0)))
    y = conv_b + sum(conv_w[j] * padded[:, j:j + S] for j in range(CONV_WIDTH))
    a, b = jnp.split(y, 2, axis=-1)
    return (jax.nn.silu(a) * b) @ w_down

def setup_inputs(seed: int = 0) -> dict:
    key = jax.random.key(seed)
    ks = jax.random.split(key, 20)
    f = jnp.float32
    D = D_MODEL
    nrm = lambda k, shape, fan: jax.random.normal(k, shape, f) * (fan ** -0.5)
    return {
        "x": jax.random.normal(ks[0], (BATCH, SEQ, D), f),
        "c": jax.random.normal(ks[1], (BATCH, D), f),
        "w_ada": nrm(ks[2], (DEPTH, D, N_MOD * D), D) * 0.5,
        "b_ada": jax.random.normal(ks[3], (DEPTH, N_MOD * D), f) * 0.02,
        "norm1_g": 1.0 + 0.05 * jax.random.normal(ks[4], (DEPTH, D), f),
        "w_in": nrm(ks[5], (DEPTH, D, IN_TOTAL), D),
        "q_norm_g": 1.0 + 0.05 * jax.random.normal(ks[6], (DEPTH, HEAD_DIM), f),
        "k_norm_g": 1.0 + 0.05 * jax.random.normal(ks[7], (DEPTH, HEAD_DIM), f),
        "w_attn_br": nrm(ks[8], (DEPTH, ATTN_WIDTH, D), ATTN_WIDTH),
        "w_pool_grp": nrm(ks[9], (DEPTH, POOL_GROUPS, POOL_GROUP_DIM, POOL_GROUP_DIM), POOL_GROUP_DIM),
        "pool_scale": 1.0 + 0.1 * jax.random.normal(ks[10], (DEPTH, POOL_WIDTH), f),
        "w_pool_br": nrm(ks[11], (DEPTH, POOL_WIDTH, D), POOL_WIDTH),
        "w_out": nrm(ks[12], (DEPTH, D, D), D),
        "norm2_g": 1.0 + 0.05 * jax.random.normal(ks[13], (DEPTH, D), f),
        "w_up": nrm(ks[14], (DEPTH, D, 2 * D_FF), D),
        "conv_w": nrm(ks[15], (DEPTH, CONV_WIDTH, 2 * D_FF), CONV_WIDTH),
        "conv_b": jax.random.normal(ks[16], (DEPTH, 2 * D_FF), f) * 0.02,
        "w_down": nrm(ks[17], (DEPTH, D_FF, D), D_FF),
    }

def reference(x, c, w_ada, b_ada, norm1_g, w_in, q_norm_g, k_norm_g, w_attn_br,
              w_pool_grp, pool_scale, w_pool_br, w_out, norm2_g, w_up, conv_w,
              conv_b, w_down):
    B, S, D = x.shape
    for l in range(DEPTH):
        mod = jax.nn.silu(c) @ w_ada[l] + b_ada[l]
        shift1, scale1, gate1, shift2, scale2, gate2 = jnp.split(mod, N_MOD, axis=-1)

        h = modulate(x, norm1_g[l], shift1, scale1)
        proj = h @ w_in[l]
        q, k, v, qi, ki, wi, u_pool, g_attn, g_pool = split_cols(proj, IN_SIZES)
        q = rms_norm(q.reshape(B, S, N_HEADS, HEAD_DIM), q_norm_g[l])
        k = rms_norm(k.reshape(B, S, N_HEADS, HEAD_DIM), k_norm_g[l])
        v = v.reshape(B, S, N_HEADS, HEAD_DIM)
        qi = qi.reshape(B, S, IDX_HEADS, IDX_DIM) * (IDX_DIM ** -0.5)
        wi = wi * (IDX_HEADS ** -0.5)
        attn = dsa_sparse_attention(q, k, v, qi, ki, wi).reshape(B, S, ATTN_WIDTH)
        y_attn = attn @ w_attn_br[l]
        y_pool = multiscale_pool(u_pool, w_pool_grp[l], pool_scale[l]) @ w_pool_br[l]
        merged = jax.nn.sigmoid(g_attn) * y_attn + jax.nn.sigmoid(g_pool) * y_pool
        x = x + gate1[:, None, :] * (merged @ w_out[l])

        h2 = modulate(x, norm2_g[l], shift2, scale2)
        x = x + gate2[:, None, :] * conv_ffn(h2, w_up[l], conv_w[l], conv_b[l], w_down[l])
    return x


_drawn_inputs = setup_inputs


def setup_inputs(seed=0):
    import zlib

    import numpy as np

    out = dict(_drawn_inputs(seed))
    spreads = {}
    factors = {'norm1_g': 3.005,
     'q_norm_g': 8.0,
     'k_norm_g': 8.0,
     'pool_scale': 3.569,
     'norm2_g': 3.736,
     'conv_b': 8.0}
    for name, (base, spread) in spreads.items():
        noise = np.random.default_rng([zlib.crc32(name.encode()), seed]).standard_normal(out[name].shape)
        drawn = base * np.exp(spread * noise) if base else spread * noise
        out[name] = __import__('jax').numpy.asarray(drawn.astype(out[name].dtype))
    for name, factor in factors.items():
        out[name] = (out[name] * factor).astype(out[name].dtype)
    return out
```

```python
from contextlib import ExitStack

import concourse.bass as bass
from concourse import mybir

F32 = mybir.dt.float32
F32R = mybir.dt.float32r
ALU = mybir.AluOpType
ACT = mybir.ActivationFunctionType
AX_X = mybir.AxisListType.X

P = 128
S, D, FF = 512, 1024, 2816
H, HD = 8, 64
IH = 4
TOPK = 128
TAPS = 3
EPS = 1e-6
NT = S // P
KD = D // P
KA = H * HD // P
KF = FF // P
NPAIR = H // 2
WINDOWS = (2, 4, 8, 16)
PAD = 16
WU = KD * P

C_Q, C_K, C_V, C_QI, C_KI = 0, 512, 1024, 1536, 1792
C_U = C_KI + HD + IH
C_GA, C_GP = C_U + 512, C_U + 512 + D

BIG = 1e32
FUTURE = -3.0e38
TAKEN = -3.4e38
TAKEN_BELOW = -3.2e38

NSTAGE = 3
NRING = 3
NBANK = 3


def slope(h):
    return 2.0 ** (-8.0 * (h + 1) / H)


def offset(i):
    return i * (i + 1) // 2 * P


NPAIRS = offset(NT)
STEPS = NT * H
SLOTS = STEPS + 5
MC, WC = 480, NT * 2 * H
ROW_LOADS = 12


def filler(t):
    p, n = divmod(t // 2, 4)
    return ("gp" if n < 2 else "pb", 2 * p + n % 2)


class Schedule:

    def __init__(self):
        self.items = []
        self.units = []
        self.unit = {}
        self.chunk = {}
        self.drains = []
        self.last_use = []
        self.item_of = []
        self.mods = 0

    def mod(self, j, q):
        self.items.append(("mod", j, q))
        self.mods += 2
        self.last_use.append(("mod", self.mods))

    def load(self, w, columns, k0, k1, names):
        self.items.append(("w", w, columns, k0, k1))
        for part, name in enumerate(names):
            self.units.append((k1 - k0, part))
            self.item_of.append(len(self.items) - 1)
            if name is not None:
                self.unit[name] = len(self.units) - 1
        self.last_use.append(("unit", len(self.units)))

    def opens(self, *named):
        for name, drain in named:
            self.chunk[name] = len(self.chunk)
            self.drains.append(drain)

    def group(self, g):
        self.units.append((1, g))
        self.item_of.append(None)
        self.unit["mg", g] = len(self.units) - 1
        self.opens((("mg", g), "dve"))

    def pair(self, w, kind, m, c0, nk, drain):
        self.load(w, (c0 + m * P,), 0, nk, [(kind, m), (kind, m + 1)])
        self.opens(((kind, m), drain), ((kind, m + 1), drain))


def schedule():
    s = Schedule()
    for j in range(2):
        for q in range(KD // 2):
            s.mod(j, q)
    s.pair("in", "qi", 0, C_QI, KD, "dve")
    s.load("in", (C_KI,), 0, KD, [("kw", 0)])
    s.opens((("kw", 0), "dve"))
    for kind, c0, drain in (("q", C_Q, "dve"), ("k", C_K, "act"), ("v", C_V, "act")):
        for m in range(0, KA, 2):
            s.pair("in", kind, m, c0, KD, drain)
    s.load("in", (C_U,), 0, KD, [("u", 0), ("u", 1)])
    s.opens((("u", 0), "act"), (("u", 1), "act"))
    s.group(0)
    s.items.append(("w", "in", (C_U + 2 * P,), 0, KD))
    item = len(s.items) - 1
    s.last_use.append(None)
    for part, g in ((0, 1), (1, 2)):
        s.units.append((KD, part))
        s.item_of.append(item)
        s.unit["u", 2 + part] = len(s.units) - 1
        s.opens((("u", 2 + part), "act"))
        if part:
            s.last_use[item] = ("unit", len(s.units))
        s.group(g)
    s.group(3)
    for p in range(KD // 2):
        s.pair("in", "gp", 2 * p, C_GP, KD, "act")
        s.mod(2, p)
        s.pair("pb", "pb", 2 * p, 0, KA, "dve")
    for p in range(KD // 2):
        s.pair("in", "ga", 2 * p, C_GA, KD, "act")
        s.mod(3 + p // 2, 2 * (p % 2))
        s.pair("ab", "ab", 2 * p, 0, KA, "dve")
        s.mod(3 + p // 2, 2 * (p % 2) + 1)
    for p in range(KD // 2):
        s.pair("out", "wo", 2 * p, 0, KD, "dve")
        s.mod(5, p)
    for m in range(KF):
        s.load("up", (m * P, FF + m * P), 0, KD, [("ua", m), ("ub", m)])
        s.opens((("ua", m), "dve"), (("ub", m), "dve"))
    for m in range(0, KD, 2):
        for k0 in range(0, KF, KD):
            k1 = min(k0 + KD, KF)
            last = k1 == KF
            s.load("down", (m * P,), k0, k1, [("dn", m) if last else None, ("dn", m + 1) if last else None])
        s.opens((("dn", m), "dve"), (("dn", m + 1), "dve"))
    return s


def build_layer(nc, x, c, w_ada, b_ada, norm1_g, w_in, q_norm_g, k_norm_g, w_attn_br, w_pool_grp, pool_scale,
                w_pool_br, w_out, norm2_g, w_up, conv_w, conv_b, w_down, out):
    sch = schedule()
    drained_count = []
    so_far = {"act": 0, "dve": 0}
    for who in sch.drains:
        so_far[who] += 1
        drained_count.append((who, so_far[who]))

    ada = w_ada[0].rearrange("(k p) n -> p k n", p=P)
    weights = {
        "in": w_in[0].rearrange("(k p) n -> p k n", p=P),
        "ab": w_attn_br[0].rearrange("(k p) n -> p k n", p=P),
        "pb": w_pool_br[0].rearrange("(k p) n -> p k n", p=P),
        "out": w_out[0].rearrange("(k p) n -> p k n", p=P),
        "up": w_up[0].rearrange("(k p) n -> p k n", p=P),
        "down": w_down[0].rearrange("(k p) n -> p k n", p=P),
    }
    out_v = out[0].rearrange("(t p) f -> p t f", p=P)

    with ExitStack() as ctx:
        at = [nc.sbuf_base + (-nc.sbuf_base) % 32]

        def place(name, shape, dt, where=None):
            size = 4
            for n in shape[1:]:
                size *= n
            if where is None:
                where = at[0]
                at[0] += size + (-size) % 32
            return nc.alloc_sbuf_tensor_at(name, shape, dt, offset=where)

        xT = place("xT", [P, KD, S], F32)
        hT = place("hT", [P, 2, KD, S], F32R)
        wsplit = place("wsplit", [P, NRING, 2, WU], F32R)
        stage = place("stage", [P, NSTAGE, 2 * WU], F32)
        ident = place("ident", [P, P], F32)
        ones = place("ones", [P, P], F32)
        halves = place("halves", [P, 2], F32)
        vec = place("vec", [P, 78], F32)
        conv = place("conv", [P, (TAPS + 1) * 2 * KF], F32)
        csil = place("csil", [P, KD], F32)
        qgain = place("qgain", [P, 1], F32)
        mod = place("mod", [P, 6 * KD], F32)
        gs = place("gs", [P, 2, KD], F32)
        invn = place("invn", [P, PAD], F32)
        stat = place("stat", [P, 3, NT * 2 * H], F32)
        tstat = place("tstat", [P, 4, NT], F32)
        alibi = place("alibi", [P, NT * H], F32)
        wi = place("wi", [P, NT * IH], F32)
        top8 = place("top8", [P, NT, 8], F32)
        smax = place("smax", [P, STEPS], F32)
        sbias = place("sbias", [P, STEPS], F32)
        ssum = place("ssum", [P, STEPS], F32)
        sinv = place("sinv", [P, STEPS], F32)

        K1 = 1024
        base = at[0]
        assert base + 107 * K1 <= nc.sbuf_usable_end, (base, nc.sbuf_usable_end)

        def arena(name, shape, dt, kb):
            return place(name, shape, dt, base + int(kb * K1))

        xn = arena("xn", [P, NT, D], F32, 0)
        rows = arena("rows", [P, 3, P], F32, 20)
        junk = arena("junk", [P, 2, D], F32, 24)
        qT = arena("qT", [P, 2, KA, S], F32R, 0)
        kT = arena("kT", [P, 2, KA, S], F32R, 16)
        vS = arena("vS", [P, NT, H, 2, HD], F32R, 32)
        kraw = arena("kraw", [P, KA, S], F32, 48)
        sq = arena("sq", [P, 2, S], F32, 56)
        dist = arena("dist", [P, S], F32, 60)
        wgrp = arena("wgrp", [P, KA, P], F32, 62)
        qiT = arena("qiT", [P, 2, 2, S], F32R, 64)
        kiT = arena("kiT", [P, 2, S], F32R, 72)
        vraw = arena("vraw", [P, 2, S], F32, 80)
        wiT = arena("wiT", [P, S], F32, 84)
        cap = arena("cap", [P, P], F32, 86.5)
        dsel = arena("dsel", [P, NPAIRS], F32, 88)
        iscore = arena("iscore", [P, NPAIRS - P], F32, 93)
        work = arena("work", [P, NPAIRS - P], F32, 97.5)
        relu = arena("relu", [P, 2, S], F32, 102)
        kroot = arena("kroot", [P, 2, S], F32, 93)
        knorm = arena("knorm", [P, 2, S], F32, 97)
        u = arena("u", [P, PAD + S], F32, 80)
        wsum = [arena(f"wsum{n}", [P, PAD + S], F32, 82.125 + 2.125 * n) for n in range(2)]
        pooled = arena("pooled", [P, 2, S], F32R, 103)
        pmean = arena("pmean", [P, S], F32, 101)
        mix = arena("mix", [P, 2, KA, S], F32R, 64)
        ypool = arena("ypool", [P, KD, S], F32, 48)
        pT = arena("pT", [P, 2, 2, S], F32R, 80)
        logit = arena("logit", [P, 2, S], F32, 93)
        prob = arena("prob", [P, 2, S], F32, 97)
        araw = arena("araw", [P, S], F32, 101)
        macc = arena("macc", [P, D], F32, 103)
        nrm = arena("nrm", [P, 2, S], F32, 97)
        diag = arena("diag", [P, NT, P], F32, 101)
        merged = arena("merged", [P, 2, KD, S], F32R, 16)
        tga = arena("tga", [P, 2, S], F32, 80)
        msum = arena("msum", [P, 2, S], F32, 84)
        sq2 = arena("sq2", [P, 2, S], F32, 80)
        guT = arena("guT", [P, 2, KF, S], F32R, 0)
        ya = arena("ya", [P, 2, S], F32, 88)
        yb = arena("yb", [P, 2, S], F32, 92)
        ost = arena("ost", [P, 2, NT, P], F32, 96)

        banks = [ctx.enter_context(nc.psum_tensor(f"bank{n}", [P, S], F32)) for n in range(8)]
        SC, PT, OB = banks[3:5], banks[5:7], banks[7]

        def sem(name):
            return ctx.enter_context(nc.semaphore(name))

        rows_in = sem("rows_in")
        x_in = sem("x_in")
        wgrp_in = sem("wgrp_in")
        stage_in = [sem(f"stage_in{n}") for n in range(NSTAGE)]
        stored = [sem(f"stored{n}") for n in range(2)]
        consts = sem("consts")
        vecs = sem("vecs")
        high = sem("high")
        low = sem("low")
        used = sem("used")
        drained = {"act": sem("drained_act"), "dve": sem("drained_dve")}
        act_step = sem("act_step")
        dve_step = sem("dve_step")
        rows_t = sem("rows_t")
        c_silu = sem("c_silu")
        x_sum = sem("x_sum")
        x_t = sem("x_t")
        x_kept = [sem("x_kept_even"), sem("x_kept_odd")]
        mean_ok = sem("mean_ok")
        root_ok = sem("root_ok")
        diag_ok = sem("diag_ok")
        root_b = sem("root_b")
        mod_sum = sem("mod_sum")
        mod_col = sem("mod_col")
        mod_ok = sem("mod_ok")
        n_ok = sem("n_ok")
        h_hi = sem("h_hi")
        h_lo = sem("h_lo")
        sq_ok = sem("sq_ok")
        sq_used = sem("sq_used")
        qk_mean = sem("qk_mean")
        qk_root = sem("qk_root")
        kroot_ok = sem("kroot_ok")
        kroot_t = sem("kroot_t")
        kn_ok = sem("kn_ok")
        k_hi = sem("k_hi")
        k_lo = sem("k_lo")
        part_hi = sem("part_hi")
        wi_t = sem("wi_t")
        wi_row = sem("wi_row")
        wi_ok = sem("wi_ok")
        i_dot = sem("i_dot")
        i_relu = sem("i_relu")
        i_sum = sem("i_sum")
        sel_ok = sem("sel_ok")
        v_t = sem("v_t")
        v_hi = sem("v_hi")
        v_lo = sem("v_lo")
        p_ok = sem("p_ok")
        p_hi = sem("p_hi")
        p_lo = sem("p_lo")
        score = sem("score")
        logit_ok = sem("logit_ok")
        bias_ok = sem("bias_ok")
        exp_ok = sem("exp_ok")
        prob_ok = sem("prob_ok")
        prob_t = sem("prob_t")
        pt_hi = sem("pt_hi")
        pt_lo = sem("pt_lo")
        pv_ok = sem("pv_ok")
        head_lo = sem("head_lo")
        head_ok = sem("head_ok")
        pair_hi = sem("pair_hi")
        pair_lo = sem("pair_lo")
        m_ok = sem("m_ok")
        m_hi = sem("m_hi")
        m_lo = sem("m_lo")
        x2_sq = sem("x2_sq")
        x2_sum = sem("x2_sum")
        y_tap = sem("y_tap")
        silu_ok = sem("silu_ok")
        g_ok = sem("g_ok")
        gu_hi = sem("gu_hi")
        gu_lo = sem("gu_lo")
        out_t = sem("out_t")
        out_ok = sem("out_ok")

        class Progress:

            def __init__(self, eng, step):
                self.eng, self.step, self.n, self.last = eng, step, {}, None

            def did(self, ins, signal=None):
                signal = self.step if signal is None else signal
                self.n[id(signal)] = self.n.get(id(signal), 0) + 1
                ins.then_inc(signal, 1)
                self.last = (signal, self.n[id(signal)])
                return self.last

            def settle(self, mark=None):
                signal, n = mark or self.last
                self.eng.wait_ge(signal, n)

        def bank(name):
            return banks[sch.chunk[name] % NBANK]

        def await_chunk(eng, name):
            eng.wait_ge(used, sch.unit[name] + 1)

        def await_drained(eng, name):
            who, n = drained_count[sch.chunk[name]]
            eng.wait_ge(drained[who], n)

        def await_bank(eng, name):
            if sch.chunk[name] >= NBANK:
                who, n = drained_count[sch.chunk[name] - NBANK]
                eng.wait_ge(drained[who], n)

        landed = []
        slot_total = [0] * NSTAGE
        for n, item in enumerate(sch.items):
            slot_total[n % NSTAGE] += 16 * (len(item[2]) if item[0] == "w" else 1)
            landed.append(slot_total[n % NSTAGE])

        def await_item(eng, n):
            eng.wait_ge(stage_in[n % NSTAGE], landed[n])

        def unit_source(n):
            nk, part = sch.units[n]
            item = sch.item_of[n]
            if item is None:
                return wgrp[:, part:part + 1, :]
            slot = stage[:, item % NSTAGE, :]
            if len(sch.items[item][2]) == 2:
                return slot[:, part * WU:part * WU + nk * P].rearrange("p (k n) -> p k n", n=P)
            wide = 2 * P if not (sch.items[item][1] == "in" and sch.items[item][2] == (C_KI,)) else P
            return slot[:, 0:nk * wide].rearrange("p (k n) -> p k n", n=wide)[:, :, part * P:(part + 1) * P]

        def unit_split(n, part):
            nk = sch.units[n][0]
            return wsplit[:, n % NRING, part, 0:nk * P].rearrange("p (k n) -> p k n", n=P)

        block = ctx.enter_context(nc.Block())

        @block.sync
        def _(sp):
            nc_rows = [
                (0, 0, c[0].rearrange("(k p) -> k p", p=P)),
                (0, 8, b_ada[0].rearrange("(k p) -> k p", p=P)),
                (0, 56, norm1_g[0].rearrange("(k p) -> k p", p=P)),
                (0, 64, norm2_g[0].rearrange("(k p) -> k p", p=P)),
                (0, 72, pool_scale[0].rearrange("(k p) -> k p", p=P)),
            ]
            for tile, r, src in nc_rows:
                sp.dma_start(rows[r:r + src.shape[0], tile, :], src).then_inc(rows_in, 16)
            for r, src in ((76, q_norm_g), (77, k_norm_g)):
                for half in range(2):
                    sp.dma_start(rows[r:r + 1, 0, half * HD:(half + 1) * HD], src).then_inc(rows_in, 16)
            taps = conv_w[0].rearrange("j (m p) -> (j m) p", p=P)
            sp.dma_start(rows[:, 1, :], taps[0:P, :]).then_inc(rows_in, 16)
            sp.dma_start(rows[0:TAPS * 2 * KF - P, 2, :], taps[P:TAPS * 2 * KF, :]).then_inc(rows_in, 16)
            sp.dma_start(rows[TAPS * 2 * KF - P:(TAPS + 1) * 2 * KF - P, 2, :],
                         conv_b[0].rearrange("(m p) -> m p", p=P)).then_inc(rows_in, 16)
            for t in range(NT):
                sp.dma_start(xn[:, t, :], x[0, t * P:(t + 1) * P, :]).then_inc(x_in, 16)
            sp.dma_start(wgrp[:, :, :], w_pool_grp[0].rearrange("g c d -> c g d")).then_inc(wgrp_in, 16)
            for n, item in enumerate(sch.items):
                if n >= NSTAGE:
                    kind, count = sch.last_use[n - NSTAGE]
                    sp.wait_ge(mod_sum if kind == "mod" else low, count)
                slot = stage[:, n % NSTAGE, :]
                if item[0] == "mod":
                    _, j, q = item
                    sp.dma_start(slot.rearrange("p (k n) -> p k n", k=2), ada[:, 2 * q:2 * q + 2, j * D:(j + 1) * D]
                                 ).then_inc(stage_in[n % NSTAGE], 16)
                    continue
                _, w, columns, k0, k1 = item
                if len(columns) == 2:
                    for part, c0 in enumerate(columns):
                        sp.dma_start(slot[:, part * WU:(part + 1) * WU].rearrange("p (k n) -> p k n", n=P),
                                     weights[w][:, k0:k1, c0:c0 + P]).then_inc(stage_in[n % NSTAGE], 16)
                    continue
                c0, = columns
                wide = P if (w, c0) == ("in", C_KI) else 2 * P
                sp.dma_start(slot[:, 0:(k1 - k0) * wide].rearrange("p (k n) -> p k n", n=wide),
                             weights[w][:, k0:k1, c0:c0 + wide]).then_inc(stage_in[n % NSTAGE], 16)
            for m in range(KD):
                sp.wait_ge(out_ok, m + 1)
                sp.dma_start(out_v[:, :, m * P:(m + 1) * P], ost[:, m % 2, :, :]).then_inc(stored[m % 2], 16)
            for n in range(2):
                sp.wait_ge(stored[n], 16 * (KD // 2))

        @block.gpsimd
        def _(pool):
            pool.memset(ident[:, :], 0.0).then_inc(consts, 1)
            pool.memset(cap[:, :], -TAKEN_BELOW).then_inc(consts, 1)
            pool.memset(halves[:, :], 1.0).then_inc(consts, 1)
            pool.memset(ones[:, :], 1.0).then_inc(consts, 1)
            pool.iota(dist[:, :], [[-1, S]], base=(NT - 1) * P, channel_multiplier=1,
                      allow_small_or_imprecise_dtypes=True).then_inc(consts, 1)
            pool.iota(invn[:, :], [[1, PAD]], base=1, channel_multiplier=0,
                      allow_small_or_imprecise_dtypes=True).then_inc(consts, 1)
            pool.wait_ge(consts, 6)
            pool.affine_select(out=ident[:, :], in_=ident[:, :], compare_op=ALU.not_equal, fill=1.0, base=0,
                               pattern=[[-1, P]], channel_multiplier=1).then_inc(consts, 1)
            pool.affine_select(out=cap[:, :], in_=cap[:, :], compare_op=ALU.is_ge, fill=FUTURE, base=0,
                               pattern=[[-1, P]], channel_multiplier=1).then_inc(consts, 1)
            pool.affine_select(out=halves[:, 0:1], in_=halves[:, 0:1], compare_op=ALU.is_gt, fill=0.0, base=HD,
                               pattern=[[0, 1]], channel_multiplier=-1).then_inc(consts, 1)
            pool.affine_select(out=halves[:, 1:2], in_=halves[:, 1:2], compare_op=ALU.is_ge, fill=0.0, base=-HD,
                               pattern=[[0, 1]], channel_multiplier=1).then_inc(consts, 1)
            pool.affine_select(out=dsel[:, 0:P], in_=dist[:, (NT - 1) * P:S], compare_op=ALU.is_ge, fill=BIG, base=0,
                               pattern=[[-1, P]], channel_multiplier=1).then_inc(consts, 1)
            for n in range(len(sch.units)):
                pool.wait_ge(high, n + 1)
                if n >= NRING:
                    pool.wait_ge(used, n - NRING + 1)
                pool.tensor_tensor(unit_split(n, 1), unit_source(n), unit_split(n, 0).bitcast(F32),
                                   ALU.subtract).then_inc(low, 1)

        @block.scalar
        def _(act):
            me = Progress(act, act_step)
            made = [0]

            def high_parts(upto):
                while made[0] < min(upto, len(sch.units)):
                    n = made[0]
                    if sch.item_of[n] is None:
                        act.wait_ge(wgrp_in, 16)
                    else:
                        await_item(act, sch.item_of[n])
                    if n >= NRING:
                        act.wait_ge(used, n - NRING + 1)
                        act.wait_ge(low, n - NRING + 1)
                    me.did(act.activation(unit_split(n, 0), unit_source(n), ACT.Copy), high)
                    made[0] += 1

            def chunk(name):
                await_chunk(act, name)
                high_parts(sch.unit[name] + 1 + NRING)

            def store_copy(m):
                act.wait_ge(out_t, m + 1)
                if m >= 2:
                    act.wait_ge(stored[m % 2], 16 * (m // 2))
                me.did(act.activation(ost[:, m % 2, :, :], PT[m % 2][:, :].rearrange("p (t f) -> p t f", t=NT),
                                      ACT.Copy), out_ok)

            act.wait_ge(vecs, 1)
            me.did(act.activation(csil[:, :], vec[:, 0:KD], ACT.Silu), c_silu)
            act.wait_ge(x_in, 16 * NT)
            for t in range(NT):
                if t >= 2:
                    act.wait_ge(x_sum, t - 1)
                me.did(act.activation(junk[:, t % 2, :], xn[:, t, :], ACT.Square,
                                      accum_out=tstat[:, 0, t:t + 1]), x_sum)
            for k in range(KD):
                if k % 2 == 0:
                    act.wait_ge(x_t, k + 1)
                    me.did(act.activation(xT[:, k, :], (SC + PT)[k % 4][:, :], ACT.Copy), x_kept[0])
            act.wait_ge(mean_ok, 1)
            me.did(act.activation(tstat[:, 2, :], tstat[:, 1, :], ACT.Sqrt), root_ok)
            high_parts(NRING)

            def h_high(which, shift):
                act.wait_ge(mod_ok, shift + 1)
                for k in range(KD):
                    act.wait_ge(n_ok, which * KD + k + 1)
                    me.did(act.activation(hT[:, 0, k, :], nrm[:, k % 2, :], ACT.Identity,
                                          bias=mod[:, shift * KD + k:shift * KD + k + 1]), h_hi)

            h_high(0, 0)
            for m in range(2):
                chunk(("qi", m))
                me.did(act.activation(qiT[:, 0, m, :], bank(("qi", m))[:, :], ACT.Copy), part_hi)
            chunk(("kw", 0))
            b = bank(("kw", 0))
            me.did(act.activation(wiT[0:IH, :], b[HD:HD + IH, :], ACT.Copy), wi_row)
            me.did(act.activation(kiT[0:HD, 0, :], b[0:HD, :], ACT.Copy), part_hi)
            me.did(act.activation(kiT[HD:P, 0, :], b[0:HD, :], ACT.Copy), part_hi)

            def indexer(i):
                for h in range(IH):
                    n = (i - 1) * IH + h
                    act.wait_ge(i_dot, n + 1)
                    if n >= 2:
                        act.wait_ge(i_sum, n - 1)
                    me.did(act.activation(relu[:, n % 2, 0:(i + 1) * P], SC[n % 2][:, 0:(i + 1) * P], ACT.Relu,
                                          scale=HD ** -0.5), i_relu)

            for n in range(2 * KA):
                kind, m = ("q", n) if n < KA else ("k", n - KA)
                name = (kind, m)
                chunk(name)
                if n >= 2:
                    act.wait_ge(sq_used, n - 1)
                me.did(act.activation(sq[:, n % 2, :], bank(name)[:, :], ACT.Square), sq_ok)
                if kind == "q":
                    me.did(act.activation(qT[:, 0, m, :], bank(name)[:, :], ACT.Copy, scale=qgain[:, 0:1]), part_hi)
                    if m < NT - 1:
                        indexer(m + 1)
                else:
                    me.did(act.activation(kraw[:, m, :], bank(name)[:, :], ACT.Copy), drained["act"])

            def v_high(m):
                act.wait_ge(v_t, m + 1)
                me.did(act.activation(vS[:, :, 2 * m:2 * m + 2, 0, :],
                                      PT[m % 2][:, :].rearrange("p (t h d) -> p t h d", t=NT, h=2), ACT.Copy), v_hi)

            for m in range(KA):
                chunk(("v", m))
                if m >= 2:
                    act.wait_ge(v_t, m - 1)
                me.did(act.activation(vraw[:, m % 2, :], bank(("v", m))[:, :], ACT.Copy), drained["act"])
                if m:
                    v_high(m - 1)
                else:
                    act.wait_ge(qk_mean, 1)
                    me.did(act.activation(stat[:, 1, :], stat[:, 0, :], ACT.Sqrt), qk_root)
            def mixed(g):
                name = ("mg", g)
                chunk(name)
                me.did(act.activation(mix[:, 0, g, :], bank(name)[:, :], ACT.Copy,
                                      scale=vec[:, 72 + g:73 + g]), part_hi)

            def k_high(m):
                act.wait_ge(kn_ok, m + 1)
                me.did(act.activation(kT[:, 0, m, :], knorm[:, m % 2, :], ACT.Copy), k_hi)

            for g in range(KA):
                chunk(("u", g))
                if g == 0:
                    act.wait_ge(v_t, KA)
                else:
                    act.wait_ge(p_ok, g)
                me.did(act.activation(u[:, PAD:PAD + S], bank(("u", g))[:, :], ACT.Copy), drained["act"])
                if g == 0:
                    v_high(KA - 1)
                else:
                    mixed(g - 1)
                act.wait_ge(p_ok, g + 1)
                if g:
                    act.wait_ge(used, sch.unit["mg", g - 1] + 1)
                me.did(act.activation(pooled[:, 0, :], pmean[:, :], ACT.Copy), p_hi)
                k_high(g)
            mixed(KA - 1)

            for t in range(SLOTS):
                if t >= 7 and t % NT == 3:
                    h = t // NT - 1
                    act.wait_ge(pv_ok, NT * (h + 1))
                    if h % 2 == 0 and h:
                        act.wait_ge(pair_lo, h // 2)
                    r = (h % 2) * HD
                    me.did(act.activation(araw[r:r + HD, :], OB[HD:P, :], ACT.Copy), head_lo)
                if t < STEPS:
                    h, i = divmod(t, NT)
                    n = (i + 1) * P
                    act.wait_ge(bias_ok, t + 1)
                    if t >= 2:
                        act.wait_ge(prob_t, t - 1)
                    r = i * 2 * H + h
                    me.did(act.activation(prob[:, t % 2, 0:n], logit[:, t % 2, 0:n], ACT.Exp,
                                          bias=sbias[:, t:t + 1], scale=stat[:, 2, r:r + 1],
                                          accum_out=ssum[:, t:t + 1]), exp_ok)
                if 2 <= t < STEPS + 2:
                    n = ((t - 2) % NT + 1) * P
                    act.wait_ge(prob_t, t - 1)
                    if t >= 4:
                        act.wait_ge(pv_ok, t - 3)
                    me.did(act.activation(pT[:, t % 2, 0, 0:n], PT[t % 2][:, 0:n], ACT.Copy), pt_hi)
                if t >= 12 and t % (2 * NT) == NT:
                    m = t // (2 * NT) - 1
                    act.wait_ge(head_ok, 2 * m + 2)
                    me.did(act.activation(qT[:, 0, m, :], araw[:, :], ACT.Copy), pair_hi)
                if t % 2 == 1 and t < STEPS:
                    name = filler(t - 1)
                    chunk(name)
                    if name[0] == "gp":
                        me.did(act.activation(ypool[:, name[1], :], bank(name)[:, :], ACT.Tanh, scale=0.5),
                               drained["act"])

            def merged_high(m):
                act.wait_ge(m_ok, m + 1)
                me.did(act.activation(merged[:, 0, m, :], msum[:, m % 2, :], ACT.Copy, scale=0.5), m_hi)

            for m in range(0, KD, 2):
                for n in (m, m + 1):
                    chunk(("ga", n))
                    if n >= 2:
                        act.wait_ge(m_ok, n - 1)
                    me.did(act.activation(tga[:, n % 2, :], bank(("ga", n))[:, :], ACT.Tanh, scale=0.5),
                           drained["act"])
                for n in (m, m + 1):
                    chunk(("ab", n))
                    merged_high(n)

            for m in range(KD):
                chunk(("wo", m))
                await_drained(act, ("wo", m))
                if m >= 2:
                    act.wait_ge(x2_sum, m - 1)
                me.did(act.activation(sq2[:, m % 2, :], xT[:, m, :], ACT.Square), x2_sq)
            act.wait_ge(mean_ok, 2)
            me.did(act.activation(tstat[:, 2, :], tstat[:, 1, :], ACT.Sqrt), root_ok)
            h_high(1, 3)

            def last_tap(kind, m, y):
                col = m if kind == "ua" else KF + m
                chunk((kind, m))
                me.did(act.activation(y[:, m % 2, :], bank((kind, m))[:, :], ACT.Identity,
                                      bias=conv[:, TAPS * 2 * KF + col:TAPS * 2 * KF + col + 1],
                                      scale=conv[:, (TAPS - 1) * 2 * KF + col:(TAPS - 1) * 2 * KF + col + 1]), y_tap)

            def gu_high(m):
                act.wait_ge(g_ok, m + 1)
                me.did(act.activation(guT[:, 0, m, :], ya[:, m % 2, :], ACT.Copy), gu_hi)

            for m in range(KF):
                if m >= 2:
                    act.wait_ge(gu_lo, m - 1)
                last_tap("ua", m, ya)
                if m:
                    gu_high(m - 1)
                last_tap("ub", m, yb)
                await_drained(act, ("ua", m))
                me.did(act.activation(ya[:, m % 2, :], ya[:, m % 2, :], ACT.Silu), silu_ok)
            gu_high(KF - 1)

            for m in range(0, KD, 2):
                for n in range(sch.unit["dn", m] - 4, sch.unit["dn", m] + 2):
                    act.wait_ge(used, n + 1)
                    high_parts(n + 1 + NRING)
                    if m and n == sch.unit["dn", m] - 2:
                        for r in (m - 2, m - 1):
                            store_copy(r)
            for r in (KD - 2, KD - 1):
                store_copy(r)

        @block.vector
        def _(dve):
            me = Progress(dve, dve_step)

            def copy_of(out_ap, in_ap):
                return dve.tensor_copy(out_ap, in_ap)

            dve.wait_ge(rows_t, 1)
            me.did(copy_of(vec[:, :], OB[:, 0:78]))
            me.did(copy_of(conv[:, 0:P], OB[:, P:2 * P]))
            me.did(copy_of(conv[:, P:(TAPS + 1) * 2 * KF], OB[:, 2 * P:(TAPS + 1) * 2 * KF + P]))
            me.settle()
            me.did(dve.tensor_scalar(qgain[:, :], vec[:, 76:77], HD ** -0.5, None, ALU.mult), vecs)
            dve.wait_ge(consts, 11)
            me.did(dve.reciprocal(invn[:, :], invn[:, :]))

            def mod_rows(j, q):
                item = sch.items.index(("mod", j, q))
                await_item(dve, item)
                slot = stage[:, item % NSTAGE, :]
                for r in range(2):
                    k = 2 * q + r
                    rows_k = slot[:, r * D:(r + 1) * D]
                    if k == 0:
                        if j:
                            dve.wait_ge(mod_col, j)
                        me.did(dve.tensor_scalar(macc[:, :], rows_k, csil[:, 0:1], None, ALU.mult), mod_sum)
                    else:
                        dve.wait_ge(mod_sum, KD * j + k)
                        me.did(dve.scalar_tensor_tensor(out=macc[:, :], in0=rows_k, scalar=csil[:, k:k + 1],
                                                        in1=macc[:, :], op0=ALU.mult, op1=ALU.add), mod_sum)

            def mod_vector(j):
                dve.wait_ge(mod_col, j + 1)
                me.did(dve.tensor_tensor(mod[:, j * KD:(j + 1) * KD], OB[:, MC:MC + KD],
                                         vec[:, 8 + j * KD:8 + (j + 1) * KD], ALU.add), mod_ok)
                if j in (1, 4):
                    me.settle()
                    gain = vec[:, 56:64] if j == 1 else vec[:, 64:72]
                    me.did(dve.scalar_tensor_tensor(out=gs[:, j // 4, :], in0=mod[:, j * KD:(j + 1) * KD], scalar=1.0,
                                                    in1=gain, op0=ALU.add, op1=ALU.mult))

            def roots(which):
                me.did(dve.tensor_scalar(tstat[:, 1, :], tstat[:, 0, :], 1.0 / D, EPS, ALU.mult, ALU.add), mean_ok)
                dve.wait_ge(root_ok, which + 1)
                me.did(dve.reciprocal(tstat[:, 3, :], tstat[:, 2, :]))
                me.settle()
                for t in range(NT):
                    last = me.did(dve.tensor_scalar(diag[:, t, :], ident[:, :], tstat[:, 3, t:t + 1], None, ALU.mult),
                                  diag_ok)

            def norm(which, shift):
                dve.wait_ge(root_b, which + 1)
                me.settle()

                def low_part(k):
                    dve.wait_ge(h_hi, which * KD + k + 1)
                    me.did(dve.scalar_tensor_tensor(
                        out=hT[:, 1, k, :], in0=nrm[:, k % 2, :], scalar=mod[:, shift * KD + k:shift * KD + k + 1],
                        in1=hT[:, 0, k, :].bitcast(F32), op0=ALU.add, op1=ALU.subtract), h_lo)

                for k in range(KD):
                    if k >= 2:
                        dve.wait_ge(h_lo, which * KD + k - 1)
                    me.did(dve.scalar_tensor_tensor(out=nrm[:, k % 2, :], in0=xT[:, k, :], scalar=gs[:, which, k:k + 1],
                                                    in1=SC[0][:, :], op0=ALU.mult, op1=ALU.mult), n_ok)
                    if k:
                        low_part(k - 1)
                low_part(KD - 1)

            for k in range(1, KD, 2):
                dve.wait_ge(x_t, k + 1)
                me.did(copy_of(xT[:, k, :], (SC + PT)[k % 4][:, :]), x_kept[1])
            dve.wait_ge(x_sum, NT)
            roots(0)
            dve.wait_ge(c_silu, 1)
            for j in range(2):
                for q in range(KD // 2):
                    mod_rows(j, q)
                mod_vector(j)
            dve.wait_ge(x_kept[0], KD // 2)
            norm(0, 0)

            def low_of(out_ap, full, hi, signal):
                me.did(dve.tensor_tensor(out_ap, full, hi.bitcast(F32), ALU.subtract), signal)

            for m in range(2):
                dve.wait_ge(part_hi, m + 1)
                low_of(qiT[:, 1, m, :], bank(("qi", m))[:, :], qiT[:, 0, m, :], drained["dve"])
            dve.wait_ge(part_hi, 4)
            b = bank(("kw", 0))
            me.did(dve.tensor_tensor(kiT[HD:P, 1, :], b[0:HD, :], kiT[0:HD, 0, :].bitcast(F32), ALU.subtract))
            low_of(kiT[0:HD, 1, :], b[0:HD, :], kiT[0:HD, 0, :], drained["dve"])
            dve.wait_ge(wi_t, 1)
            me.did(dve.tensor_scalar(wi[:, :], OB[:, WC:WC + NT * IH], IH ** -0.5, None, ALU.mult), wi_ok)

            def row_of(tensor, i):
                return tensor[:, offset(i) - P:offset(i + 1) - P]

            def indexer(i):
                acc = row_of(iscore, i)
                for h in range(IH):
                    n = (i - 1) * IH + h
                    dve.wait_ge(i_relu, n + 1)
                    me.settle()
                    w = wi[:, i * IH + h:i * IH + h + 1]
                    r = relu[:, n % 2, 0:(i + 1) * P]
                    if h == 0:
                        me.did(dve.tensor_scalar(acc, r, w, None, ALU.mult), i_sum)
                    else:
                        me.did(dve.scalar_tensor_tensor(out=acc, in0=r, scalar=w, in1=acc, op0=ALU.mult, op1=ALU.add),
                               i_sum)
                me.settle()
                me.did(dve.tensor_tensor(acc[:, i * P:], acc[:, i * P:], cap[:, :], ALU.min))

            rounds = [0]

            def top_rounds(n):
                for _ in range(n):
                    src = work if rounds[0] else iscore
                    me.settle()
                    found = [me.did(dve.max(top8[:, i, :], row_of(src, i))) for i in range(1, NT)]
                    for i in range(1, NT):
                        me.settle(found[i - 1])
                        me.did(dve.match_replace(out=row_of(work, i), in_to_replace=top8[:, i, :],
                                                 in_values=row_of(src, i), imm_value=TAKEN))
                    rounds[0] += 1

            for m in range(KA):
                dve.wait_ge(part_hi, 4 + m + 1)
                me.did(dve.scalar_tensor_tensor(out=qT[:, 1, m, :], in0=bank(("q", m))[:, :], scalar=qgain[:, 0:1],
                                                in1=qT[:, 0, m, :].bitcast(F32), op0=ALU.mult, op1=ALU.subtract),
                       drained["dve"])
                if m < NT - 1:
                    indexer(m + 1)
            top_rounds(1)
            for m in range(KA):
                top_rounds(2)
            dve.wait_ge(sq_used, 2 * KA)
            me.did(dve.tensor_scalar(stat[:, 0, :], OB[:, 0:NT * 2 * H], 1.0 / HD, EPS, ALU.mult, ALU.add), qk_mean)

            def v_low(m):
                dve.wait_ge(v_hi, m + 1)
                low_of(vS[:, :, 2 * m:2 * m + 2, 1, :], PT[m % 2][:, :].rearrange("p (t h d) -> p t h d", t=NT, h=2),
                       vS[:, :, 2 * m:2 * m + 2, 0, :], v_lo)

            top_rounds(1)
            for m in range(KA - 1):
                v_low(m)
                top_rounds(2)
            assert rounds[0] == TOPK // 8
            me.settle()
            for i in range(1, NT):
                me.did(dve.tensor_scalar(dsel[:, offset(i):offset(i + 1)], row_of(work, i), TAKEN_BELOW, BIG,
                                         ALU.is_gt, ALU.mult))
            me.settle()
            for i in range(1, NT):
                me.did(dve.tensor_tensor(dsel[:, offset(i):offset(i + 1)], dsel[:, offset(i):offset(i + 1)],
                                         dist[:, (NT - 1 - i) * P:S], ALU.add), sel_ok)
            v_low(KA - 1)
            dve.wait_ge(qk_root, 1)
            me.did(dve.reciprocal(stat[:, 2, :], stat[:, 1, :]))
            for h in range(H):
                me.did(dve.tensor_scalar(alibi[:, :].rearrange("p (t h) -> p h t", h=H)[:, h, :],
                                         stat[:, 1, :].rearrange("p (t h) -> p h t", h=2 * H)[:, h, :],
                                         -slope(h), None, ALU.mult))
            me.did(dve.memset(u[:, 0:PAD], 0.0))

            def k_spread(m):
                src = stat[:, 2, :].rearrange("p (t h) -> p t h", h=2 * H)[:, :, H + 2 * m:H + 2 * m + 2]
                if m >= 2:
                    dve.wait_ge(kroot_t, m - 1)
                me.did(copy_of(kroot[:, m % 2, :].rearrange("p (t h d) -> p t h d", t=NT, h=2),
                               src.unsqueeze(3).to_broadcast([P, NT, 2, HD])), kroot_ok)

            def k_normed(m):
                dve.wait_ge(kroot_t, m + 1)
                dve.wait_ge(drained["act"], drained_count[sch.chunk["k", m]][1])
                if m >= 2:
                    me.settle()
                    dve.wait_ge(k_hi, m - 1)
                me.did(dve.scalar_tensor_tensor(out=knorm[:, m % 2, :], in0=kraw[:, m, :], scalar=vec[:, 77:78],
                                                in1=SC[m % 2][:, :], op0=ALU.mult, op1=ALU.mult), kn_ok)

            def k_low(m):
                dve.wait_ge(k_hi, m + 1)
                low_of(kT[:, 1, m, :], knorm[:, m % 2, :], kT[:, 0, m, :], k_lo)

            def mixed(g):
                dve.wait_ge(part_hi, 4 + KA + g + 1)
                me.did(dve.scalar_tensor_tensor(out=mix[:, 1, g, :], in0=bank(("mg", g))[:, :],
                                                scalar=vec[:, 72 + g:73 + g], in1=mix[:, 0, g, :].bitcast(F32),
                                                op0=ALU.mult, op1=ALU.subtract), drained["dve"])

            for g, window in enumerate(WINDOWS):
                me.settle()
                k_spread(g)
                dve.wait_ge(drained["act"], drained_count[sch.chunk["u", g]][1])
                src, have, n = u, 1, 0
                while have < window:
                    me.settle()
                    me.did(dve.tensor_tensor(wsum[n % 2][:, 2 * have - 1:], src[:, 2 * have - 1:],
                                             src[:, have - 1:PAD + S - have], ALU.add))
                    src, have, n = wsum[n % 2], 2 * have, n + 1
                if g:
                    dve.wait_ge(p_hi, g)
                me.settle()
                me.did(dve.scalar_tensor_tensor(out=pmean[:, window - 1:], in0=src[:, PAD + window - 1:],
                                                scalar=1.0 / window, in1=u[:, PAD + window - 1:],
                                                op0=ALU.mult, op1=ALU.subtract))
                me.did(dve.tensor_tensor(pmean[:, 0:window - 1], src[:, PAD:PAD + window - 1], invn[:, 0:window - 1],
                                         ALU.mult))
                me.settle()
                me.did(dve.tensor_tensor(pmean[:, 0:window - 1], pmean[:, 0:window - 1], u[:, PAD:PAD + window - 1],
                                         ALU.subtract), p_ok)
                if g:
                    mixed(g - 1)
                k_normed(g)
                dve.wait_ge(p_hi, g + 1)
                low_of(pooled[:, 1, :], pmean[:, :], pooled[:, 0, :], p_lo)
                k_low(g)
            mixed(KA - 1)

            for t in range(SLOTS):
                if t >= 7 and t % NT == 3:
                    h = t // NT - 1
                    dve.wait_ge(head_lo, h + 1)
                    r = (h % 2) * HD
                    me.did(dve.tensor_tensor(araw[r:r + HD, :], OB[0:HD, :], araw[r:r + HD, :], ALU.add), head_ok)
                if t < STEPS:
                    h, i = divmod(t, NT)
                    n = (i + 1) * P
                    dve.wait_ge(score, t + 1)
                    if t >= 2:
                        dve.wait_ge(exp_ok, t - 1)
                    me.settle()
                    me.did(dve.scalar_tensor_tensor(out=logit[:, t % 2, 0:n], in0=dsel[:, offset(i):offset(i + 1)],
                                                    scalar=alibi[:, i * H + h:i * H + h + 1], in1=SC[t % 2][:, 0:n],
                                                    op0=ALU.mult, op1=ALU.add), logit_ok)
                    me.settle()
                    me.did(dve.tensor_reduce(smax[:, t:t + 1], logit[:, t % 2, 0:n], AX_X, ALU.max))
                    me.settle()
                    r = i * 2 * H + h
                    me.did(dve.tensor_scalar(sbias[:, t:t + 1], smax[:, t:t + 1], stat[:, 2, r:r + 1], -1.0,
                                             ALU.mult, ALU.mult), bias_ok)
                if 1 <= t < STEPS + 1:
                    n = ((t - 1) % NT + 1) * P
                    dve.wait_ge(exp_ok, t)
                    me.did(dve.reciprocal(sinv[:, t - 1:t], ssum[:, t - 1:t]))
                    me.settle()
                    me.did(dve.tensor_scalar(prob[:, (t - 1) % 2, 0:n], prob[:, (t - 1) % 2, 0:n],
                                             sinv[:, t - 1:t], None, ALU.mult), prob_ok)
                if 2 <= t < STEPS + 2:
                    n = ((t - 2) % NT + 1) * P
                    dve.wait_ge(pt_hi, t - 1)
                    low_of(pT[:, t % 2, 1, 0:n], PT[t % 2][:, 0:n], pT[:, t % 2, 0, 0:n], pt_lo)
                if t >= 12 and t % (2 * NT) == NT:
                    m = t // (2 * NT) - 1
                    dve.wait_ge(pair_hi, m + 1)
                    low_of(qT[:, 1, m, :], araw[:, :], qT[:, 0, m, :], pair_lo)
                if t % 2 == 1 and t < STEPS:
                    name = filler(t - 1)
                    if name[0] == "pb":
                        m = name[1]
                        await_chunk(dve, name)
                        dve.wait_ge(drained["act"], drained_count[sch.chunk["gp", m]][1])
                        me.did(dve.scalar_tensor_tensor(out=ypool[:, m, :], in0=ypool[:, m, :], scalar=1.0,
                                                        in1=bank(name)[:, :], op0=ALU.add, op1=ALU.mult),
                               drained["dve"])
                    elif name[1] % 2:
                        mod_rows(2, name[1] // 2)
            mod_vector(2)

            def merged_low(m):
                dve.wait_ge(m_hi, m + 1)
                me.did(dve.scalar_tensor_tensor(out=merged[:, 1, m, :], in0=msum[:, m % 2, :], scalar=0.5,
                                                in1=merged[:, 0, m, :].bitcast(F32), op0=ALU.mult, op1=ALU.subtract),
                       m_lo)

            for m in range(KD):
                p = m // 2
                j = 3 + p // 2
                if m % 2 == 0:
                    mod_rows(j, 2 * (p % 2))
                await_chunk(dve, ("ab", m))
                dve.wait_ge(drained["act"], drained_count[sch.chunk["ga", m]][1])
                if m >= 2:
                    dve.wait_ge(m_lo, m - 1)
                me.did(dve.scalar_tensor_tensor(out=msum[:, m % 2, :], in0=tga[:, m % 2, :], scalar=1.0,
                                                in1=bank(("ab", m))[:, :], op0=ALU.add, op1=ALU.mult), drained["dve"])
                me.settle()
                me.did(dve.tensor_tensor(msum[:, m % 2, :], msum[:, m % 2, :], ypool[:, m, :], ALU.add), m_ok)
                if m:
                    merged_low(m - 1)
                if m % 2:
                    mod_rows(j, 2 * (p % 2) + 1)
                    if p % 2:
                        mod_vector(j)
            merged_low(KD - 1)

            for m in range(KD):
                await_chunk(dve, ("wo", m))
                me.did(dve.scalar_tensor_tensor(out=xT[:, m, :], in0=bank(("wo", m))[:, :],
                                                scalar=mod[:, 2 * KD + m:2 * KD + m + 1], in1=xT[:, m, :],
                                                op0=ALU.mult, op1=ALU.add), drained["dve"])
                if m % 2 and m < KD - 1:
                    mod_rows(5, m // 2)
            dve.wait_ge(x2_sum, KD)
            me.did(dve.tensor_reduce(tstat[:, 0, :], OB[:, 0:KD * NT].rearrange("p (m t) -> p t m", t=NT), AX_X,
                                     ALU.add))
            me.settle()
            roots(1)
            norm(1, 3)
            mod_rows(5, KD // 2 - 1)
            mod_vector(5)

            def first_taps(kind, m, y):
                col = m if kind == "ua" else KF + m
                dve.wait_ge(y_tap, 2 * m + (1 if kind == "ua" else 2))
                for back in (1, 2):
                    if back == 2:
                        me.settle()
                    w = conv[:, (TAPS - 1 - back) * 2 * KF + col:(TAPS - 1 - back) * 2 * KF + col + 1]
                    me.did(dve.scalar_tensor_tensor(out=y[:, m % 2, back:], in0=bank((kind, m))[:, 0:S - back],
                                                    scalar=w, in1=y[:, m % 2, back:], op0=ALU.mult, op1=ALU.add),
                           drained["dve"] if back == 2 else None)

            def gu_low(m):
                dve.wait_ge(gu_hi, m + 1)
                low_of(guT[:, 1, m, :], ya[:, m % 2, :], guT[:, 0, m, :], gu_lo)

            for m in range(KF):
                first_taps("ua", m, ya)
                if m:
                    gu_low(m - 1)
                first_taps("ub", m, yb)
                dve.wait_ge(silu_ok, m + 1)
                me.settle()
                me.did(dve.tensor_tensor(ya[:, m % 2, :], ya[:, m % 2, :], yb[:, m % 2, :], ALU.mult), g_ok)
            gu_low(KF - 1)
            for m in range(KD):
                await_chunk(dve, ("dn", m))
                me.did(dve.scalar_tensor_tensor(out=xT[:, m, :], in0=bank(("dn", m))[:, :],
                                                scalar=mod[:, 5 * KD + m:5 * KD + m + 1], in1=xT[:, m, :],
                                                op0=ALU.mult, op1=ALU.add), drained["dve"])

        @block.tensor
        def _(pe):
            def unit_products(n, out_bank, rhs, k0, first, last):
                nk = sch.units[n][0]
                hi, lo = unit_split(n, 0), unit_split(n, 1)
                pe.wait_ge(high, n + 1)
                for k in range(nk):
                    for part in range(2):
                        pe.matmul(out_bank[:, :], hi[:, k, :], rhs[:, part, k0 + k, :],
                                  start=first and k == 0 and part == 0, stop=False)
                pe.wait_ge(low, n + 1)
                for k in range(nk):
                    mm = pe.matmul(out_bank[:, :], lo[:, k, :], rhs[:, 0, k0 + k, :], start=False,
                                   stop=last and k == nk - 1)
                mm.then_inc(used, 1)

            def product(name, rhs, k0=0):
                await_bank(pe, name)
                unit_products(sch.unit[name], bank(name), rhs, k0, True, True)

            pe.wait_ge(consts, 11)
            pe.wait_ge(rows_in, 16 * ROW_LOADS)
            pe.transpose(OB[:, 0:78], rows[0:78, 0, :], ident[0:78, 0:78])
            pe.transpose(OB[:, P:2 * P], rows[:, 1, :], ident[:, :])
            left = (TAPS + 1) * 2 * KF - P
            pe.transpose(OB[:, 2 * P:2 * P + left], rows[0:left, 2, :], ident[0:left, 0:left]).then_inc(rows_t, 1)
            pe.wait_ge(x_in, 16 * NT)
            for k in range(KD):
                if k >= 4:
                    pe.wait_ge(x_kept[k % 2], (k - 4) // 2 + 1)
                for t in range(NT):
                    mm = pe.transpose((SC + PT)[k % 4][:, t * P:(t + 1) * P], xn[:, t, k * P:(k + 1) * P],
                                      ident[:, :])
                mm.then_inc(x_t, 1)

            def spread_roots(which):
                pe.wait_ge(diag_ok, NT * (which + 1))
                for t in range(NT):
                    mm = pe.matmul(SC[0][:, t * P:(t + 1) * P], ones[:, :], diag[:, t, :], start=True, stop=True)
                mm.then_inc(root_b, 1)

            def mod_columns(j):
                pe.wait_ge(mod_sum, KD * (j + 1))
                if j:
                    pe.wait_ge(mod_ok, j)
                for k in range(KD):
                    mm = pe.matmul(OB[:, MC + k:MC + k + 1], macc[:, k * P:(k + 1) * P], ones[:, 0:1],
                                   start=True, stop=True)
                mm.then_inc(mod_col, 1)

            pe.wait_ge(x_kept[0], KD // 2)
            pe.wait_ge(vecs, 1)
            spread_roots(0)
            mod_columns(0)
            mod_columns(1)
            pe.wait_ge(h_lo, KD)
            pe.wait_ge(h_hi, KD)
            for m in range(2):
                product(("qi", m), hT)
            product(("kw", 0), hT)
            pe.wait_ge(wi_row, 1)
            for t in range(NT):
                mm = pe.transpose(OB[:, WC + t * IH:WC + (t + 1) * IH], wiT[0:IH, t * P:(t + 1) * P],
                                  ident[0:IH, 0:IH])
            mm.then_inc(wi_t, 1)

            THREE = ((0, 0), (0, 1), (1, 0))

            def indexer(i):
                for h in range(IH):
                    n = (i - 1) * IH + h
                    if n == 0:
                        await_drained(pe, ("kw", 0))
                    if n >= 2:
                        pe.wait_ge(i_relu, n - 1)
                    r = slice((h % 2) * HD, (h % 2 + 1) * HD)
                    for a, b in THREE:
                        mm = pe.matmul(SC[n % 2][:, 0:(i + 1) * P], qiT[r, a, h // 2, i * P:(i + 1) * P],
                                       kiT[r, b, 0:(i + 1) * P], start=(a, b) == (0, 0), stop=a == 1)
                    mm.then_inc(i_dot, 1)

            def squares(n):
                pe.wait_ge(sq_ok, n + 1)
                if n == 0:
                    pe.wait_ge(wi_ok, 1)
                for t in range(NT):
                    mm = pe.matmul(OB[:, t * 2 * H + 2 * n:t * 2 * H + 2 * n + 2], sq[:, n % 2, t * P:(t + 1) * P],
                                   halves[:, :], start=True, stop=True)
                mm.then_inc(sq_used, 1)

            for n in range(2 * KA):
                product(("q", n) if n < KA else ("k", n - KA), hT)
                if n:
                    squares(n - 1)
                if 1 <= n < NT:
                    indexer(n)

            def v_turn(m):
                pe.wait_ge(drained["act"], drained_count[sch.chunk["v", m]][1])
                if m >= 2:
                    pe.wait_ge(v_lo, m - 1)
                for t in range(NT):
                    mm = pe.transpose(PT[m % 2][:, t * P:(t + 1) * P], vraw[:, m % 2, t * P:(t + 1) * P], ident[:, :])
                mm.then_inc(v_t, 1)

            for m in range(KA):
                product(("v", m), hT)
                if m:
                    v_turn(m - 1)
                else:
                    squares(2 * KA - 1)

            def k_turn(m):
                pe.wait_ge(kroot_ok, m + 1)
                if m >= 2:
                    pe.wait_ge(kn_ok, m - 1)
                for t in range(NT):
                    mm = pe.transpose(SC[m % 2][:, t * P:(t + 1) * P], kroot[:, m % 2, t * P:(t + 1) * P], ident[:, :])
                mm.then_inc(kroot_t, 1)

            def group(g):
                pe.wait_ge(p_lo, g + 1)
                product(("mg", g), pooled[:, :, :].rearrange("p a (k n) -> p a k n", k=1))

            product(("u", 0), hT)
            v_turn(KA - 1)
            for g in range(1, KA):
                product(("u", g), hT)
                k_turn(g - 1)
                group(g - 1)
            k_turn(KA - 1)
            group(KA - 1)

            for t in range(SLOTS):
                if t < STEPS:
                    h, i = divmod(t, NT)
                    r = slice((h % 2) * HD, (h % 2 + 1) * HD)
                    if t == 0:
                        pe.wait_ge(k_lo, KA)
                    if t >= 2:
                        pe.wait_ge(logit_ok, t - 1)
                    for a, b in THREE:
                        mm = pe.matmul(SC[t % 2][:, 0:(i + 1) * P], qT[r, a, h // 2, i * P:(i + 1) * P],
                                       kT[r, b, h // 2, 0:(i + 1) * P], start=(a, b) == (0, 0), stop=a == 1)
                    mm.then_inc(score, 1)
                if 2 <= t < STEPS + 2:
                    i = (t - 2) % NT
                    pe.wait_ge(prob_ok, t - 1)
                    if t >= 4:
                        pe.wait_ge(pt_lo, t - 3)
                    for j in range(i + 1):
                        mm = pe.transpose(PT[t % 2][:, j * P:(j + 1) * P], prob[:, t % 2, j * P:(j + 1) * P],
                                          ident[:, :])
                    mm.then_inc(prob_t, 1)
                if t % 2 == 0 and t < STEPS:
                    name = filler(t)
                    product(name, hT if name[0] == "gp" else mix)
                if 3 <= t < STEPS + 3:
                    h, i = divmod(t - 3, NT)
                    pe.wait_ge(pt_lo, t - 2)
                    if i == 0 and h:
                        pe.wait_ge(head_ok, h)
                    for j in range(i + 1):
                        for part in range(2):
                            mm = pe.matmul(OB[:, i * P:(i + 1) * P], vS[:, j, h, :, :],
                                           pT[:, (t - 1) % 2, part, j * P:(j + 1) * P],
                                           start=j == 0 and part == 0, stop=j == i and part == 1)
                    mm.then_inc(pv_ok, 1)
            pe.wait_ge(head_ok, H)
            mod_columns(2)
            for m in range(0, KD, 2):
                for n in (m, m + 1):
                    product(("ga", n), hT)
                if m == 4:
                    mod_columns(3)
                if m == 0:
                    pe.wait_ge(pair_lo, NPAIR)
                for n in (m, m + 1):
                    product(("ab", n), qT)

            def token_squares(m):
                pe.wait_ge(x2_sq, m + 1)
                if m == 0:
                    pe.wait_ge(mod_ok, 5)
                for t in range(NT):
                    mm = pe.matmul(OB[:, m * NT + t:m * NT + t + 1], sq2[:, m % 2, t * P:(t + 1) * P], ones[:, 0:1],
                                   start=True, stop=True)
                mm.then_inc(x2_sum, 1)

            mod_columns(4)
            pe.wait_ge(m_lo, KD)
            for m in range(KD):
                product(("wo", m), merged)
                if m:
                    token_squares(m - 1)
            token_squares(KD - 1)
            spread_roots(1)

            pe.wait_ge(h_lo, 2 * KD)
            for m in range(KF):
                product(("ua", m), hT)
                product(("ub", m), hT)
                if m == 0:
                    mod_columns(5)

            def out_turn(m):
                pe.wait_ge(drained["dve"], drained_count[sch.chunk["dn", m]][1])
                if m >= 2:
                    pe.wait_ge(out_ok, m - 1)
                for t in range(NT):
                    mm = pe.transpose(PT[m % 2][:, t * P:(t + 1) * P], xT[:, m, t * P:(t + 1) * P], ident[:, :])
                mm.then_inc(out_t, 1)

            for m in range(0, KD, 2):
                n = sch.unit["dn", m] - 4
                for k0 in range(0, KF, KD):
                    pe.wait_ge(gu_lo, min(k0 + KD, KF))
                    for half in range(2):
                        if k0 == 0:
                            await_bank(pe, ("dn", m + half))
                        unit_products(n, bank(("dn", m + half)), guT, k0, k0 == 0, k0 + KD >= KF)
                        n += 1
                    if m and k0 == 0:
                        out_turn(m - 2)
                        out_turn(m - 1)
            out_turn(KD - 2)
            out_turn(KD - 1)


_INS = ['x', 'c', 'w_ada', 'b_ada', 'norm1_g', 'w_in', 'q_norm_g', 'k_norm_g', 'w_attn_br', 'w_pool_grp', 'pool_scale',
        'w_pool_br', 'w_out', 'norm2_g', 'w_up', 'conv_w', 'conv_b', 'w_down']
_OUTS = [((1, 512, 1024), 'float32')]


def kernel(**inputs):
    import numpy as _np
    import concourse.bacc as _bacc
    from concourse import mybir as _mybir
    from concourse.bass_utils import run_bass_kernel_spmd as _run

    nc = _bacc.Bacc("TRN2", target_bir_lowering=False, num_devices=1)
    arrays, args = {}, []
    for name in _INS:
        a = _np.ascontiguousarray(inputs[name])
        arrays[f"in_{name}_dram"] = a
        args.append(nc.dram_tensor(f"in_{name}_dram", a.shape, _mybir.dt.from_np(a.dtype), kind="ExternalInput").ap())
    for i, (shape, dtype) in enumerate(_OUTS):
        dt = _mybir.dt.from_np(_np.dtype(dtype))
        args.append(nc.dram_tensor(f"out_{i}_dram", shape, dt, kind="ExternalOutput").ap())
    build_layer(nc, *args)
    r = _run(nc, [arrays], core_ids=[0])
    got = tuple(r.results[0][f"out_{i}_dram"] for i in range(len(_OUTS)))
    return got[0]
```

```python
from contextlib import ExitStack

import concourse.bass as bass
from concourse import mybir

F32 = mybir.dt.float32
F32R = mybir.dt.float32r
ALU = mybir.AluOpType
ACT = mybir.ActivationFunctionType
AX_X = mybir.AxisListType.X

P = 128
S, D, FF = 512, 1024, 2816
H, HD = 8, 64
IH = 4
TOPK = 128
TAPS = 3
EPS = 1e-6
NT = S // P
KD = D // P
KA = H * HD // P
KF = FF // P
NPAIR = H // 2
WINDOWS = (2, 4, 8, 16)
PAD = 16
WU = KD * P

C_Q, C_K, C_V, C_QI, C_KI = 0, 512, 1024, 1536, 1792
C_U = C_KI + HD + IH
C_GA, C_GP = C_U + 512, C_U + 512 + D

V_ADA, V_NORM1, V_NORM2, V_POOL, V_Q, V_K, V_END = 0, 48, 56, 64, 68, 69, 70

BIG = 1e32
FUTURE = -3.0e38
TAKEN = -3.4e38
TAKEN_BELOW = -3.2e38

NSTAGE = 3
NRING = 3
NBANK = 3


def slope(h):
    return 2.0 ** (-8.0 * (h + 1) / H)


def offset(i):
    return i * (i + 1) // 2 * P


NPAIRS = offset(NT)
STEPS = NT * H
SLOTS = STEPS + 5
ORDER = (0, 3, 1, 2)
MC, WC = 480, NT * 2 * H
MOD2_SLOT = STEPS // 2 + 2
ROW_LOADS = 11


def step_of(t):
    return t // NT, ORDER[t % NT]


def filler(t):
    if t < STEPS:
        p, n = divmod(t // 2, 4)
        return ("gp" if n < 2 else "pb", 2 * p + n % 2), "low" if t % 2 else "high"
    return {STEPS: (("ga", 0), "high"), STEPS + 1: (("ga", 0), "low"),
            STEPS + 3: (("ga", 1), "high"), STEPS + 4: (("ga", 1), "low")}.get(t)


class Schedule:

    def __init__(self):
        self.items = []
        self.units = []
        self.unit = {}
        self.chunk = {}
        self.drains = []
        self.last_use = []
        self.item_of = []
        self.mods = KD

    def mod(self, j, q):
        self.items.append(("mod", j, q))
        self.mods += 2
        self.last_use.append(("mod", self.mods))

    def load(self, w, columns, k0, k1, names):
        self.items.append(("w", w, columns, k0, k1))
        for part, name in enumerate(names):
            self.units.append((k1 - k0, part))
            self.item_of.append(len(self.items) - 1)
            if name is not None:
                self.unit[name] = len(self.units) - 1
        self.last_use.append(("unit", len(self.units)))

    def opens(self, *named):
        for name, drain in named:
            self.chunk[name] = len(self.chunk)
            self.drains.append(drain)

    def group(self, g):
        self.units.append((1, g))
        self.item_of.append(None)
        self.unit["mg", g] = len(self.units) - 1
        self.opens((("mg", g), "dve"))

    def pair(self, w, kind, m, c0, nk, drain):
        self.load(w, (c0 + m * P,), 0, nk, [(kind, m), (kind, m + 1)])
        self.opens(((kind, m), drain), ((kind, m + 1), drain))


def schedule():
    s = Schedule()
    s.pair("in", "qi", 0, C_QI, KD, "dve")
    s.load("in", (C_KI,), 0, KD, [("kw", 0)])
    s.opens((("kw", 0), "dve"))
    for kind, c0, drain in (("q", C_Q, "dve"), ("k", C_K, "act")):
        for m in range(0, KA, 2):
            s.pair("in", kind, m, c0, KD, drain)
    staged = {}
    for kind, m in (("u", 0), ("u", 1), ("u", 2), ("mg", 0), ("u", 3), ("mg", 1), ("v", 0), ("mg", 2), ("v", 1),
                    ("mg", 3), ("v", 2), ("v", 3)):
        if kind == "mg":
            s.group(m)
            continue
        if m % 2 == 0:
            s.items.append(("w", "in", ((C_U if kind == "u" else C_V) + m * P,), 0, KD))
            s.last_use.append(None)
            staged[kind] = len(s.items) - 1
        s.units.append((KD, m % 2))
        s.item_of.append(staged[kind])
        s.unit[kind, m] = len(s.units) - 1
        s.opens(((kind, m), "act"))
        if m % 2:
            s.last_use[staged[kind]] = ("unit", len(s.units))
    for p in range(KD // 2):
        s.pair("in", "gp", 2 * p, C_GP, KD, "act")
        s.mod(2 + p // 2, 2 * (p % 2))
        s.pair("pb", "pb", 2 * p, 0, KA, "dve")
        s.mod(2 + p // 2, 2 * (p % 2) + 1)
    for p in range(KD // 2):
        s.pair("in", "ga", 2 * p, C_GA, KD, "act")
        s.mod(4, p)
        s.pair("ab", "ab", 2 * p, 0, KA, "dve")
    for p in range(KD // 2):
        s.pair("out", "wo", 2 * p, 0, KD, "dve")
        s.mod(5, p)
    for m in range(KF):
        s.load("up", (m * P, FF + m * P), 0, KD, [("ua", m), ("ub", m)])
        s.opens((("ua", m), "dve"), (("ub", m), "dve"))
    for m in range(0, KD, 2):
        for k0 in range(0, KF, KD):
            k1 = min(k0 + KD, KF)
            last = k1 == KF
            s.load("down", (m * P,), k0, k1, [("dn", m) if last else None, ("dn", m + 1) if last else None])
        s.opens((("dn", m), "dve"), (("dn", m + 1), "dve"))
    return s


def build_layer(nc, x, c, w_ada, b_ada, norm1_g, w_in, q_norm_g, k_norm_g, w_attn_br, w_pool_grp, pool_scale,
                w_pool_br, w_out, norm2_g, w_up, conv_w, conv_b, w_down, out):
    sch = schedule()
    drained_count = []
    so_far = {"act": 0, "dve": 0}
    for who in sch.drains:
        so_far[who] += 1
        drained_count.append((who, so_far[who]))

    ada = w_ada[0].rearrange("(k p) n -> p k n", p=P)
    weights = {
        "in": w_in[0].rearrange("(k p) n -> p k n", p=P),
        "ab": w_attn_br[0].rearrange("(k p) n -> p k n", p=P),
        "pb": w_pool_br[0].rearrange("(k p) n -> p k n", p=P),
        "out": w_out[0].rearrange("(k p) n -> p k n", p=P),
        "up": w_up[0].rearrange("(k p) n -> p k n", p=P),
        "down": w_down[0].rearrange("(k p) n -> p k n", p=P),
    }
    out_v = out[0].rearrange("(t p) f -> p t f", p=P)

    with ExitStack() as ctx:
        at = [nc.sbuf_base + (-nc.sbuf_base) % 32]

        def place(name, shape, dt, where=None):
            size = 4
            for n in shape[1:]:
                size *= n
            if where is None:
                where = at[0]
                at[0] += size + (-size) % 32
            return nc.alloc_sbuf_tensor_at(name, shape, dt, offset=where)

        xT = place("xT", [P, KD, S], F32)
        wsplit = place("wsplit", [P, NRING, 2, WU], F32R)
        stage = place("stage", [P, NSTAGE, 2 * WU], F32)
        ident = place("ident", [P, P], F32)
        ones = place("ones", [P, P], F32)
        halves = place("halves", [P, 2], F32)
        vec = place("vec", [P, V_END], F32)
        conv = place("conv", [P, (TAPS + 1) * 2 * KF], F32)
        csil = place("csil", [P, KD], F32)
        qgain = place("qgain", [P, 1], F32)
        mod = place("mod", [P, 6 * KD], F32)
        gs = place("gs", [P, 2, KD], F32)
        invn = place("invn", [P, PAD], F32)
        stat = place("stat", [P, 3, NT * 2 * H], F32)
        tstat = place("tstat", [P, 4, NT], F32)
        alibi = place("alibi", [P, NT * H], F32)
        wi = place("wi", [P, NT * IH], F32)
        top8 = place("top8", [P, NT, 8], F32)
        smax = place("smax", [P, STEPS], F32)
        sbias = place("sbias", [P, STEPS], F32)
        ssum = place("ssum", [P, STEPS], F32)
        sinv = place("sinv", [P, STEPS], F32)

        hT_at = at[0]
        hT = place("hT", [P, 2, KD, S], F32R)
        K1 = 1024
        base = at[0]
        assert base + 107 * K1 <= nc.sbuf_usable_end, (base, nc.sbuf_usable_end)

        def arena(name, shape, dt, kb):
            return place(name, shape, dt, base + int(kb * K1))

        xn = arena("xn", [P, NT, D], F32, 0)
        rows = arena("rows", [P, 3, P], F32, 20)
        crow = arena("crow", [KD, P], F32, 22)
        mrow = arena("mrow", [1, D], F32, 32)
        junk = arena("junk", [P, 2, D], F32, 24)
        ada_first = [[place(f"ada{q}_{j}", [P, 2, D], F32,
                            hT_at + n * 8 * K1 if n < 4 else base + (36, 44, 52, 64)[n - 4] * K1)
                      for j, n in enumerate((2 * q, 2 * q + 1))] for q in range(KD // 2)]
        qT = arena("qT", [P, 2, KA, S], F32R, 0)
        kT = arena("kT", [P, 2, KA, S], F32R, 16)
        vS = arena("vS", [P, NT, H, 2, HD], F32R, 32)
        kraw = arena("kraw", [P, KA, S], F32, 48)
        sq = arena("sq", [P, 2, S], F32, 56)
        dist = arena("dist", [P, S], F32, 60)
        wgrp = arena("wgrp", [P, KA, P], F32, 62)
        qiT = arena("qiT", [P, 2, 2, S], F32R, 64)
        kiT = arena("kiT", [P, 2, S], F32R, 72)
        vraw = arena("vraw", [P, 2, S], F32, 28)
        wiT = arena("wiT", [P, S], F32, 84)
        cap = arena("cap", [P, P], F32, 86.5)
        dsel = arena("dsel", [P, NPAIRS], F32, 88)
        iscore = arena("iscore", [P, NPAIRS - P], F32, 93)
        work = arena("work", [P, NPAIRS - P], F32, 97.5)
        relu = arena("relu", [P, 2, S], F32, 102)
        kroot = arena("kroot", [P, 2, S], F32, 80)
        knorm = arena("knorm", [P, 2, S], F32, 84)
        u = [arena(f"u{n}", [P, PAD + S], F32, 16 + 2.0625 * n) for n in range(2)]
        wsum = [arena(f"wsum{n}", [P, PAD + S], F32, 20.125 + 2.0625 * n) for n in range(2)]
        pmean = arena("pmean", [P, S], F32, 24.25)
        pooled = arena("pooled", [P, 2, S], F32R, 103)
        mix = arena("mix", [P, 2, KA, S], F32R, 64)
        ypool = arena("ypool", [P, KD, S], F32, 48)
        pT = arena("pT", [P, 2, 2, S], F32R, 80)
        logit = arena("logit", [P, 2, S], F32, 93)
        prob = arena("prob", [P, 2, S], F32, 97)
        araw = arena("araw", [P, S], F32, 101)
        macc = arena("macc", [P, D], F32, 103)
        nrm = arena("nrm", [P, 2, S], F32, 97)
        diag = arena("diag", [P, NT, P], F32, 101)
        merged = arena("merged", [P, 2, KD, S], F32R, 16)
        tga = arena("tga", [P, 2, S], F32, 88)
        msum = arena("msum", [P, 2, S], F32, 84)
        sq2 = arena("sq2", [P, 2, S], F32, 80)
        guT = arena("guT", [P, 2, KF, S], F32R, 0)
        ya = arena("ya", [P, 2, S], F32, 88)
        yb = arena("yb", [P, 2, S], F32, 92)
        ost = arena("ost", [P, 2, NT, P], F32, 96)

        banks = [ctx.enter_context(nc.psum_tensor(f"bank{n}", [P, S], F32)) for n in range(8)]
        SC, PT, OB = banks[3:5], banks[5:7], banks[7]

        def sem(name):
            return ctx.enter_context(nc.semaphore(name))

        rows_in = sem("rows_in")
        x_in = sem("x_in")
        wgrp_in = sem("wgrp_in")
        ada_in = [[sem(f"ada_in{q}_{j}") for j in range(2)] for q in range(KD // 2)]
        stage_in = [sem(f"stage_in{n}") for n in range(NSTAGE)]
        stored = [sem(f"stored{n}") for n in range(2)]
        consts = sem("consts")
        vecs = sem("vecs")
        high = sem("high")
        low = sem("low")
        used = sem("used")
        drained = {"act": sem("drained_act"), "dve": sem("drained_dve")}
        act_step = sem("act_step")
        dve_step = sem("dve_step")
        rows_t = sem("rows_t")
        c_in = sem("c_in")
        c_t = sem("c_t")
        c_silu = sem("c_silu")
        x_sum = sem("x_sum")
        x_t = sem("x_t")
        x_kept = [sem("x_kept_even"), sem("x_kept_odd")]
        mean_ok = sem("mean_ok")
        root_ok = sem("root_ok")
        diag_ok = sem("diag_ok")
        root_b = sem("root_b")
        mod_sum = sem("mod_sum")
        mod_first = sem("mod_first")
        mod_row = sem("mod_row")
        mod_turn = sem("mod_turn")
        mod_col = sem("mod_col")
        mod_ok = sem("mod_ok")
        n_ok = sem("n_ok")
        h_hi = sem("h_hi")
        h_lo = sem("h_lo")
        sq_ok = sem("sq_ok")
        sq_used = sem("sq_used")
        qk_mean = sem("qk_mean")
        qk_root = sem("qk_root")
        qk_inv = sem("qk_inv")
        kroot_ok = sem("kroot_ok")
        kroot_t = sem("kroot_t")
        kn_ok = sem("kn_ok")
        k_hi = sem("k_hi")
        k_lo = sem("k_lo")
        part_hi = sem("part_hi")
        wi_t = sem("wi_t")
        wi_row = sem("wi_row")
        wi_ok = sem("wi_ok")
        i_dot = sem("i_dot")
        i_relu = sem("i_relu")
        i_sum = sem("i_sum")
        sel_ok = sem("sel_ok")
        v_t = sem("v_t")
        v_hi = sem("v_hi")
        v_lo = sem("v_lo")
        w_step = sem("w_step")
        w_ok = sem("w_ok")
        pad_ok = sem("pad_ok")
        p_ok = sem("p_ok")
        p_hi = sem("p_hi")
        p_lo = sem("p_lo")
        linear = sem("linear")
        score = sem("score")
        logit_ok = sem("logit_ok")
        bias_ok = sem("bias_ok")
        exp_ok = sem("exp_ok")
        prob_ok = sem("prob_ok")
        prob_t = sem("prob_t")
        pt_hi = sem("pt_hi")
        pt_lo = sem("pt_lo")
        pv_ok = sem("pv_ok")
        head_lo = sem("head_lo")
        head_ok = sem("head_ok")
        pair_hi = sem("pair_hi")
        pair_lo = sem("pair_lo")
        m_ok = sem("m_ok")
        m_hi = sem("m_hi")
        m_lo = sem("m_lo")
        x2_sq = sem("x2_sq")
        x2_sum = sem("x2_sum")
        y_tap = sem("y_tap")
        silu_ok = sem("silu_ok")
        g_ok = sem("g_ok")
        gu_hi = sem("gu_hi")
        gu_lo = sem("gu_lo")
        out_t = sem("out_t")
        out_ok = sem("out_ok")

        class Progress:

            def __init__(self, eng, step):
                self.eng, self.step, self.n, self.last = eng, step, {}, None

            def did(self, ins, signal=None):
                signal = self.step if signal is None else signal
                self.n[id(signal)] = self.n.get(id(signal), 0) + 1
                ins.then_inc(signal, 1)
                self.last = (signal, self.n[id(signal)])
                return self.last

            def settle(self, mark=None):
                signal, n = mark or self.last
                self.eng.wait_ge(signal, n)

        def bank(name):
            return banks[sch.chunk[name] % NBANK]

        def await_chunk(eng, name):
            eng.wait_ge(used, sch.unit[name] + 1)

        def await_drained(eng, name):
            who, n = drained_count[sch.chunk[name]]
            eng.wait_ge(drained[who], n)

        def await_bank(eng, name):
            if sch.chunk[name] >= NBANK:
                who, n = drained_count[sch.chunk[name] - NBANK]
                eng.wait_ge(drained[who], n)

        landed = []
        slot_total = [0] * NSTAGE
        for n, item in enumerate(sch.items):
            slot_total[n % NSTAGE] += 16 * (len(item[2]) if item[0] == "w" else 1)
            landed.append(slot_total[n % NSTAGE])

        def await_item(eng, n):
            eng.wait_ge(stage_in[n % NSTAGE], landed[n])

        def unit_source(n):
            nk, part = sch.units[n]
            item = sch.item_of[n]
            if item is None:
                return wgrp[:, part:part + 1, :]
            slot = stage[:, item % NSTAGE, :]
            if len(sch.items[item][2]) == 2:
                return slot[:, part * WU:part * WU + nk * P].rearrange("p (k n) -> p k n", n=P)
            wide = 2 * P if not (sch.items[item][1] == "in" and sch.items[item][2] == (C_KI,)) else P
            return slot[:, 0:nk * wide].rearrange("p (k n) -> p k n", n=wide)[:, :, part * P:(part + 1) * P]

        def unit_split(n, part):
            nk = sch.units[n][0]
            return wsplit[:, n % NRING, part, 0:nk * P].rearrange("p (k n) -> p k n", n=P)

        block = ctx.enter_context(nc.Block())

        @block.sync
        def _(sp):
            def load_item(n):
                item = sch.items[n]
                if n >= NSTAGE:
                    kind, count = sch.last_use[n - NSTAGE]
                    sp.wait_ge({"mod": mod_sum, "unit": low}[kind], count)
                slot = stage[:, n % NSTAGE, :]
                if item[0] == "mod":
                    _, j, q = item
                    sp.dma_start(slot.rearrange("p (k n) -> p k n", k=2), ada[:, 2 * q:2 * q + 2, j * D:(j + 1) * D]
                                 ).then_inc(stage_in[n % NSTAGE], 16)
                    return
                _, w, columns, k0, k1 = item
                if len(columns) == 2:
                    for part, c0 in enumerate(columns):
                        sp.dma_start(slot[:, part * WU:(part + 1) * WU].rearrange("p (k n) -> p k n", n=P),
                                     weights[w][:, k0:k1, c0:c0 + P]).then_inc(stage_in[n % NSTAGE], 16)
                    return
                c0, = columns
                wide = P if (w, c0) == ("in", C_KI) else 2 * P
                sp.dma_start(slot[:, 0:(k1 - k0) * wide].rearrange("p (k n) -> p k n", n=wide),
                             weights[w][:, k0:k1, c0:c0 + wide]).then_inc(stage_in[n % NSTAGE], 16)

            def load_first(q, j):
                sp.dma_start(ada_first[q][j][:, :, :], ada[:, 2 * q:2 * q + 2, j * D:(j + 1) * D]
                             ).then_inc(ada_in[q][j], 16)

            sp.dma_start(crow[:, :], c[0].rearrange("(k p) -> k p", p=P)).then_inc(c_in, 16)
            for t in range(NT):
                sp.dma_start(xn[:, t, :], x[0, t * P:(t + 1) * P, :]).then_inc(x_in, 16)
            load_first(0, 0)
            for r, src in ((V_ADA, b_ada), (V_NORM1, norm1_g), (V_NORM2, norm2_g), (V_POOL, pool_scale)):
                v = src[0].rearrange("(k p) -> k p", p=P)
                sp.dma_start(rows[r:r + v.shape[0], 0, :], v).then_inc(rows_in, 16)
            load_first(0, 1)
            for r, src in ((V_Q, q_norm_g), (V_K, k_norm_g)):
                for half in range(2):
                    sp.dma_start(rows[r:r + 1, 0, half * HD:(half + 1) * HD], src).then_inc(rows_in, 16)
            load_first(1, 0)
            taps = conv_w[0].rearrange("j (m p) -> (j m) p", p=P)
            sp.dma_start(rows[:, 1, :], taps[0:P, :]).then_inc(rows_in, 16)
            sp.dma_start(rows[0:TAPS * 2 * KF - P, 2, :], taps[P:TAPS * 2 * KF, :]).then_inc(rows_in, 16)
            sp.dma_start(rows[TAPS * 2 * KF - P:(TAPS + 1) * 2 * KF - P, 2, :],
                         conv_b[0].rearrange("(m p) -> m p", p=P)).then_inc(rows_in, 16)
            sp.dma_start(wgrp[:, :, :], w_pool_grp[0].rearrange("g c d -> c g d")).then_inc(wgrp_in, 16)
            for q in range(1, KD // 2):
                for j in range(2):
                    if (q, j) != (1, 0):
                        load_first(q, j)
            for n in range(len(sch.items)):
                load_item(n)
            for m in range(KD):
                sp.wait_ge(out_ok, m + 1)
                sp.dma_start(out_v[:, :, m * P:(m + 1) * P], ost[:, m % 2, :, :]).then_inc(stored[m % 2], 16)
            for n in range(2):
                sp.wait_ge(stored[n], 16 * (KD // 2))

        @block.gpsimd
        def _(pool):
            pool.memset(ident[:, :], 0.0).then_inc(consts, 1)
            pool.memset(cap[:, :], -TAKEN_BELOW).then_inc(consts, 1)
            pool.memset(halves[:, :], 1.0).then_inc(consts, 1)
            pool.memset(ones[:, :], 1.0).then_inc(consts, 1)
            pool.iota(dist[:, :], [[-1, S]], base=(NT - 1) * P, channel_multiplier=1,
                      allow_small_or_imprecise_dtypes=True).then_inc(consts, 1)
            pool.iota(invn[:, :], [[1, PAD]], base=1, channel_multiplier=0,
                      allow_small_or_imprecise_dtypes=True).then_inc(consts, 1)
            pool.wait_ge(consts, 6)
            pool.affine_select(out=ident[:, :], in_=ident[:, :], compare_op=ALU.not_equal, fill=1.0, base=0,
                               pattern=[[-1, P]], channel_multiplier=1).then_inc(consts, 1)
            pool.affine_select(out=cap[:, :], in_=cap[:, :], compare_op=ALU.is_ge, fill=FUTURE, base=0,
                               pattern=[[-1, P]], channel_multiplier=1).then_inc(consts, 1)
            pool.affine_select(out=halves[:, 0:1], in_=halves[:, 0:1], compare_op=ALU.is_gt, fill=0.0, base=HD,
                               pattern=[[0, 1]], channel_multiplier=-1).then_inc(consts, 1)
            pool.affine_select(out=halves[:, 1:2], in_=halves[:, 1:2], compare_op=ALU.is_ge, fill=0.0, base=-HD,
                               pattern=[[0, 1]], channel_multiplier=1).then_inc(consts, 1)
            pool.affine_select(out=dsel[:, 0:P], in_=dist[:, (NT - 1) * P:S], compare_op=ALU.is_ge, fill=BIG, base=0,
                               pattern=[[-1, P]], channel_multiplier=1).then_inc(consts, 1)
            pool.memset(u[0][:, 0:PAD], 0.0).then_inc(pad_ok, 1)
            pool.memset(u[1][:, 0:PAD], 0.0).then_inc(pad_ok, 1)
            summed = [0]

            def low_parts(upto):
                while summed[0] < upto:
                    n = summed[0]
                    pool.wait_ge(high, n + 1)
                    if n >= NRING:
                        pool.wait_ge(used, n - NRING + 1)
                    pool.tensor_tensor(unit_split(n, 1), unit_source(n), unit_split(n, 0).bitcast(F32),
                                       ALU.subtract).then_inc(low, 1)
                    summed[0] += 1

            adds = [0]

            def window_sums(g):
                pool.wait_ge(drained["act"], drained_count[sch.chunk["u", g]][1])
                if g == 0:
                    pool.wait_ge(pad_ok, 2)
                else:
                    pool.wait_ge(p_ok, g)
                src, have = u[g % 2], 1
                while have < WINDOWS[g]:
                    if have > 1:
                        pool.wait_ge(w_step, adds[0])
                    dst = wsum[0] if src is not wsum[0] else wsum[1]
                    last = 2 * have == WINDOWS[g]
                    ins = pool.tensor_tensor(dst[:, 2 * have - 1:], src[:, 2 * have - 1:],
                                             src[:, have - 1:PAD + S - have], ALU.add)
                    if last:
                        ins.then_inc(w_ok, 1)
                    else:
                        ins.then_inc(w_step, 1)
                        adds[0] += 1
                    src, have = dst, 2 * have

            def pooled_low(g):
                pool.wait_ge(p_hi, g + 1)
                pool.tensor_tensor(pooled[:, 1, :], pmean[:, :], pooled[:, 0, :].bitcast(F32),
                                   ALU.subtract).then_inc(p_lo, 1)

            def k_low(m):
                pool.wait_ge(k_hi, m + 1)
                pool.tensor_tensor(kT[:, 1, m, :], knorm[:, m % 2, :], kT[:, 0, m, :].bitcast(F32),
                                   ALU.subtract).then_inc(k_lo, 1)

            def through(name):
                low_parts(sch.unit[name] + 1)

            through(("mg", 0))
            window_sums(0)
            through(("u", 3))
            window_sums(1)
            pooled_low(0)
            through(("mg", 1))
            window_sums(2)
            through(("v", 0))
            pooled_low(1)
            through(("mg", 2))
            window_sums(3)
            through(("v", 1))
            pooled_low(2)
            through(("v", 2))
            pooled_low(3)
            through(("gp", 1))
            k_low(0)
            k_low(1)
            k_low(2)
            k_low(3)
            low_parts(len(sch.units))

        @block.scalar
        def _(act):
            me = Progress(act, act_step)
            made = [0]

            def high_parts(upto):
                while made[0] < min(upto, len(sch.units)):
                    n = made[0]
                    if sch.item_of[n] is None:
                        act.wait_ge(wgrp_in, 16)
                    else:
                        await_item(act, sch.item_of[n])
                    if n >= NRING:
                        act.wait_ge(used, n - NRING + 1)
                        act.wait_ge(low, n - NRING + 1)
                    me.did(act.activation(unit_split(n, 0), unit_source(n), ACT.Copy), high)
                    made[0] += 1

            def chunk(name):
                await_chunk(act, name)
                high_parts(sch.unit[name] + 1 + NRING)

            def store_copy(m):
                act.wait_ge(out_t, m + 1)
                if m >= 2:
                    act.wait_ge(stored[m % 2], 16 * (m // 2))
                me.did(act.activation(ost[:, m % 2, :, :], PT[m % 2][:, :].rearrange("p (t f) -> p t f", t=NT),
                                      ACT.Copy), out_ok)

            act.wait_ge(c_t, 1)
            me.did(act.activation(csil[:, :], banks[2][:, 0:KD], ACT.Silu), c_silu)
            act.wait_ge(x_in, 16 * NT)
            for t in range(NT):
                if t >= 2:
                    act.wait_ge(x_sum, t - 1)
                me.did(act.activation(junk[:, t % 2, :], xn[:, t, :], ACT.Square,
                                      accum_out=tstat[:, 0, t:t + 1]), x_sum)
            for k in range(KD):
                if k % 2 == 0:
                    act.wait_ge(x_t, k + 1)
                    me.did(act.activation(xT[:, k, :], (SC + PT)[k % 4][:, :], ACT.Copy), x_kept[0])
            act.wait_ge(mean_ok, 1)
            me.did(act.activation(tstat[:, 2, :], tstat[:, 1, :], ACT.Sqrt), root_ok)
            for half in range(2):
                act.wait_ge(mod_first, 1)
                me.did(act.activation(mrow[:, half * S:(half + 1) * S], banks[half][0:1, :], ACT.Copy), mod_row)
            high_parts(NRING)

            def h_high(which, shift):
                act.wait_ge(mod_ok, shift + (2 if shift == 0 else 1))
                for k in range(KD):
                    act.wait_ge(n_ok, which * KD + k + 1)
                    me.did(act.activation(hT[:, 0, k, :], nrm[:, k % 2, :], ACT.Identity,
                                          bias=mod[:, shift * KD + k:shift * KD + k + 1]), h_hi)

            h_high(0, 0)
            for m in range(2):
                chunk(("qi", m))
                me.did(act.activation(qiT[:, 0, m, :], bank(("qi", m))[:, :], ACT.Copy), part_hi)
            chunk(("kw", 0))
            b = bank(("kw", 0))
            me.did(act.activation(wiT[0:IH, :], b[HD:HD + IH, :], ACT.Copy), wi_row)
            me.did(act.activation(kiT[0:HD, 0, :], b[0:HD, :], ACT.Copy), part_hi)
            me.did(act.activation(kiT[HD:P, 0, :], b[0:HD, :], ACT.Copy), part_hi)

            def indexer(i):
                for h in range(IH):
                    n = (i - 1) * IH + h
                    act.wait_ge(i_dot, n + 1)
                    if n >= 2:
                        act.wait_ge(i_sum, n - 1)
                    me.did(act.activation(relu[:, n % 2, 0:(i + 1) * P], SC[n % 2][:, 0:(i + 1) * P], ACT.Relu,
                                          scale=HD ** -0.5), i_relu)

            for n in range(2 * KA):
                kind, m = ("q", n) if n < KA else ("k", n - KA)
                name = (kind, m)
                chunk(name)
                if n >= 2:
                    act.wait_ge(sq_used, n - 1)
                me.did(act.activation(sq[:, n % 2, :], bank(name)[:, :], ACT.Square), sq_ok)
                if kind == "q":
                    me.did(act.activation(qT[:, 0, m, :], bank(name)[:, :], ACT.Copy, scale=qgain[:, 0:1]), part_hi)
                    for i in {0: (1, 2), 1: (3,)}.get(m, ()):
                        indexer(i)
                else:
                    me.did(act.activation(kraw[:, m, :], bank(name)[:, :], ACT.Copy), drained["act"])

            def v_high(m):
                act.wait_ge(v_t, m + 1)
                me.did(act.activation(vS[:, :, 2 * m:2 * m + 2, 0, :],
                                      PT[m % 2][:, :].rearrange("p (t h d) -> p t h d", t=NT, h=2), ACT.Copy), v_hi)

            def v_raw(m):
                chunk(("v", m))
                if m >= 2:
                    act.wait_ge(v_t, m - 1)
                me.did(act.activation(vraw[:, m % 2, :], bank(("v", m))[:, :], ACT.Copy), drained["act"])

            def mixed(g):
                name = ("mg", g)
                chunk(name)
                me.did(act.activation(mix[:, 0, g, :], bank(name)[:, :], ACT.Copy,
                                      scale=vec[:, V_POOL + g:V_POOL + g + 1]), part_hi)

            def k_spread(m):
                src = stat[:, 2, :].rearrange("p (t h) -> p t h", h=2 * H)[:, :, H + 2 * m:H + 2 * m + 2]
                if m == 0:
                    act.wait_ge(qk_inv, 1)
                if m >= 2:
                    act.wait_ge(kroot_t, m - 1)
                me.did(act.activation(kroot[:, m % 2, :].rearrange("p (t h d) -> p t h d", t=NT, h=2),
                                      src.unsqueeze(3).to_broadcast([P, NT, 2, HD]), ACT.Copy), kroot_ok)

            def k_high(m):
                act.wait_ge(kn_ok, m + 1)
                me.did(act.activation(kT[:, 0, m, :], knorm[:, m % 2, :], ACT.Copy), k_hi)

            def u_raw(g):
                chunk(("u", g))
                if g >= 2:
                    act.wait_ge(p_ok, g - 1)
                me.did(act.activation(u[g % 2][:, PAD:PAD + S], bank(("u", g))[:, :], ACT.Copy), drained["act"])

            def pooled_high(g):
                act.wait_ge(p_ok, g + 1)
                if g:
                    act.wait_ge(used, sch.unit["mg", g - 1] + 1)
                me.did(act.activation(pooled[:, 0, :], pmean[:, :], ACT.Copy), p_hi)

            u_raw(0)
            act.wait_ge(qk_mean, 1)
            me.did(act.activation(stat[:, 1, :], stat[:, 0, :], ACT.Sqrt), qk_root)
            u_raw(1)
            pooled_high(0)
            u_raw(2)
            mixed(0)
            pooled_high(1)
            u_raw(3)
            mixed(1)
            pooled_high(2)
            v_raw(0)
            mixed(2)
            pooled_high(3)
            v_raw(1)
            v_high(0)
            mixed(3)
            k_spread(0)
            k_spread(1)
            v_raw(2)
            v_high(1)
            k_high(0)
            k_spread(2)
            v_raw(3)
            v_high(2)
            k_high(1)
            k_spread(3)
            v_high(3)
            k_high(2)
            k_high(3)

            def alibi_terms(t):
                h, i = step_of(t)
                n = (i + 1) * P
                if t == 0:
                    act.wait_ge(sel_ok, NT - 1)
                if t >= 2:
                    act.wait_ge(exp_ok, t - 1)
                me.did(act.activation(logit[:, t % 2, 0:n], dsel[:, offset(i):offset(i + 1)], ACT.Copy,
                                      scale=alibi[:, i * H + h:i * H + h + 1]), linear)

            alibi_terms(0)
            def gate(n):
                chunk(("ga", n))
                if n >= 2:
                    act.wait_ge(m_ok, n - 1)
                me.did(act.activation(tga[:, n % 2, :], bank(("ga", n))[:, :], ACT.Tanh, scale=0.5), drained["act"])

            for t in range(SLOTS):
                if t >= 7 and t % NT == 3:
                    h = t // NT - 1
                    act.wait_ge(pv_ok, NT * (h + 1))
                    if h % 2 == 0 and h:
                        act.wait_ge(pair_lo, h // 2)
                    r = (h % 2) * HD
                    me.did(act.activation(araw[r:r + HD, :], OB[HD:P, :], ACT.Copy), head_lo)
                if t < STEPS:
                    if t + 1 < STEPS:
                        alibi_terms(t + 1)
                    h, i = step_of(t)
                    n = (i + 1) * P
                    act.wait_ge(bias_ok, t + 1)
                    if t >= 2:
                        act.wait_ge(prob_t, t - 1)
                    r = i * 2 * H + h
                    me.did(act.activation(prob[:, t % 2, 0:n], logit[:, t % 2, 0:n], ACT.Exp,
                                          bias=sbias[:, t:t + 1], scale=stat[:, 2, r:r + 1],
                                          accum_out=ssum[:, t:t + 1]), exp_ok)
                if 2 <= t < STEPS + 2:
                    n = (step_of(t - 2)[1] + 1) * P
                    act.wait_ge(prob_t, t - 1)
                    if t == 2:
                        act.wait_ge(k_lo, KA)
                    if t >= 4:
                        act.wait_ge(pv_ok, t - 3)
                    me.did(act.activation(pT[:, t % 2, 0, 0:n], PT[t % 2][:, 0:n], ACT.Copy), pt_hi)
                if t >= 12 and t % (2 * NT) == NT:
                    m = t // (2 * NT) - 1
                    act.wait_ge(head_ok, 2 * m + 2)
                    me.did(act.activation(qT[:, 0, m, :], araw[:, :], ACT.Copy), pair_hi)
                if t and filler(t - 1) and filler(t - 1)[1] == "low":
                    name = filler(t - 1)[0]
                    chunk(name)
                    if name[0] == "gp":
                        me.did(act.activation(ypool[:, name[1], :], bank(name)[:, :], ACT.Tanh, scale=0.5),
                               drained["act"])
                    if name[0] == "ga":
                        gate(name[1])
            gate(1)

            def merged_high(m):
                act.wait_ge(m_ok, m + 1)
                me.did(act.activation(merged[:, 0, m, :], msum[:, m % 2, :], ACT.Copy, scale=0.5), m_hi)

            for m in range(0, KD, 2):
                if m:
                    gate(m)
                    gate(m + 1)
                for n in (m, m + 1):
                    chunk(("ab", n))
                    merged_high(n)

            for m in range(KD):
                chunk(("wo", m))
                await_drained(act, ("wo", m))
                if m >= 2:
                    act.wait_ge(x2_sum, m - 1)
                me.did(act.activation(sq2[:, m % 2, :], xT[:, m, :], ACT.Square), x2_sq)
            act.wait_ge(mean_ok, 2)
            me.did(act.activation(tstat[:, 2, :], tstat[:, 1, :], ACT.Sqrt), root_ok)
            h_high(1, 3)

            def last_tap(kind, m, y):
                col = m if kind == "ua" else KF + m
                chunk((kind, m))
                me.did(act.activation(y[:, m % 2, :], bank((kind, m))[:, :], ACT.Identity,
                                      bias=conv[:, TAPS * 2 * KF + col:TAPS * 2 * KF + col + 1],
                                      scale=conv[:, (TAPS - 1) * 2 * KF + col:(TAPS - 1) * 2 * KF + col + 1]), y_tap)

            def gu_high(m):
                act.wait_ge(g_ok, m + 1)
                me.did(act.activation(guT[:, 0, m, :], ya[:, m % 2, :], ACT.Copy), gu_hi)

            for m in range(KF):
                if m >= 2:
                    act.wait_ge(gu_lo, m - 1)
                last_tap("ua", m, ya)
                if m:
                    gu_high(m - 1)
                last_tap("ub", m, yb)
                await_drained(act, ("ua", m))
                me.did(act.activation(ya[:, m % 2, :], ya[:, m % 2, :], ACT.Silu), silu_ok)
            gu_high(KF - 1)

            for m in range(0, KD, 2):
                for n in range(sch.unit["dn", m] - 4, sch.unit["dn", m] + 2):
                    act.wait_ge(used, n + 1)
                    high_parts(n + 1 + NRING)
                    if m and n == sch.unit["dn", m] - 2:
                        for r in (m - 2, m - 1):
                            store_copy(r)
            for r in (KD - 2, KD - 1):
                store_copy(r)

        @block.vector
        def _(dve):
            me = Progress(dve, dve_step)

            def copy_of(out_ap, in_ap):
                return dve.tensor_copy(out_ap, in_ap)

            def vectors():
                dve.wait_ge(rows_t, 1)
                me.did(copy_of(vec[:, :], OB[:, 0:V_END]))
                me.did(copy_of(conv[:, 0:P], OB[:, P:2 * P]))
                me.did(copy_of(conv[:, P:(TAPS + 1) * 2 * KF], OB[:, 2 * P:(TAPS + 1) * 2 * KF + P]))
                me.settle()
                me.did(dve.tensor_scalar(qgain[:, :], vec[:, V_Q:V_Q + 1], HD ** -0.5, None, ALU.mult), vecs)
                dve.wait_ge(consts, 11)
                me.did(dve.reciprocal(invn[:, :], invn[:, :]))

            def mod_rows(j, q):
                if j == 1:
                    dve.wait_ge(ada_in[q][j], 16)
                    slot = ada_first[q][j][:, :, :].rearrange("p k n -> p (k n)")
                else:
                    item = sch.items.index(("mod", j, q))
                    await_item(dve, item)
                    slot = stage[:, item % NSTAGE, :]
                for r in range(2):
                    k = 2 * q + r
                    rows_k = slot[:, r * D:(r + 1) * D]
                    if k == 0:
                        if j > 1:
                            dve.wait_ge(mod_col, j - 1)
                        me.did(dve.tensor_scalar(macc[:, :], rows_k, csil[:, 0:1], None, ALU.mult), mod_sum)
                    else:
                        dve.wait_ge(mod_sum, KD * (j - 1) + k)
                        me.did(dve.scalar_tensor_tensor(out=macc[:, :], in0=rows_k, scalar=csil[:, k:k + 1],
                                                        in1=macc[:, :], op0=ALU.mult, op1=ALU.add), mod_sum)

            def mod_vector(j):
                if j == 0:
                    dve.wait_ge(mod_turn, 1)
                    src = banks[2][:, 0:KD]
                else:
                    dve.wait_ge(mod_col, j)
                    src = (SC[0] if j == 2 else OB)[:, MC:MC + KD]
                me.did(dve.tensor_tensor(mod[:, j * KD:(j + 1) * KD], src,
                                         vec[:, V_ADA + j * KD:V_ADA + (j + 1) * KD], ALU.add), mod_ok)
                if j in (1, 4):
                    me.settle()
                    gain = vec[:, V_NORM1:V_NORM1 + KD] if j == 1 else vec[:, V_NORM2:V_NORM2 + KD]
                    me.did(dve.scalar_tensor_tensor(out=gs[:, j // 4, :], in0=mod[:, j * KD:(j + 1) * KD], scalar=1.0,
                                                    in1=gain, op0=ALU.add, op1=ALU.mult))

            def roots(which):
                me.did(dve.tensor_scalar(tstat[:, 1, :], tstat[:, 0, :], 1.0 / D, EPS, ALU.mult, ALU.add), mean_ok)
                dve.wait_ge(root_ok, which + 1)
                me.did(dve.reciprocal(tstat[:, 3, :], tstat[:, 2, :]))
                me.settle()
                for t in range(NT):
                    last = me.did(dve.tensor_scalar(diag[:, t, :], ident[:, :], tstat[:, 3, t:t + 1], None, ALU.mult),
                                  diag_ok)

            def norm(which, shift):
                dve.wait_ge(root_b, which + 1)
                me.settle()

                def low_part(k):
                    dve.wait_ge(h_hi, which * KD + k + 1)
                    me.did(dve.scalar_tensor_tensor(
                        out=hT[:, 1, k, :], in0=nrm[:, k % 2, :], scalar=mod[:, shift * KD + k:shift * KD + k + 1],
                        in1=hT[:, 0, k, :].bitcast(F32), op0=ALU.add, op1=ALU.subtract), h_lo)

                for k in range(KD):
                    if k >= 2:
                        dve.wait_ge(h_lo, which * KD + k - 1)
                    me.did(dve.scalar_tensor_tensor(out=nrm[:, k % 2, :], in0=xT[:, k, :], scalar=gs[:, which, k:k + 1],
                                                    in1=SC[0][:, :], op0=ALU.mult, op1=ALU.mult), n_ok)
                    if k:
                        low_part(k - 1)
                low_part(KD - 1)

            dve.wait_ge(c_silu, 1)
            for k in range(1, KD, 2):
                dve.wait_ge(x_t, k + 1)
                me.did(copy_of(xT[:, k, :], (SC + PT)[k % 4][:, :]), x_kept[1])
                if k == 3:
                    mod_rows(1, 0)
            dve.wait_ge(x_sum, NT)
            roots(0)
            vectors()
            for q in range(1, KD // 2):
                mod_rows(1, q)
            mod_vector(1)
            mod_vector(0)
            dve.wait_ge(x_kept[0], KD // 2)
            norm(0, 0)

            def low_of(out_ap, full, hi, signal):
                me.did(dve.tensor_tensor(out_ap, full, hi.bitcast(F32), ALU.subtract), signal)

            for m in range(2):
                dve.wait_ge(part_hi, m + 1)
                low_of(qiT[:, 1, m, :], bank(("qi", m))[:, :], qiT[:, 0, m, :], drained["dve"])
            dve.wait_ge(part_hi, 4)
            b = bank(("kw", 0))
            me.did(dve.tensor_tensor(kiT[HD:P, 1, :], b[0:HD, :], kiT[0:HD, 0, :].bitcast(F32), ALU.subtract))
            low_of(kiT[0:HD, 1, :], b[0:HD, :], kiT[0:HD, 0, :], drained["dve"])
            dve.wait_ge(wi_t, 1)
            me.did(dve.tensor_scalar(wi[:, :], OB[:, WC:WC + NT * IH], IH ** -0.5, None, ALU.mult), wi_ok)

            def row_of(tensor, i):
                return tensor[:, offset(i) - P:offset(i + 1) - P]

            def indexer(i):
                acc = row_of(iscore, i)
                for h in range(IH):
                    n = (i - 1) * IH + h
                    dve.wait_ge(i_relu, n + 1)
                    me.settle()
                    w = wi[:, i * IH + h:i * IH + h + 1]
                    r = relu[:, n % 2, 0:(i + 1) * P]
                    if h == 0:
                        me.did(dve.tensor_scalar(acc, r, w, None, ALU.mult), i_sum)
                    else:
                        me.did(dve.scalar_tensor_tensor(out=acc, in0=r, scalar=w, in1=acc, op0=ALU.mult, op1=ALU.add),
                               i_sum)
                me.settle()
                me.did(dve.tensor_tensor(acc[:, i * P:], acc[:, i * P:], cap[:, :], ALU.min))

            rounds = [0]

            def top_rounds(n):
                for _ in range(n):
                    src = work if rounds[0] else iscore
                    me.settle()
                    found = [me.did(dve.max(top8[:, i, :], row_of(src, i))) for i in range(1, NT)]
                    for i in range(1, NT):
                        me.settle(found[i - 1])
                        me.did(dve.match_replace(out=row_of(work, i), in_to_replace=top8[:, i, :],
                                                 in_values=row_of(src, i), imm_value=TAKEN))
                    rounds[0] += 1

            for m in range(KA):
                dve.wait_ge(part_hi, 4 + m + 1)
                me.did(dve.scalar_tensor_tensor(out=qT[:, 1, m, :], in0=bank(("q", m))[:, :], scalar=qgain[:, 0:1],
                                                in1=qT[:, 0, m, :].bitcast(F32), op0=ALU.mult, op1=ALU.subtract),
                       drained["dve"])
                for i in {0: (1, 2), 1: (3,)}.get(m, ()):
                    indexer(i)
                if m >= 2:
                    top_rounds(1)
            top_rounds(7)
            dve.wait_ge(sq_used, 2 * KA)
            me.did(dve.tensor_scalar(stat[:, 0, :], OB[:, 0:NT * 2 * H], 1.0 / HD, EPS, ALU.mult, ALU.add), qk_mean)

            def v_low(m):
                dve.wait_ge(v_hi, m + 1)
                low_of(vS[:, :, 2 * m:2 * m + 2, 1, :], PT[m % 2][:, :].rearrange("p (t h d) -> p t h d", t=NT, h=2),
                       vS[:, :, 2 * m:2 * m + 2, 0, :], v_lo)

            def mixed(g):
                dve.wait_ge(part_hi, 4 + KA + g + 1)
                me.did(dve.scalar_tensor_tensor(out=mix[:, 1, g, :], in0=bank(("mg", g))[:, :],
                                                scalar=vec[:, V_POOL + g:V_POOL + g + 1], in1=mix[:, 0, g, :].bitcast(F32),
                                                op0=ALU.mult, op1=ALU.subtract), drained["dve"])

            def pool_mean(g):
                window = WINDOWS[g]
                src, own = wsum[g % 2], u[g % 2]
                dve.wait_ge(w_ok, g + 1)
                if g:
                    dve.wait_ge(p_lo, g)
                me.did(dve.scalar_tensor_tensor(out=pmean[:, window - 1:], in0=src[:, PAD + window - 1:],
                                                scalar=1.0 / window, in1=own[:, PAD + window - 1:],
                                                op0=ALU.mult, op1=ALU.subtract))
                me.did(dve.tensor_tensor(pmean[:, 0:window - 1], src[:, PAD:PAD + window - 1], invn[:, 0:window - 1],
                                         ALU.mult))
                me.settle()
                me.did(dve.tensor_tensor(pmean[:, 0:window - 1], pmean[:, 0:window - 1], own[:, PAD:PAD + window - 1],
                                         ALU.subtract), p_ok)

            def k_normed(m):
                dve.wait_ge(kroot_t, m + 1)
                if m >= 2:
                    dve.wait_ge(k_lo, m - 1)
                me.did(dve.scalar_tensor_tensor(out=knorm[:, m % 2, :], in0=kraw[:, m, :], scalar=vec[:, V_K:V_K + 1],
                                                in1=SC[m % 2][:, :], op0=ALU.mult, op1=ALU.mult), kn_ok)

            top_rounds(1)
            dve.wait_ge(qk_root, 1)
            me.did(dve.reciprocal(stat[:, 2, :], stat[:, 1, :]), qk_inv)
            for h in range(H):
                me.did(dve.tensor_scalar(alibi[:, :].rearrange("p (t h) -> p h t", h=H)[:, h, :],
                                         stat[:, 1, :].rearrange("p (t h) -> p h t", h=2 * H)[:, h, :],
                                         -slope(h), None, ALU.mult))
            pool_mean(0)
            top_rounds(1)
            pool_mean(1)
            mixed(0)
            top_rounds(1)
            pool_mean(2)
            mixed(1)
            top_rounds(1)
            pool_mean(3)
            mixed(2)
            top_rounds(1)
            v_low(0)
            mixed(3)
            top_rounds(TOPK // 8 - rounds[0])
            me.settle()
            for i in range(1, NT):
                me.did(dve.tensor_scalar(dsel[:, offset(i):offset(i + 1)], row_of(work, i), TAKEN_BELOW, BIG,
                                         ALU.is_gt, ALU.mult))
            me.settle()
            for i in range(1, NT):
                me.did(dve.tensor_tensor(dsel[:, offset(i):offset(i + 1)], dsel[:, offset(i):offset(i + 1)],
                                         dist[:, (NT - 1 - i) * P:S], ALU.add), sel_ok)
            for m in range(1, KA):
                v_low(m)
                k_normed(m - 1)
            k_normed(KA - 1)

            for t in range(SLOTS):
                if t == MOD2_SLOT:
                    mod_vector(2)
                if t >= 7 and t % NT == 3:
                    h = t // NT - 1
                    dve.wait_ge(head_lo, h + 1)
                    r = (h % 2) * HD
                    me.did(dve.tensor_tensor(araw[r:r + HD, :], OB[0:HD, :], araw[r:r + HD, :], ALU.add), head_ok)
                if t < STEPS:
                    h, i = step_of(t)
                    n = (i + 1) * P
                    dve.wait_ge(linear, t + 1)
                    dve.wait_ge(score, t + 1)
                    me.did(dve.tensor_tensor_reduce(logit[:, t % 2, 0:n], logit[:, t % 2, 0:n], SC[t % 2][:, 0:n],
                                                    1.0, TAKEN, ALU.add, ALU.max, smax[:, t:t + 1]), logit_ok)
                    me.settle()
                    r = i * 2 * H + h
                    me.did(dve.tensor_scalar(sbias[:, t:t + 1], smax[:, t:t + 1], stat[:, 2, r:r + 1], -1.0,
                                             ALU.mult, ALU.mult), bias_ok)
                if 1 <= t < STEPS + 1:
                    n = (step_of(t - 1)[1] + 1) * P
                    dve.wait_ge(exp_ok, t)
                    me.did(dve.reciprocal(sinv[:, t - 1:t], ssum[:, t - 1:t]))
                    me.settle()
                    me.did(dve.tensor_scalar(prob[:, (t - 1) % 2, 0:n], prob[:, (t - 1) % 2, 0:n],
                                             sinv[:, t - 1:t], None, ALU.mult), prob_ok)
                if 2 <= t < STEPS + 2:
                    n = (step_of(t - 2)[1] + 1) * P
                    dve.wait_ge(pt_hi, t - 1)
                    low_of(pT[:, t % 2, 1, 0:n], PT[t % 2][:, 0:n], pT[:, t % 2, 0, 0:n], pt_lo)
                if t >= 12 and t % (2 * NT) == NT:
                    m = t // (2 * NT) - 1
                    dve.wait_ge(pair_hi, m + 1)
                    low_of(qT[:, 1, m, :], araw[:, :], qT[:, 0, m, :], pair_lo)
                if t and filler(t - 1) and filler(t - 1)[1] == "low" and filler(t - 1)[0][0] == "pb":
                    name = filler(t - 1)[0]
                    m = name[1]
                    await_chunk(dve, name)
                    dve.wait_ge(drained["act"], drained_count[sch.chunk["gp", m]][1])
                    me.did(dve.scalar_tensor_tensor(out=ypool[:, m, :], in0=ypool[:, m, :], scalar=1.0,
                                                    in1=bank(name)[:, :], op0=ALU.add, op1=ALU.mult),
                           drained["dve"])
                if t % 4 == 3 and t < STEPS:
                    n = t // 4
                    mod_rows(2 + n // 4, n % 4)
            mod_vector(3)

            def merged_low(m):
                dve.wait_ge(m_hi, m + 1)
                me.did(dve.scalar_tensor_tensor(out=merged[:, 1, m, :], in0=msum[:, m % 2, :], scalar=0.5,
                                                in1=merged[:, 0, m, :].bitcast(F32), op0=ALU.mult, op1=ALU.subtract),
                       m_lo)

            for m in range(KD):
                if m % 2 == 0:
                    mod_rows(4, m // 2)
                await_chunk(dve, ("ab", m))
                dve.wait_ge(drained["act"], drained_count[sch.chunk["ga", m]][1])
                if m >= 2:
                    dve.wait_ge(m_lo, m - 1)
                me.did(dve.scalar_tensor_tensor(out=msum[:, m % 2, :], in0=tga[:, m % 2, :], scalar=1.0,
                                                in1=bank(("ab", m))[:, :], op0=ALU.add, op1=ALU.mult), drained["dve"])
                me.settle()
                me.did(dve.tensor_tensor(msum[:, m % 2, :], msum[:, m % 2, :], ypool[:, m, :], ALU.add), m_ok)
                if m:
                    merged_low(m - 1)
            mod_vector(4)
            merged_low(KD - 1)

            for m in range(KD):
                if m % 2 == 0:
                    mod_rows(5, m // 2)
                await_chunk(dve, ("wo", m))
                me.did(dve.scalar_tensor_tensor(out=xT[:, m, :], in0=bank(("wo", m))[:, :],
                                                scalar=mod[:, 2 * KD + m:2 * KD + m + 1], in1=xT[:, m, :],
                                                op0=ALU.mult, op1=ALU.add), drained["dve"])
            dve.wait_ge(x2_sum, KD)
            me.did(dve.tensor_reduce(tstat[:, 0, :], OB[:, 0:KD * NT].rearrange("p (m t) -> p t m", t=NT), AX_X,
                                     ALU.add))
            me.settle()
            roots(1)
            norm(1, 3)
            mod_vector(5)

            def first_taps(kind, m, y):
                col = m if kind == "ua" else KF + m
                dve.wait_ge(y_tap, 2 * m + (1 if kind == "ua" else 2))
                for back in (1, 2):
                    if back == 2:
                        me.settle()
                    w = conv[:, (TAPS - 1 - back) * 2 * KF + col:(TAPS - 1 - back) * 2 * KF + col + 1]
                    me.did(dve.scalar_tensor_tensor(out=y[:, m % 2, back:], in0=bank((kind, m))[:, 0:S - back],
                                                    scalar=w, in1=y[:, m % 2, back:], op0=ALU.mult, op1=ALU.add),
                           drained["dve"] if back == 2 else None)

            def gu_low(m):
                dve.wait_ge(gu_hi, m + 1)
                low_of(guT[:, 1, m, :], ya[:, m % 2, :], guT[:, 0, m, :], gu_lo)

            for m in range(KF):
                first_taps("ua", m, ya)
                if m:
                    gu_low(m - 1)
                first_taps("ub", m, yb)
                dve.wait_ge(silu_ok, m + 1)
                me.settle()
                me.did(dve.tensor_tensor(ya[:, m % 2, :], ya[:, m % 2, :], yb[:, m % 2, :], ALU.mult), g_ok)
            gu_low(KF - 1)
            for m in range(KD):
                await_chunk(dve, ("dn", m))
                me.did(dve.scalar_tensor_tensor(out=xT[:, m, :], in0=bank(("dn", m))[:, :],
                                                scalar=mod[:, 5 * KD + m:5 * KD + m + 1], in1=xT[:, m, :],
                                                op0=ALU.mult, op1=ALU.add), drained["dve"])

        @block.tensor
        def _(pe):
            def high_products(n, out_bank, rhs, k0=0, first=True):
                hi = unit_split(n, 0)
                pe.wait_ge(high, n + 1)
                for k in range(sch.units[n][0]):
                    for part in range(2):
                        pe.matmul(out_bank[:, :], hi[:, k, :], rhs[:, part, k0 + k, :],
                                  start=first and k == 0 and part == 0, stop=False)

            def low_products(n, out_bank, rhs, k0=0, last=True):
                nk = sch.units[n][0]
                lo = unit_split(n, 1)
                pe.wait_ge(low, n + 1)
                for k in range(nk):
                    mm = pe.matmul(out_bank[:, :], lo[:, k, :], rhs[:, 0, k0 + k, :], start=False,
                                   stop=last and k == nk - 1)
                mm.then_inc(used, 1)

            def product(name, rhs):
                await_bank(pe, name)
                high_products(sch.unit[name], bank(name), rhs)
                low_products(sch.unit[name], bank(name), rhs)

            def first_products(names, which):
                for name in names:
                    await_bank(pe, name)
                    pe.wait_ge(high, sch.unit[name] + 1)
                    pe.wait_ge(low, sch.unit[name] + 1)
                for k in range(KD):
                    pe.wait_ge(h_hi, which * KD + k + 1)
                    for name in names:
                        for part in range(2):
                            pe.matmul(bank(name)[:, :], unit_split(sch.unit[name], part)[:, k, :], hT[:, 0, k, :],
                                      start=k == 0 and part == 0, stop=False)
                    pe.wait_ge(h_lo, which * KD + k + 1)
                    for name in names:
                        mm = pe.matmul(bank(name)[:, :], unit_split(sch.unit[name], 0)[:, k, :], hT[:, 1, k, :],
                                       start=False, stop=k == KD - 1)
                        if k == KD - 1:
                            mm.then_inc(used, 1)

            pe.wait_ge(consts, 11)
            pe.wait_ge(c_in, 16)
            pe.transpose(banks[2][:, 0:KD], crow[:, :], ident[0:KD, 0:KD]).then_inc(c_t, 1)
            pe.wait_ge(x_in, 16 * NT)
            for k in range(KD):
                if k >= 4:
                    pe.wait_ge(x_kept[k % 2], (k - 4) // 2 + 1)
                for t in range(NT):
                    mm = pe.transpose((SC + PT)[k % 4][:, t * P:(t + 1) * P], xn[:, t, k * P:(k + 1) * P],
                                      ident[:, :])
                mm.then_inc(x_t, 1)

            def spread_roots(which):
                pe.wait_ge(diag_ok, NT * (which + 1))
                for t in range(NT):
                    mm = pe.matmul(SC[0][:, t * P:(t + 1) * P], ones[:, :], diag[:, t, :], start=True, stop=True)
                mm.then_inc(root_b, 1)

            def mod_columns(j):
                pe.wait_ge(mod_sum, KD * j)
                if j == 1:
                    pe.wait_ge(vecs, 1)
                else:
                    pe.wait_ge(mod_ok, j)
                for k in range(KD):
                    mm = pe.matmul((SC[0] if j == 2 else OB)[:, MC + k:MC + k + 1], macc[:, k * P:(k + 1) * P], ones[:, 0:1],
                                   start=True, stop=True)
                mm.then_inc(mod_col, 1)

            pe.wait_ge(x_kept[0], KD // 2)
            pe.wait_ge(rows_in, 16 * ROW_LOADS)
            pe.transpose(OB[:, 0:V_END], rows[0:V_END, 0, :], ident[0:V_END, 0:V_END])
            pe.transpose(OB[:, P:2 * P], rows[:, 1, :], ident[:, :])
            left = (TAPS + 1) * 2 * KF - P
            pe.transpose(OB[:, 2 * P:2 * P + left], rows[0:left, 2, :], ident[0:left, 0:left]).then_inc(rows_t, 1)
            spread_roots(0)
            pe.wait_ge(c_silu, 1)
            for q in range(KD // 2):
                pe.wait_ge(ada_in[q][0], 16)
                for r in range(2):
                    k = 2 * q + r
                    for half in range(2):
                        mm = pe.matmul(banks[half][0:1, :], csil[:, k:k + 1],
                                       ada_first[q][0][:, r, half * S:(half + 1) * S],
                                       start=k == 0, stop=k == KD - 1)
            mm.then_inc(mod_first, 1)
            pe.wait_ge(mod_row, 2)
            for k in range(KD):
                mm = pe.matmul(banks[2][:, k:k + 1], mrow[:, k * P:(k + 1) * P], ones[0:1, 0:1], start=True, stop=True)
            mm.then_inc(mod_turn, 1)
            mod_columns(1)
            pe.wait_ge(mod_ok, 2)
            first_products((("qi", 0), ("qi", 1)), 0)
            product(("kw", 0), hT)
            pe.wait_ge(wi_row, 1)
            for t in range(NT):
                mm = pe.transpose(OB[:, WC + t * IH:WC + (t + 1) * IH], wiT[0:IH, t * P:(t + 1) * P],
                                  ident[0:IH, 0:IH])
            mm.then_inc(wi_t, 1)

            THREE = ((0, 0), (0, 1), (1, 0))

            def indexer(i):
                for h in range(IH):
                    n = (i - 1) * IH + h
                    if n == 0:
                        await_drained(pe, ("kw", 0))
                    if n >= 2:
                        pe.wait_ge(i_relu, n - 1)
                    r = slice((h % 2) * HD, (h % 2 + 1) * HD)
                    for a, b in THREE:
                        mm = pe.matmul(SC[n % 2][:, 0:(i + 1) * P], qiT[r, a, h // 2, i * P:(i + 1) * P],
                                       kiT[r, b, 0:(i + 1) * P], start=(a, b) == (0, 0), stop=a == 1)
                    mm.then_inc(i_dot, 1)

            def squares(n):
                pe.wait_ge(sq_ok, n + 1)
                if n == 0:
                    pe.wait_ge(wi_ok, 1)
                for t in range(NT):
                    mm = pe.matmul(OB[:, t * 2 * H + 2 * n:t * 2 * H + 2 * n + 2], sq[:, n % 2, t * P:(t + 1) * P],
                                   halves[:, :], start=True, stop=True)
                mm.then_inc(sq_used, 1)

            for n in range(2 * KA):
                product(("q", n) if n < KA else ("k", n - KA), hT)
                if n:
                    squares(n - 1)
                for i in {0: (1, 2), 1: (3,)}.get(n, ()):
                    indexer(i)

            def v_turn(m):
                pe.wait_ge(drained["act"], drained_count[sch.chunk["v", m]][1])
                if m >= 2:
                    pe.wait_ge(v_lo, m - 1)
                for t in range(NT):
                    mm = pe.transpose(PT[m % 2][:, t * P:(t + 1) * P], vraw[:, m % 2, t * P:(t + 1) * P], ident[:, :])
                mm.then_inc(v_t, 1)

            def k_turn(m):
                pe.wait_ge(kroot_ok, m + 1)
                if m >= 2:
                    pe.wait_ge(kn_ok, m - 1)
                for t in range(NT):
                    mm = pe.transpose(SC[m % 2][:, t * P:(t + 1) * P], kroot[:, m % 2, t * P:(t + 1) * P], ident[:, :])
                mm.then_inc(kroot_t, 1)

            def group(g):
                pe.wait_ge(p_lo, g + 1)
                product(("mg", g), pooled[:, :, :].rearrange("p a (k n) -> p a k n", k=1))

            product(("u", 0), hT)
            squares(2 * KA - 1)
            product(("u", 1), hT)
            product(("u", 2), hT)
            group(0)
            product(("u", 3), hT)
            group(1)
            product(("v", 0), hT)
            group(2)
            product(("v", 1), hT)
            v_turn(0)
            group(3)
            product(("v", 2), hT)
            v_turn(1)
            k_turn(0)
            product(("v", 3), hT)
            v_turn(2)
            k_turn(1)
            v_turn(3)
            k_turn(2)
            k_turn(3)

            for t in range(SLOTS):
                if t < STEPS:
                    h, i = step_of(t)
                    r = slice((h % 2) * HD, (h % 2 + 1) * HD)
                    if t % (2 * NT) == 0:
                        pe.wait_ge(k_lo, h // 2 + 1)
                    if t < 2:
                        pe.wait_ge(kn_ok, KA)
                    else:
                        pe.wait_ge(logit_ok, t - 1)
                    if t == MOD2_SLOT:
                        mod_columns(2)
                        pe.wait_ge(mod_ok, 3)
                    for a, b in THREE:
                        mm = pe.matmul(SC[t % 2][:, 0:(i + 1) * P], qT[r, a, h // 2, i * P:(i + 1) * P],
                                       kT[r, b, h // 2, 0:(i + 1) * P], start=(a, b) == (0, 0), stop=a == 1)
                    mm.then_inc(score, 1)
                if 2 <= t < STEPS + 2:
                    i = step_of(t - 2)[1]
                    pe.wait_ge(prob_ok, t - 1)
                    if t >= 4:
                        pe.wait_ge(pt_lo, t - 3)
                    for j in range(i + 1):
                        mm = pe.transpose(PT[t % 2][:, j * P:(j + 1) * P], prob[:, t % 2, j * P:(j + 1) * P],
                                          ident[:, :])
                    mm.then_inc(prob_t, 1)
                if filler(t):
                    name, part = filler(t)
                    if part == "high":
                        await_bank(pe, name)
                    (high_products if part == "high" else low_products)(
                        sch.unit[name], bank(name), mix if name[0] == "pb" else hT)
                if 3 <= t < STEPS + 3:
                    h, i = step_of(t - 3)
                    pe.wait_ge(pt_lo, t - 2)
                    if (t - 3) % NT == 0 and h:
                        pe.wait_ge(head_ok, h)
                    for j in range(i + 1):
                        for part in range(2):
                            mm = pe.matmul(OB[:, i * P:(i + 1) * P], vS[:, j, h, :, :],
                                           pT[:, (t - 1) % 2, part, j * P:(j + 1) * P],
                                           start=j == 0 and part == 0, stop=j == i and part == 1)
                    mm.then_inc(pv_ok, 1)
            pe.wait_ge(head_ok, H)
            mod_columns(3)
            for m in range(0, KD, 2):
                for n in (m, m + 1):
                    if m:
                        product(("ga", n), hT)
                if m == 0:
                    pe.wait_ge(pair_lo, NPAIR)
                for n in (m, m + 1):
                    product(("ab", n), qT)

            def token_squares(m):
                pe.wait_ge(x2_sq, m + 1)
                if m == 0:
                    pe.wait_ge(mod_ok, 5)
                for t in range(NT):
                    mm = pe.matmul(OB[:, m * NT + t:m * NT + t + 1], sq2[:, m % 2, t * P:(t + 1) * P], ones[:, 0:1],
                                   start=True, stop=True)
                mm.then_inc(x2_sum, 1)

            mod_columns(4)
            pe.wait_ge(m_lo, KD)
            for m in range(KD):
                product(("wo", m), merged)
                if m:
                    token_squares(m - 1)
            token_squares(KD - 1)
            spread_roots(1)

            for m in range(KF):
                if m == 0:
                    first_products((("ua", 0), ("ub", 0)), 1)
                else:
                    product(("ua", m), hT)
                    product(("ub", m), hT)
                if m == 0:
                    mod_columns(5)

            def out_turn(m):
                pe.wait_ge(drained["dve"], drained_count[sch.chunk["dn", m]][1])
                if m >= 2:
                    pe.wait_ge(out_ok, m - 1)
                for t in range(NT):
                    mm = pe.transpose(PT[m % 2][:, t * P:(t + 1) * P], xT[:, m, t * P:(t + 1) * P], ident[:, :])
                mm.then_inc(out_t, 1)

            for m in range(0, KD, 2):
                n = sch.unit["dn", m] - 4
                for k0 in range(0, KF, KD):
                    pe.wait_ge(gu_lo, min(k0 + KD, KF))
                    for half in range(2):
                        if k0 == 0:
                            await_bank(pe, ("dn", m + half))
                        high_products(n, bank(("dn", m + half)), guT, k0, k0 == 0)
                        low_products(n, bank(("dn", m + half)), guT, k0, k0 + KD >= KF)
                        n += 1
                    if m and k0 == 0:
                        out_turn(m - 2)
                        out_turn(m - 1)
            out_turn(KD - 2)
            out_turn(KD - 1)


_INS = ['x', 'c', 'w_ada', 'b_ada', 'norm1_g', 'w_in', 'q_norm_g', 'k_norm_g', 'w_attn_br', 'w_pool_grp', 'pool_scale',
        'w_pool_br', 'w_out', 'norm2_g', 'w_up', 'conv_w', 'conv_b', 'w_down']
_OUTS = [((1, 512, 1024), 'float32')]


def kernel(**inputs):
    import numpy as _np
    import concourse.bacc as _bacc
    from concourse import mybir as _mybir
    from concourse.bass_utils import run_bass_kernel_spmd as _run

    nc = _bacc.Bacc("TRN2", target_bir_lowering=False, num_devices=1)
    arrays, args = {}, []
    for name in _INS:
        a = _np.ascontiguousarray(inputs[name])
        arrays[f"in_{name}_dram"] = a
        args.append(nc.dram_tensor(f"in_{name}_dram", a.shape, _mybir.dt.from_np(a.dtype), kind="ExternalInput").ap())
    for i, (shape, dtype) in enumerate(_OUTS):
        dt = _mybir.dt.from_np(_np.dtype(dtype))
        args.append(nc.dram_tensor(f"out_{i}_dram", shape, dt, kind="ExternalOutput").ap())
    build_layer(nc, *args)
    r = _run(nc, [arrays], core_ids=[0])
    got = tuple(r.results[0][f"out_{i}_dram"] for i in range(len(_OUTS)))
    return got[0]
```

```python
from contextlib import ExitStack

import concourse.bass as bass
from concourse import mybir

F32 = mybir.dt.float32
F32R = mybir.dt.float32r
ALU = mybir.AluOpType
ACT = mybir.ActivationFunctionType
AX_X = mybir.AxisListType.X

P = 128
S, D, FF = 512, 1024, 2816
H, HD = 8, 64
IH = 4
TOPK = 128
TAPS = 3
EPS = 1e-6
NT = S // P
KD = D // P
KA = H * HD // P
KF = FF // P
NPAIR = H // 2
WINDOWS = (2, 4, 8, 16)
PAD = 16
WU = KD * P

C_Q, C_K, C_V, C_QI, C_KI = 0, 512, 1024, 1536, 1792
C_U = C_KI + HD + IH
C_GA, C_GP = C_U + 512, C_U + 512 + D

V_ADA, V_NORM1, V_NORM2, V_POOL, V_Q, V_K, V_END = 0, 48, 56, 64, 68, 69, 70

BIG = 1e32
FUTURE = -3.0e38
TAKEN = -3.4e38
TAKEN_BELOW = -3.2e38

NSTAGE = 3
NRING = 3
NBANK = 3


def slope(h):
    return 2.0 ** (-8.0 * (h + 1) / H)


def offset(i):
    return i * (i + 1) // 2 * P


NPAIRS = offset(NT)
STEPS = NT * H
SLOTS = STEPS + 4
ORDER = (0, 3, 1, 2)
FILLERS = tuple((kind, m + n) for kind, m in (("gp", 2), ("pb", 0), ("gp", 4), ("pb", 2), ("gp", 6), ("pb", 4),
                                              ("pb", 6), ("ga", 0), ("ga", 2)) for n in range(2))
MC, WC = 480, NT * 2 * H
ROW_LOADS = 11


def index_steps(n):
    return range(IH * (n - 1), IH * n) if n else ()


def step_of(t):
    return t // NT ^ 1, ORDER[t % NT]


def filler(t):
    return FILLERS[t // 2], "low" if t % 2 else "high"


SOURCES = {
    "qi": ("in", C_QI, KD, "dve", 2), "kw": ("in", C_KI, KD, "dve", 1), "q": ("in", C_Q, KD, "dve", 2),
    "u": ("in", C_U, KD, "act", 2), "v": ("in", C_V, KD, "act", 2), "k": ("in", C_K, KD, "act", 2),
    "gp": ("in", C_GP, KD, "act", 2), "ga": ("in", C_GA, KD, "act", 2), "pb": ("pb", 0, KA, "dve", 4),
    "ab": ("ab", 0, KA, "dve", 4), "wo": ("out", 0, KD, "dve", 2),
}


class Schedule:

    def __init__(self):
        self.items = []
        self.last_use = []
        self.open = {}
        self.units = []
        self.item_of = []
        self.unit = {}
        self.chunk = {}
        self.bank = []
        self.before = []
        self.drains = []
        self.mods = KD

    def mod(self, j, q):
        self.items.append(("mod", j, q))
        self.mods += 2
        self.last_use.append(("mod", self.mods))

    def stage(self, w, columns, k0, k1, chunks):
        self.items.append(("w", w, columns, k0, k1, chunks))
        self.last_use.append(None)
        return len(self.items) - 1

    def split(self, item, part, name=None):
        self.units.append((self.items[item][4] - self.items[item][3], part))
        self.item_of.append(item)
        self.last_use[item] = ("unit", len(self.units))
        if name is not None:
            self.unit[name] = len(self.units) - 1

    def opens(self, name, drain):
        n = len(self.chunk)
        banks = NBANK - 1 if name in FILLERS else NBANK
        b = (self.bank[-1] + 1) % banks if n else 0
        self.before.append(max((k for k in range(n) if self.bank[k] == b), default=None))
        self.bank.append(b)
        self.chunk[name] = n
        self.drains.append(drain)

    def product(self, kind, m):
        if kind == "mg":
            self.units.append((1, m))
            self.item_of.append(None)
            self.unit[kind, m] = len(self.units) - 1
            self.opens((kind, m), "dve")
            return
        w, c0, nk, drain, together = SOURCES[kind]
        if m % together == 0:
            self.open[kind] = self.stage(w, (c0 + m * P,), 0, nk, together)
        self.split(self.open[kind], m % together, (kind, m))
        self.opens((kind, m), drain)


def schedule():
    s = Schedule()
    for kind, n in (("qi", 2), ("kw", 1), ("q", KA), ("u", KA), ("v", KA)):
        for m in range(n):
            s.product(kind, m)
    for name in (("k", 0), ("mg", 0), ("k", 1), ("mg", 1), ("k", 2), ("mg", 2), ("k", 3), ("gp", 0), ("mg", 3),
                 ("gp", 1)):
        s.product(*name)
    for n, name in enumerate(FILLERS):
        s.product(*name)
        if n % 4 == 3:
            s.mod(2, n // 4)
    for m in range(0, KD, 2):
        s.product("ab", m)
        s.product("ab", m + 1)
        if m + 4 < KD:
            s.product("ga", m + 4)
            s.product("ga", m + 5)
    for m in range(KD):
        s.product("wo", m)
    for m in range(KF):
        item = s.stage("up", (m * P, FF + m * P), 0, KD, 1)
        for part, kind in enumerate(("ua", "ub")):
            s.split(item, part, (kind, m))
            s.opens((kind, m), "dve")
    for m in range(0, KD, 2):
        for k0 in range(0, KF, KD):
            k1 = min(k0 + KD, KF)
            item = s.stage("down", (m * P,), k0, k1, 2)
            for part in range(2):
                s.split(item, part, ("dn", m + part) if k1 == KF else None)
        for part in range(2):
            s.opens(("dn", m + part), "dve")
    return s


def build_layer(nc, x, c, w_ada, b_ada, norm1_g, w_in, q_norm_g, k_norm_g, w_attn_br, w_pool_grp, pool_scale,
                w_pool_br, w_out, norm2_g, w_up, conv_w, conv_b, w_down, out):
    sch = schedule()
    drained_count = []
    so_far = {"act": 0, "dve": 0}
    for who in sch.drains:
        so_far[who] += 1
        drained_count.append((who, so_far[who]))

    ada = w_ada[0].rearrange("(k p) n -> p k n", p=P)
    weights = {
        "in": w_in[0].rearrange("(k p) n -> p k n", p=P),
        "ab": w_attn_br[0].rearrange("(k p) n -> p k n", p=P),
        "pb": w_pool_br[0].rearrange("(k p) n -> p k n", p=P),
        "out": w_out[0].rearrange("(k p) n -> p k n", p=P),
        "up": w_up[0].rearrange("(k p) n -> p k n", p=P),
        "down": w_down[0].rearrange("(k p) n -> p k n", p=P),
    }
    out_v = out[0].rearrange("(t p) f -> p t f", p=P)

    with ExitStack() as ctx:
        at = [nc.sbuf_base + (-nc.sbuf_base) % 32]

        def place(name, shape, dt, where=None):
            size = 4
            for n in shape[1:]:
                size *= n
            if where is None:
                where = at[0]
                at[0] += size + (-size) % 32
            return nc.alloc_sbuf_tensor_at(name, shape, dt, offset=where)

        xT = place("xT", [P, KD, S], F32)
        wsplit = place("wsplit", [P, NRING, 2, WU], F32R)
        stage = place("stage", [P, NSTAGE, 2 * WU], F32)
        ident = place("ident", [P, P], F32)
        ones = place("ones", [P, P], F32)
        halves = place("halves", [P, 2], F32)
        vec = place("vec", [P, V_END], F32)
        conv = place("conv", [P, (TAPS + 1) * 2 * KF], F32)
        csil = place("csil", [P, KD], F32)
        qgain = place("qgain", [P, 1], F32)
        mod = place("mod", [P, 6 * KD], F32)
        gs = place("gs", [P, 2, KD], F32)
        invn = place("invn", [P, PAD], F32)
        stat = place("stat", [P, 3, NT * 2 * H], F32)
        tstat = place("tstat", [P, 4, NT], F32)
        alibi = place("alibi", [P, NT * H], F32)
        wi = place("wi", [P, NT * IH], F32)
        top8 = place("top8", [P, NT, 8], F32)
        smax = place("smax", [P, STEPS], F32)
        sbias = place("sbias", [P, STEPS], F32)
        ssum = place("ssum", [P, STEPS], F32)
        sinv = place("sinv", [P, STEPS], F32)

        hT_at = at[0]
        hT = place("hT", [P, 2, KD, S], F32R)
        K1 = 1024
        base = at[0]
        assert base + 107 * K1 <= nc.sbuf_usable_end, (base, nc.sbuf_usable_end)

        def arena(name, shape, dt, kb):
            return place(name, shape, dt, base + int(kb * K1))

        xn = arena("xn", [P, NT, D], F32, 0)
        rows = arena("rows", [P, 3, P], F32, 20)
        crow = arena("crow", [KD, P], F32, 22)
        mrow = arena("mrow", [1, D], F32, 32)
        junk = arena("junk", [P, 2, D], F32, 24)
        ada_first = [[place(f"ada{q}_{j}", [P, 2, D], F32,
                            hT_at + n * 8 * K1 if n < 4 else base + (36, 44, 52, 64)[n - 4] * K1)
                      for j, n in enumerate((2 * q, 2 * q + 1))] for q in range(KD // 2)]
        qT = arena("qT", [P, 2, KA, S], F32R, 0)
        kT = arena("kT", [P, 2, KA, S], F32R, 16)
        vS = arena("vS", [P, NT, 2, H, HD], F32R, 32)
        kraw = arena("kraw", [P, KA, S], F32, 24)
        sq = arena("sq", [P, 2, S], F32, 84)
        dist = arena("dist", [P, S], F32, 78)
        wgrp = arena("wgrp", [P, KA, P], F32, 62)
        qiT = arena("qiT", [P, 2, 2, S], F32R, 64)
        kiT = arena("kiT", [P, 2, S], F32R, 72)
        vraw = arena("vraw", [P, 2, S], F32, 93)
        wiT = arena("wiT", [P, S], F32, 97)
        cap = arena("cap", [P, P], F32, 60)
        dsel = arena("dsel", [P, NPAIRS], F32, 88)
        iscore = arena("iscore", [P, NPAIRS - P], F32, 93)
        work = arena("work", [P, NPAIRS - P], F32, 97.5)
        relu = arena("relu", [P, 2, S], F32, 102)
        kroot = arena("kroot", [P, KA, S], F32, 16)
        u = [arena(f"u{n}", [P, PAD + S], F32, 64 + 2.0625 * n) for n in range(2)]
        wsum = [arena(f"wsum{n}", [P, PAD + S], F32, 68.125 + 2.0625 * n) for n in range(2)]
        pmean = [arena(f"pmean{n}", [P, S], F32, 72.25 + 2 * n) for n in range(2)]
        pooled = [arena(f"pooled{n}", [P, 2, S], F32R, (103, 80)[n]) for n in range(2)]
        mix = arena("mix", [P, 2, KA, S], F32R, 48)
        ypool = arena("ypool", [P, KD, S], F32, 64)
        pT = arena("pT", [P, 2, 2, S], F32R, 80)
        logit = arena("logit", [P, 2, S], F32, 93)
        prob = arena("prob", [P, 2, S], F32, 97)
        macc = arena("macc", [P, D], F32, 103)
        nrm = arena("nrm", [P, 2, S], F32, 97)
        diag = arena("diag", [P, NT, P], F32, 101)
        merged = arena("merged", [P, 2, KD, S], F32R, 16)
        tga = arena("tga", [P, 4, S], F32, 48)
        msum = arena("msum", [P, 2, S], F32, 84)
        sq2 = arena("sq2", [P, 2, S], F32, 80)
        sqsum = arena("sqsum", [P, S], F32, 84)
        ada_mid = [arena(f"ada_mid{n}", [P, 2, D], F32, (88, 56)[n]) for n in range(2)]
        ada_last = [arena(f"ada_last{q}", [P, 2, D], F32, (20, 28, 36, 72)[q]) for q in range(KD // 2)]
        guT = arena("guT", [P, 2, KF, S], F32R, 0)
        ya = arena("ya", [P, 2, S], F32, 88)
        yb = arena("yb", [P, 2, S], F32, 92)
        ost = arena("ost", [P, 2, NT, P], F32, 96)

        banks = [ctx.enter_context(nc.psum_tensor(f"bank{n}", [P, S], F32)) for n in range(8)]
        SC, PT, OB = banks[3:5], banks[5:7], banks[7]
        HEADS = (OB, banks[2])

        def sem(name):
            return ctx.enter_context(nc.semaphore(name))

        rows_in = sem("rows_in")
        x_in = sem("x_in")
        wgrp_in = sem("wgrp_in")
        ada_mid_in = [sem(f"ada_mid_in{n}") for n in range(2)]
        ada_last_in = [sem(f"ada_last_in{q}") for q in range(KD // 2)]
        ada_in = [[sem(f"ada_in{q}_{j}") for j in range(2)] for q in range(KD // 2)]
        ada_end_in = sem("ada_end_in")
        stage_in = [sem(f"stage_in{n}") for n in range(NSTAGE)]
        stored = [sem(f"stored{n}") for n in range(2)]
        consts = sem("consts")
        vecs = sem("vecs")
        high = sem("high")
        low = sem("low")
        used = sem("used")
        drained = {"act": sem("drained_act"), "dve": sem("drained_dve")}
        act_step = sem("act_step")
        dve_step = sem("dve_step")
        rows_t = sem("rows_t")
        c_in = sem("c_in")
        c_t = sem("c_t")
        c_silu = sem("c_silu")
        x_sum = sem("x_sum")
        x_t = sem("x_t")
        x_kept = [sem("x_kept_even"), sem("x_kept_odd")]
        mean_ok = sem("mean_ok")
        root_ok = sem("root_ok")
        diag_ok = sem("diag_ok")
        root_b = sem("root_b")
        mod_sum = sem("mod_sum")
        mod_term = sem("mod_term")
        mod_first = sem("mod_first")
        mod_row = sem("mod_row")
        mod_turn = sem("mod_turn")
        mod_col = sem("mod_col")
        mod_ok = sem("mod_ok")
        n_ok = sem("n_ok")
        h_hi = sem("h_hi")
        h_lo = sem("h_lo")
        sq_ok = sem("sq_ok")
        sq_used = sem("sq_used")
        qk_mean = sem("qk_mean")
        qk_root = sem("qk_root")
        qk_inv = sem("qk_inv")
        kroot_ok = sem("kroot_ok")
        kroot_t = sem("kroot_t")
        kn_ok = sem("kn_ok")
        k_hi = sem("k_hi")
        k_lo = sem("k_lo")
        part_hi = sem("part_hi")
        wi_t = sem("wi_t")
        wi_row = sem("wi_row")
        wi_ok = sem("wi_ok")
        i_dot = sem("i_dot")
        i_relu = sem("i_relu")
        i_sum = sem("i_sum")
        sel_ok = sem("sel_ok")
        v_t = sem("v_t")
        v_hi = sem("v_hi")
        v_lo = sem("v_lo")
        w_step = sem("w_step")
        w_ok = sem("w_ok")
        pad_ok = sem("pad_ok")
        p_ok = sem("p_ok")
        p_hi = sem("p_hi")
        p_lo = sem("p_lo")
        linear = sem("linear")
        score = sem("score")
        logit_ok = sem("logit_ok")
        bias_ok = sem("bias_ok")
        exp_ok = sem("exp_ok")
        prob_ok = sem("prob_ok")
        prob_t = sem("prob_t")
        pt_hi = sem("pt_hi")
        pt_lo = sem("pt_lo")
        pv_ok = sem("pv_ok")
        pair_hi = sem("pair_hi")
        pair_lo = sem("pair_lo")
        m_ok = sem("m_ok")
        m_hi = sem("m_hi")
        m_lo = sem("m_lo")
        x2_sq = sem("x2_sq")
        x2_add = sem("x2_add")
        x2_sum = sem("x2_sum")
        y_tap = sem("y_tap")
        silu_ok = sem("silu_ok")
        g_ok = sem("g_ok")
        gu_hi = sem("gu_hi")
        gu_lo = sem("gu_lo")
        out_t = sem("out_t")
        out_ok = sem("out_ok")

        class Progress:

            def __init__(self, eng, step):
                self.eng, self.step, self.n, self.last = eng, step, {}, None

            def did(self, ins, signal=None):
                signal = self.step if signal is None else signal
                self.n[id(signal)] = self.n.get(id(signal), 0) + 1
                ins.then_inc(signal, 1)
                self.last = (signal, self.n[id(signal)])
                return self.last

            def settle(self, mark=None):
                signal, n = mark or self.last
                self.eng.wait_ge(signal, n)

        def bank(name):
            return banks[sch.bank[sch.chunk[name]]]

        def await_chunk(eng, name):
            eng.wait_ge(used, sch.unit[name] + 1)

        def await_drained(eng, name):
            who, n = drained_count[sch.chunk[name]]
            eng.wait_ge(drained[who], n)

        def await_bank(eng, name):
            before = sch.before[sch.chunk[name]]
            if before is not None:
                who, n = drained_count[before]
                eng.wait_ge(drained[who], n)

        landed = []
        slot_total = [0] * NSTAGE
        for n, item in enumerate(sch.items):
            slot_total[n % NSTAGE] += 16 * (len(item[2]) if item[0] == "w" else 1)
            landed.append(slot_total[n % NSTAGE])

        def await_item(eng, n):
            eng.wait_ge(stage_in[n % NSTAGE], landed[n])

        def unit_source(n):
            nk, part = sch.units[n]
            item = sch.item_of[n]
            if item is None:
                return wgrp[:, part:part + 1, :]
            slot = stage[:, item % NSTAGE, :]
            if len(sch.items[item][2]) == 2:
                return slot[:, part * WU:part * WU + nk * P].rearrange("p (k n) -> p k n", n=P)
            wide = sch.items[item][5] * P
            return slot[:, 0:nk * wide].rearrange("p (k n) -> p k n", n=wide)[:, :, part * P:(part + 1) * P]

        def unit_split(n, part):
            nk = sch.units[n][0]
            return wsplit[:, n % NRING, part, 0:nk * P].rearrange("p (k n) -> p k n", n=P)

        block = ctx.enter_context(nc.Block())

        @block.sync
        def _(sp):
            def load_item(n):
                item = sch.items[n]
                if n >= NSTAGE:
                    kind, count = sch.last_use[n - NSTAGE]
                    sp.wait_ge({"mod": mod_sum, "unit": low}[kind], count)
                slot = stage[:, n % NSTAGE, :]
                if item[0] == "mod":
                    _, j, q = item
                    sp.dma_start(slot.rearrange("p (k n) -> p k n", k=2), ada[:, 2 * q:2 * q + 2, j * D:(j + 1) * D]
                                 ).then_inc(stage_in[n % NSTAGE], 16)
                    return
                _, w, columns, k0, k1, chunks = item
                if len(columns) == 2:
                    for part, c0 in enumerate(columns):
                        sp.dma_start(slot[:, part * WU:(part + 1) * WU].rearrange("p (k n) -> p k n", n=P),
                                     weights[w][:, k0:k1, c0:c0 + P]).then_inc(stage_in[n % NSTAGE], 16)
                    return
                c0, = columns
                wide = chunks * P
                sp.dma_start(slot[:, 0:(k1 - k0) * wide].rearrange("p (k n) -> p k n", n=wide),
                             weights[w][:, k0:k1, c0:c0 + wide]).then_inc(stage_in[n % NSTAGE], 16)

            def load_first(q, j):
                if (q, j) == (KD // 2 - 1, 1):
                    for r, landed_in in enumerate((ada_in[q][j], ada_end_in)):
                        sp.dma_start(ada_first[q][j][:, r, :], ada[:, 2 * q + r, j * D:(j + 1) * D]
                                     ).then_inc(landed_in, 16)
                    return
                sp.dma_start(ada_first[q][j][:, :, :], ada[:, 2 * q:2 * q + 2, j * D:(j + 1) * D]
                             ).then_inc(ada_in[q][j], 16)

            def load_last(q):
                sp.dma_start(ada_last[q][:, :, :], ada[:, 2 * q:2 * q + 2, 5 * D:6 * D]
                             ).then_inc(ada_last_in[q], 16)

            sp.dma_start(crow[:, :], c[0].rearrange("(k p) -> k p", p=P)).then_inc(c_in, 16)
            for t in range(NT):
                sp.dma_start(xn[:, t, :], x[0, t * P:(t + 1) * P, :]).then_inc(x_in, 16)
            load_first(0, 0)
            for r, src in ((V_ADA, b_ada), (V_NORM1, norm1_g), (V_NORM2, norm2_g), (V_POOL, pool_scale)):
                v = src[0].rearrange("(k p) -> k p", p=P)
                sp.dma_start(rows[r:r + v.shape[0], 0, :], v).then_inc(rows_in, 16)
            load_first(0, 1)
            for r, src in ((V_Q, q_norm_g), (V_K, k_norm_g)):
                for half in range(2):
                    sp.dma_start(rows[r:r + 1, 0, half * HD:(half + 1) * HD], src).then_inc(rows_in, 16)
            load_first(1, 0)
            taps = conv_w[0].rearrange("j (m p) -> (j m) p", p=P)
            sp.dma_start(rows[:, 1, :], taps[0:P, :]).then_inc(rows_in, 16)
            sp.dma_start(rows[0:TAPS * 2 * KF - P, 2, :], taps[P:TAPS * 2 * KF, :]).then_inc(rows_in, 16)
            sp.dma_start(rows[TAPS * 2 * KF - P:(TAPS + 1) * 2 * KF - P, 2, :],
                         conv_b[0].rearrange("(m p) -> m p", p=P)).then_inc(rows_in, 16)
            sp.dma_start(wgrp[:, :, :], w_pool_grp[0].rearrange("g c d -> c g d")).then_inc(wgrp_in, 16)
            for q in range(1, KD // 2):
                for j in range(2):
                    if (q, j) != (1, 0):
                        load_first(q, j)
            for n, item in enumerate(sch.items):
                if item[:3] == ("w", "up", (3 * P, FF + 3 * P)):
                    sp.wait_ge(used, sch.unit["wo", KD - 1] + 1)
                    for q in range(KD // 2):
                        load_last(q)
                load_item(n)
            for m in range(KD):
                sp.wait_ge(out_ok, m + 1)
                sp.dma_start(out_v[:, :, m * P:(m + 1) * P], ost[:, m % 2, :, :]).then_inc(stored[m % 2], 16)
            for n in range(2):
                sp.wait_ge(stored[n], 16 * (KD // 2))

        @block.gpsimd
        def _(pool):
            pool.memset(ident[:, :], 0.0).then_inc(consts, 1)
            pool.memset(cap[:, :], -TAKEN_BELOW).then_inc(consts, 1)
            pool.memset(halves[:, :], 1.0).then_inc(consts, 1)
            pool.memset(ones[:, :], 1.0).then_inc(consts, 1)
            pool.iota(dist[:, :], [[-1, S]], base=(NT - 1) * P, channel_multiplier=1,
                      allow_small_or_imprecise_dtypes=True).then_inc(consts, 1)
            pool.iota(invn[:, :], [[1, PAD]], base=1, channel_multiplier=0,
                      allow_small_or_imprecise_dtypes=True).then_inc(consts, 1)
            pool.wait_ge(consts, 6)
            pool.affine_select(out=ident[:, :], in_=ident[:, :], compare_op=ALU.not_equal, fill=1.0, base=0,
                               pattern=[[-1, P]], channel_multiplier=1).then_inc(consts, 1)
            pool.affine_select(out=cap[:, :], in_=cap[:, :], compare_op=ALU.is_ge, fill=FUTURE, base=0,
                               pattern=[[-1, P]], channel_multiplier=1).then_inc(consts, 1)
            pool.affine_select(out=halves[:, 0:1], in_=halves[:, 0:1], compare_op=ALU.is_gt, fill=0.0, base=HD,
                               pattern=[[0, 1]], channel_multiplier=-1).then_inc(consts, 1)
            pool.affine_select(out=halves[:, 1:2], in_=halves[:, 1:2], compare_op=ALU.is_ge, fill=0.0, base=-HD,
                               pattern=[[0, 1]], channel_multiplier=1).then_inc(consts, 1)
            pool.affine_select(out=dsel[:, 0:P], in_=dist[:, (NT - 1) * P:S], compare_op=ALU.is_ge, fill=BIG, base=0,
                               pattern=[[-1, P]], channel_multiplier=1).then_inc(consts, 1)
            summed = [0]

            def low_parts(upto):
                while summed[0] < upto:
                    n = summed[0]
                    pool.wait_ge(high, n + 1)
                    if n >= NRING:
                        pool.wait_ge(used, n - NRING + 1)
                    pool.tensor_tensor(unit_split(n, 1), unit_source(n), unit_split(n, 0).bitcast(F32),
                                       ALU.subtract).then_inc(low, 1)
                    summed[0] += 1

            adds = [0]

            def window_sums(g):
                pool.wait_ge(drained["act"], drained_count[sch.chunk["u", g]][1])
                if g:
                    pool.wait_ge(p_ok, g)
                if g < 2:
                    pool.memset(u[g][:, 0:PAD], 0.0).then_inc(pad_ok, 1)
                    pool.wait_ge(pad_ok, g + 1)
                src, have = u[g % 2], 1
                while have < WINDOWS[g]:
                    if have > 1:
                        pool.wait_ge(w_step, adds[0])
                    dst = wsum[0] if src is not wsum[0] else wsum[1]
                    last = 2 * have == WINDOWS[g]
                    ins = pool.tensor_tensor(dst[:, 2 * have - 1:], src[:, 2 * have - 1:],
                                             src[:, have - 1:PAD + S - have], ALU.add)
                    if last:
                        ins.then_inc(w_ok, 1)
                    else:
                        ins.then_inc(w_step, 1)
                        adds[0] += 1
                    src, have = dst, 2 * have

            def pooled_low(g):
                pool.wait_ge(p_hi, g + 1)
                pool.tensor_tensor(pooled[g % 2][:, 1, :], pmean[g % 2][:, :], pooled[g % 2][:, 0, :].bitcast(F32),
                                   ALU.subtract).then_inc(p_lo, 1)

            def k_low(m):
                pool.wait_ge(k_hi, m + 1)
                pool.tensor_tensor(kT[:, 1, m, :], kraw[:, m, :], kT[:, 0, m, :].bitcast(F32),
                                   ALU.subtract).then_inc(k_lo, 1)

            def through(name):
                low_parts(sch.unit[name] + 1)

            def mod_rows(j, q):
                item = sch.items.index(("mod", j, q))
                await_item(pool, item)
                if q == 0:
                    pool.wait_ge(used, sch.unit["mg", KA - 2] + 1)
                    pool.wait_ge(mod_col, j - 1)
                for r in range(2):
                    k = 2 * q + r
                    row = stage[:, item % NSTAGE, r * D:(r + 1) * D]
                    c_k = csil[:, k:k + 1].to_broadcast([P, D])
                    pool.wait_ge(mod_sum, KD * (j - 1) + k)
                    if k == 0:
                        pool.tensor_tensor(macc[:, :], row, c_k, ALU.mult).then_inc(mod_sum, 1)
                    else:
                        pool.tensor_tensor(row, row, c_k, ALU.mult).then_inc(mod_term, 1)
                        pool.wait_ge(mod_term, k)
                        pool.tensor_tensor(macc[:, :], macc[:, :], row, ALU.add).then_inc(mod_sum, 1)

            through(("u", 3))
            window_sums(0)
            through(("v", 0))
            window_sums(1)
            pooled_low(0)
            through(("v", 1))
            window_sums(2)
            through(("v", 2))
            pooled_low(1)
            window_sums(3)
            through(("mg", 1))
            through(("k", 2))
            pooled_low(2)
            through(("k", 3))
            pooled_low(3)
            through(("gp", 1))
            k_low(0)
            k_low(1)
            through(("gp", 2))
            k_low(2)
            k_low(3)
            for n, name in enumerate(FILLERS):
                through(name)
                if n % 4 == 3:
                    mod_rows(2, n // 4)
            for m in range(1, KD - 1):
                low_parts(min(sch.unit["wo", m] + 3, sch.unit["wo", KD - 1] + 1))
                pool.wait_ge(x2_sq, m + 1)
                if m > 1:
                    pool.wait_ge(x2_add, m - 1)
                pool.tensor_tensor(sqsum[:, :], sqsum[:, :], sq2[:, m % 2, :], ALU.add).then_inc(x2_add, 1)
            low_parts(len(sch.units))

        @block.scalar
        def _(act):
            me = Progress(act, act_step)
            made = [0]

            def high_parts(upto):
                while made[0] < min(upto, len(sch.units)):
                    n = made[0]
                    if sch.item_of[n] is None:
                        act.wait_ge(wgrp_in, 16)
                    else:
                        await_item(act, sch.item_of[n])
                    if n >= NRING:
                        act.wait_ge(used, n - NRING + 1)
                        act.wait_ge(low, n - NRING + 1)
                    me.did(act.activation(unit_split(n, 0), unit_source(n), ACT.Copy), high)
                    made[0] += 1

            def chunk(name):
                await_chunk(act, name)
                high_parts(sch.unit[name] + 1 + NRING)

            def store_copy(m):
                act.wait_ge(out_t, m + 1)
                if m >= 2:
                    act.wait_ge(stored[m % 2], 16 * (m // 2))
                me.did(act.activation(ost[:, m % 2, :, :], PT[m % 2][:, :].rearrange("p (t f) -> p t f", t=NT),
                                      ACT.Copy), out_ok)

            act.wait_ge(c_t, 1)
            me.did(act.activation(csil[:, :], banks[2][:, 0:KD], ACT.Silu), c_silu)
            act.wait_ge(x_in, 16 * NT)
            for t in range(NT):
                if t >= 2:
                    act.wait_ge(x_sum, t - 1)
                me.did(act.activation(junk[:, t % 2, :], xn[:, t, :], ACT.Square,
                                      accum_out=tstat[:, 0, t:t + 1]), x_sum)
            for k in range(KD):
                if k % 2 == 0:
                    act.wait_ge(x_t, k + 1)
                    me.did(act.activation(xT[:, k, :], (SC + PT)[k % 4][:, :], ACT.Copy), x_kept[0])
            act.wait_ge(mean_ok, 1)
            me.did(act.activation(tstat[:, 2, :], tstat[:, 1, :], ACT.Sqrt), root_ok)
            for half in range(2):
                act.wait_ge(mod_first, 1)
                me.did(act.activation(mrow[:, half * S:(half + 1) * S], banks[half][0:1, :], ACT.Copy), mod_row)
            high_parts(NRING)

            def h_high(which, shift):
                act.wait_ge(mod_ok, shift + (2 if shift == 0 else 1))
                for k in range(KD):
                    act.wait_ge(n_ok, which * KD + k + 1)
                    me.did(act.activation(hT[:, 0, k, :], nrm[:, k % 2, :], ACT.Identity,
                                          bias=mod[:, shift * KD + k:shift * KD + k + 1]), h_hi)

            h_high(0, 0)
            for m in range(2):
                chunk(("qi", m))
                me.did(act.activation(qiT[:, 0, m, :], bank(("qi", m))[:, :], ACT.Copy), part_hi)
            chunk(("kw", 0))
            b = bank(("kw", 0))
            me.did(act.activation(wiT[0:IH, :], b[HD:HD + IH, :], ACT.Copy), wi_row)
            me.did(act.activation(kiT[0:HD, 0, :], b[0:HD, :], ACT.Copy), part_hi)
            me.did(act.activation(kiT[HD:P, 0, :], b[0:HD, :], ACT.Copy), part_hi)

            def index_relu(n):
                i = n // IH + 1
                act.wait_ge(i_dot, n + 1)
                if n >= 2:
                    act.wait_ge(i_sum, n - 1)
                me.did(act.activation(relu[:, n % 2, 0:(i + 1) * P], SC[n % 2][:, 0:(i + 1) * P], ACT.Relu,
                                      scale=HD ** -0.5), i_relu)

            def squared(n, name):
                if n >= 2:
                    act.wait_ge(sq_used, n - 1)
                me.did(act.activation(sq[:, n % 2, :], bank(name)[:, :], ACT.Square), sq_ok)

            for m in range(KA):
                for k in index_steps(m)[:3]:
                    index_relu(k)
                chunk(("q", m))
                squared(m, ("q", m))
                me.did(act.activation(qT[:, 0, m, :], bank(("q", m))[:, :], ACT.Copy, scale=qgain[:, 0:1]), part_hi)
                for k in index_steps(m)[3:]:
                    index_relu(k)

            def v_high(m):
                act.wait_ge(v_t, m + 1)
                me.did(act.activation(vS[:, :, 0, 2 * m:2 * m + 2, :],
                                      PT[m % 2][:, :].rearrange("p (t h d) -> p t h d", t=NT, h=2), ACT.Copy), v_hi)

            def v_raw(m):
                chunk(("v", m))
                if m >= 2:
                    act.wait_ge(v_t, m - 1)
                me.did(act.activation(vraw[:, m % 2, :], bank(("v", m))[:, :], ACT.Copy), drained["act"])

            def mixed(g):
                name = ("mg", g)
                chunk(name)
                me.did(act.activation(mix[:, 0, g, :], bank(name)[:, :], ACT.Copy,
                                      scale=vec[:, V_POOL + g:V_POOL + g + 1]), part_hi)

            def k_spread(m):
                src = stat[:, 2, :].rearrange("p (t h) -> p t h", h=2 * H)[:, :, H + 2 * m:H + 2 * m + 2]
                if m == 0:
                    act.wait_ge(qk_inv, 1)
                me.did(act.activation(kroot[:, m, :].rearrange("p (t h d) -> p t h d", t=NT, h=2),
                                      src.unsqueeze(3).to_broadcast([P, NT, 2, HD]), ACT.Copy), kroot_ok)

            def k_high(m):
                act.wait_ge(kn_ok, m + 1)
                me.did(act.activation(kT[:, 0, m, :], kraw[:, m, :], ACT.Copy), k_hi)

            def u_raw(g):
                chunk(("u", g))
                if g >= 2:
                    act.wait_ge(p_ok, g - 1)
                me.did(act.activation(u[g % 2][:, PAD:PAD + S], bank(("u", g))[:, :], ACT.Copy), drained["act"])

            def pooled_high(g):
                act.wait_ge(p_ok, g + 1)
                if g >= 2:
                    act.wait_ge(used, sch.unit["mg", g - 2] + 1)
                me.did(act.activation(pooled[g % 2][:, 0, :], pmean[g % 2][:, :], ACT.Copy), p_hi)

            def k_raw(m):
                chunk(("k", m))
                squared(KA + m, ("k", m))
                me.did(act.activation(kraw[:, m, :], bank(("k", m))[:, :], ACT.Copy), drained["act"])

            def pool_gate(m):
                chunk(("gp", m))
                me.did(act.activation(ypool[:, m, :], bank(("gp", m))[:, :], ACT.Tanh, scale=0.5), drained["act"])

            u_raw(0)
            u_raw(1)
            pooled_high(0)
            u_raw(2)
            u_raw(3)
            pooled_high(1)
            v_raw(0)
            v_raw(1)
            v_high(0)
            v_raw(2)
            v_high(1)
            v_raw(3)
            v_high(2)
            k_raw(0)
            v_high(3)
            mixed(0)
            pooled_high(2)
            k_raw(1)
            mixed(1)
            pooled_high(3)
            k_raw(2)
            mixed(2)
            k_raw(3)
            act.wait_ge(qk_mean, 1)
            me.did(act.activation(stat[:, 1, :], stat[:, 0, :], ACT.Sqrt), qk_root)
            for m in range(KA):
                k_spread(m)
            pool_gate(0)
            k_high(0)
            mixed(KA - 1)
            k_high(1)

            def alibi_terms(t):
                h, i = step_of(t)
                n = (i + 1) * P
                if t == 0:
                    act.wait_ge(sel_ok, NT - 1)
                if t >= 2:
                    act.wait_ge(exp_ok, t - 1)
                me.did(act.activation(logit[:, t % 2, 0:n], dsel[:, offset(i):offset(i + 1)], ACT.Copy,
                                      scale=alibi[:, i * H + h:i * H + h + 1]), linear)

            alibi_terms(0)
            k_high(2)
            k_high(3)
            pool_gate(1)
            def gate(n):
                chunk(("ga", n))
                if n == 0:
                    act.wait_ge(used, sch.unit["pb", KD - 1] + 1)
                if n >= 4:
                    act.wait_ge(m_ok, n - 3)
                me.did(act.activation(tga[:, n % 4, :], bank(("ga", n))[:, :], ACT.Tanh, scale=0.5), drained["act"])

            for t in range(SLOTS):
                if t >= 11 and t % (2 * NT) == 3:
                    m = t // (2 * NT) - 1
                    act.wait_ge(pv_ok, 2 * NT * (m + 1))
                    me.did(act.activation(qT[:, 0, m, :], HEADS[m % 2][:, :], ACT.Copy), pair_hi)
                if t < STEPS:
                    if t + 1 < STEPS:
                        alibi_terms(t + 1)
                    h, i = step_of(t)
                    n = (i + 1) * P
                    act.wait_ge(bias_ok, t + 1)
                    if t >= 2:
                        act.wait_ge(prob_t, t - 1)
                    r = i * 2 * H + h
                    me.did(act.activation(prob[:, t % 2, 0:n], logit[:, t % 2, 0:n], ACT.Exp,
                                          bias=sbias[:, t:t + 1], scale=stat[:, 2, r:r + 1],
                                          accum_out=ssum[:, t:t + 1]), exp_ok)
                if 2 <= t < STEPS + 2:
                    n = (step_of(t - 2)[1] + 1) * P
                    act.wait_ge(prob_t, t - 1)
                    if t >= 4:
                        act.wait_ge(pv_ok, t - 3)
                    me.did(act.activation(pT[:, t % 2, 0, 0:n], PT[t % 2][:, 0:n], ACT.Copy), pt_hi)
                if t and filler(t - 1)[1] == "low":
                    kind, m = filler(t - 1)[0]
                    if kind == "gp":
                        pool_gate(m)
                    if kind == "ga":
                        gate(m)
                    if kind == "pb":
                        chunk((kind, m))
            gate(3)

            def load_mid(n):
                j, q = divmod(n, KD // 2)
                if n == 0:
                    act.wait_ge(exp_ok, STEPS)
                if n == 1:
                    act.wait_ge(used, sch.unit["pb", KD - 1] + 1)
                if n >= 2:
                    act.wait_ge(mod_sum, 2 * KD + 2 * (n - 1))
                act.dma_start(ada_mid[n % 2][:, :, :], ada[:, 2 * q:2 * q + 2, (3 + j) * D:(4 + j) * D]
                              ).then_inc(ada_mid_in[n % 2], 16)

            def merged_high(m):
                act.wait_ge(m_ok, m + 1)
                me.did(act.activation(merged[:, 0, m, :], msum[:, m % 2, :], ACT.Copy, scale=0.5), m_hi)

            load_mid(0)
            load_mid(1)
            for m in range(0, KD, 2):
                for n in (m, m + 1):
                    chunk(("ab", n))
                    merged_high(n)
                    if n in (2, 4):
                        load_mid(n // 2 + 1)
                if m + 4 < KD:
                    gate(m + 4)
                    gate(m + 5)

            for m in range(KD):
                chunk(("wo", m))
                await_drained(act, ("wo", m))
                if m == 0:
                    act.wait_ge(m_lo, KD)
                if m >= 3:
                    act.wait_ge(x2_add, m - 2)
                me.did(act.activation(sqsum[:, :] if m == 0 else sq2[:, m % 2, :], xT[:, m, :], ACT.Square), x2_sq)
                if m < 4:
                    load_mid(m + 4)
                if m == KD - 2:
                    me.did(act.activation(tstat[:, 2, 0:1], ones[:, 0:1], ACT.Sqrt))
            act.wait_ge(mean_ok, 2)
            me.did(act.activation(tstat[:, 2, :], tstat[:, 1, :], ACT.Sqrt), root_ok)
            h_high(1, 3)

            def last_tap(kind, m, y):
                col = m if kind == "ua" else KF + m
                chunk((kind, m))
                me.did(act.activation(y[:, m % 2, :], bank((kind, m))[:, :], ACT.Identity,
                                      bias=conv[:, TAPS * 2 * KF + col:TAPS * 2 * KF + col + 1],
                                      scale=conv[:, (TAPS - 1) * 2 * KF + col:(TAPS - 1) * 2 * KF + col + 1]), y_tap)

            def gu_high(m):
                act.wait_ge(g_ok, m + 1)
                me.did(act.activation(guT[:, 0, m, :], ya[:, m % 2, :], ACT.Copy), gu_hi)

            for m in range(KF):
                if m >= 2:
                    act.wait_ge(gu_lo, m - 1)
                last_tap("ua", m, ya)
                if m:
                    gu_high(m - 1)
                last_tap("ub", m, yb)
                await_drained(act, ("ua", m))
                me.did(act.activation(ya[:, m % 2, :], ya[:, m % 2, :], ACT.Silu), silu_ok)
            gu_high(KF - 1)

            for m in range(0, KD, 2):
                for n in range(sch.unit["dn", m] - 4, sch.unit["dn", m] + 2):
                    act.wait_ge(used, n + 1)
                    high_parts(n + 1 + NRING)
                    if m and n == sch.unit["dn", m] - 2:
                        for r in (m - 2, m - 1):
                            store_copy(r)
            for r in (KD - 2, KD - 1):
                store_copy(r)

        @block.vector
        def _(dve):
            me = Progress(dve, dve_step)

            def copy_of(out_ap, in_ap):
                return dve.tensor_copy(out_ap, in_ap)

            def vectors():
                dve.wait_ge(rows_t, 1)
                me.did(copy_of(vec[:, :], OB[:, 0:V_END]))
                me.did(copy_of(conv[:, 0:P], OB[:, P:2 * P]))
                me.did(copy_of(conv[:, P:(TAPS + 1) * 2 * KF], OB[:, 2 * P:(TAPS + 1) * 2 * KF + P]))
                me.settle()
                me.did(dve.tensor_scalar(qgain[:, :], vec[:, V_Q:V_Q + 1], HD ** -0.5, None, ALU.mult), vecs)
                dve.wait_ge(consts, 11)
                me.did(dve.reciprocal(invn[:, :], invn[:, :]))

            def mod_row_of(j, k):
                q, r = divmod(k, 2)
                if j == 1:
                    if r == 0:
                        dve.wait_ge(ada_in[q][j], 16)
                    elif q == KD // 2 - 1:
                        dve.wait_ge(ada_end_in, 16)
                    row = ada_first[q][j][:, r, :]
                elif j in (3, 4):
                    n = (j - 3) * (KD // 2) + q
                    if r == 0:
                        dve.wait_ge(ada_mid_in[n % 2], 16 * (n // 2 + 1))
                    row = ada_mid[n % 2][:, r, :]
                elif j == 5:
                    if r == 0:
                        dve.wait_ge(ada_last_in[q], 16)
                    row = ada_last[q][:, r, :]
                else:
                    item = sch.items.index(("mod", j, q))
                    if r == 0:
                        await_item(dve, item)
                    row = stage[:, item % NSTAGE, r * D:(r + 1) * D]
                if k == 0:
                    if j > 1:
                        dve.wait_ge(mod_col, j - 1)
                    me.did(dve.tensor_scalar(macc[:, :], row, csil[:, 0:1], None, ALU.mult), mod_sum)
                else:
                    dve.wait_ge(mod_sum, KD * (j - 1) + k)
                    me.did(dve.scalar_tensor_tensor(out=macc[:, :], in0=row, scalar=csil[:, k:k + 1],
                                                    in1=macc[:, :], op0=ALU.mult, op1=ALU.add), mod_sum)

            def mod_rows(j, q):
                mod_row_of(j, 2 * q)
                mod_row_of(j, 2 * q + 1)

            def mod_vector(j):
                if j == 0:
                    dve.wait_ge(mod_turn, 1)
                    src = banks[2][:, 0:KD]
                else:
                    dve.wait_ge(mod_col, j)
                    src = (OB if j == 1 else PT[0])[:, MC:MC + KD]
                me.did(dve.tensor_tensor(mod[:, j * KD:(j + 1) * KD], src,
                                         vec[:, V_ADA + j * KD:V_ADA + (j + 1) * KD], ALU.add), mod_ok)
                if j in (1, 4):
                    me.settle()
                    gain = vec[:, V_NORM1:V_NORM1 + KD] if j == 1 else vec[:, V_NORM2:V_NORM2 + KD]
                    me.did(dve.scalar_tensor_tensor(out=gs[:, j // 4, :], in0=mod[:, j * KD:(j + 1) * KD], scalar=1.0,
                                                    in1=gain, op0=ALU.add, op1=ALU.mult))

            def roots(which):
                me.did(dve.tensor_scalar(tstat[:, 1, :], tstat[:, 0, :], 1.0 / D, EPS, ALU.mult, ALU.add), mean_ok)
                dve.wait_ge(root_ok, which + 1)
                me.did(dve.reciprocal(tstat[:, 3, :], tstat[:, 2, :]))
                me.settle()
                for t in range(NT):
                    last = me.did(dve.tensor_scalar(diag[:, t, :], ident[:, :], tstat[:, 3, t:t + 1], None, ALU.mult),
                                  diag_ok)

            def norm(which, shift):
                dve.wait_ge(root_b, which + 1)
                me.settle()

                def low_part(k):
                    dve.wait_ge(h_hi, which * KD + k + 1)
                    me.did(dve.scalar_tensor_tensor(
                        out=hT[:, 1, k, :], in0=nrm[:, k % 2, :], scalar=mod[:, shift * KD + k:shift * KD + k + 1],
                        in1=hT[:, 0, k, :].bitcast(F32), op0=ALU.add, op1=ALU.subtract), h_lo)

                for k in range(KD):
                    if k >= 2:
                        dve.wait_ge(h_lo, which * KD + k - 1)
                    me.did(dve.scalar_tensor_tensor(out=nrm[:, k % 2, :], in0=xT[:, k, :], scalar=gs[:, which, k:k + 1],
                                                    in1=SC[0][:, :], op0=ALU.mult, op1=ALU.mult), n_ok)
                    if k:
                        low_part(k - 1)
                low_part(KD - 1)

            dve.wait_ge(c_silu, 1)
            for k in range(1, KD, 2):
                dve.wait_ge(x_t, k + 1)
                me.did(copy_of(xT[:, k, :], (SC + PT)[k % 4][:, :]), x_kept[1])
                if k == 3:
                    mod_rows(1, 0)
            dve.wait_ge(x_sum, NT)
            roots(0)
            vectors()
            for q in range(1, KD // 2):
                mod_rows(1, q)
            mod_vector(1)
            mod_vector(0)
            dve.wait_ge(x_kept[0], KD // 2)
            norm(0, 0)

            def low_of(out_ap, full, hi, signal):
                me.did(dve.tensor_tensor(out_ap, full, hi.bitcast(F32), ALU.subtract), signal)

            for m in range(2):
                dve.wait_ge(part_hi, m + 1)
                low_of(qiT[:, 1, m, :], bank(("qi", m))[:, :], qiT[:, 0, m, :], drained["dve"])
            dve.wait_ge(part_hi, 4)
            b = bank(("kw", 0))
            me.did(dve.tensor_tensor(kiT[HD:P, 1, :], b[0:HD, :], kiT[0:HD, 0, :].bitcast(F32), ALU.subtract))
            low_of(kiT[0:HD, 1, :], b[0:HD, :], kiT[0:HD, 0, :], drained["dve"])
            dve.wait_ge(wi_t, 1)
            me.did(dve.tensor_scalar(wi[:, :], OB[:, WC:WC + NT * IH], IH ** -0.5, None, ALU.mult), wi_ok)

            def row_of(tensor, i):
                return tensor[:, offset(i) - P:offset(i + 1) - P]

            def index_sum(n):
                i, h = n // IH + 1, n % IH
                acc = row_of(iscore, i)
                dve.wait_ge(i_relu, n + 1)
                me.settle()
                w = wi[:, i * IH + h:i * IH + h + 1]
                r = relu[:, n % 2, 0:(i + 1) * P]
                if h == 0:
                    me.did(dve.tensor_scalar(acc, r, w, None, ALU.mult), i_sum)
                else:
                    me.did(dve.scalar_tensor_tensor(out=acc, in0=r, scalar=w, in1=acc, op0=ALU.mult, op1=ALU.add),
                           i_sum)
                if h == IH - 1:
                    me.settle()
                    me.did(dve.tensor_tensor(acc[:, i * P:], acc[:, i * P:], cap[:, :], ALU.min))

            rounds = [0]

            def top_rounds(n):
                for _ in range(n):
                    src = work if rounds[0] else iscore
                    me.settle()
                    found = [me.did(dve.max(top8[:, i, :], row_of(src, i))) for i in range(1, NT)]
                    for i in range(1, NT):
                        me.settle(found[i - 1])
                        me.did(dve.match_replace(out=row_of(work, i), in_to_replace=top8[:, i, :],
                                                 in_values=row_of(src, i), imm_value=TAKEN))
                    rounds[0] += 1

            for n in range(KA):
                for k in index_steps(n)[:3]:
                    index_sum(k)
                dve.wait_ge(part_hi, 4 + n + 1)
                me.did(dve.scalar_tensor_tensor(out=qT[:, 1, n, :], in0=bank(("q", n))[:, :], scalar=qgain[:, 0:1],
                                                in1=qT[:, 0, n, :].bitcast(F32), op0=ALU.mult, op1=ALU.subtract),
                       drained["dve"])
                for k in index_steps(n)[3:]:
                    index_sum(k)

            def v_low(m):
                dve.wait_ge(v_hi, m + 1)
                low_of(vS[:, :, 1, 2 * m:2 * m + 2, :], PT[m % 2][:, :].rearrange("p (t h d) -> p t h d", t=NT, h=2),
                       vS[:, :, 0, 2 * m:2 * m + 2, :], v_lo)

            def mixed(g):
                dve.wait_ge(part_hi, 4 + KA + g + 1)
                me.did(dve.scalar_tensor_tensor(out=mix[:, 1, g, :], in0=bank(("mg", g))[:, :],
                                                scalar=vec[:, V_POOL + g:V_POOL + g + 1],
                                                in1=mix[:, 0, g, :].bitcast(F32),
                                                op0=ALU.mult, op1=ALU.subtract), drained["dve"])

            def pool_mean(g):
                window = WINDOWS[g]
                src, own, mean = wsum[g % 2], u[g % 2], pmean[g % 2]
                dve.wait_ge(w_ok, g + 1)
                if g >= 2:
                    dve.wait_ge(p_lo, g - 1)
                me.did(dve.scalar_tensor_tensor(out=mean[:, window - 1:], in0=src[:, PAD + window - 1:],
                                                scalar=1.0 / window, in1=own[:, PAD + window - 1:],
                                                op0=ALU.mult, op1=ALU.subtract))
                me.did(dve.tensor_tensor(mean[:, 0:window - 1], src[:, PAD:PAD + window - 1], invn[:, 0:window - 1],
                                         ALU.mult))
                me.settle()
                me.did(dve.tensor_tensor(mean[:, 0:window - 1], mean[:, 0:window - 1], own[:, PAD:PAD + window - 1],
                                         ALU.subtract), p_ok)

            def k_normed(m):
                dve.wait_ge(kroot_t, m + 1)
                me.did(dve.scalar_tensor_tensor(out=kraw[:, m, :], in0=kraw[:, m, :], scalar=vec[:, V_K:V_K + 1],
                                                in1=(SC + PT)[m][:, :], op0=ALU.mult, op1=ALU.mult), kn_ok)

            top_rounds(4)
            pool_mean(0)
            top_rounds(2)
            pool_mean(1)
            top_rounds(2)
            pool_mean(2)
            top_rounds(2)
            pool_mean(3)
            for m in range(3):
                top_rounds(1)
                v_low(m)
            v_low(3)
            for m in range(2):
                top_rounds(1)
                mixed(m)
            top_rounds(TOPK // 8 - rounds[0])
            me.settle()
            for i in range(1, NT):
                me.did(dve.tensor_scalar(dsel[:, offset(i):offset(i + 1)], row_of(work, i), TAKEN_BELOW, BIG,
                                         ALU.is_gt, ALU.mult))
            me.settle()
            for i in range(1, NT):
                me.did(dve.tensor_tensor(dsel[:, offset(i):offset(i + 1)], dsel[:, offset(i):offset(i + 1)],
                                         dist[:, (NT - 1 - i) * P:S], ALU.add), sel_ok)
            mixed(2)
            dve.wait_ge(sq_used, 2 * KA)
            me.did(dve.tensor_scalar(stat[:, 0, :], OB[:, 0:NT * 2 * H], 1.0 / HD, EPS, ALU.mult, ALU.add), qk_mean)
            dve.wait_ge(qk_root, 1)
            me.did(dve.reciprocal(stat[:, 2, :], stat[:, 1, :]), qk_inv)
            for h in range(H):
                me.did(dve.tensor_scalar(alibi[:, :].rearrange("p (t h) -> p h t", h=H)[:, h, :],
                                         stat[:, 1, :].rearrange("p (t h) -> p h t", h=2 * H)[:, h, :],
                                         -slope(h), None, ALU.mult))
            k_normed(0)
            mixed(KA - 1)
            k_normed(1)
            k_normed(2)
            k_normed(3)

            for t in range(SLOTS):
                if t < STEPS:
                    h, i = step_of(t)
                    n = (i + 1) * P
                    dve.wait_ge(linear, t + 1)
                    dve.wait_ge(score, t + 1)
                    me.did(dve.tensor_tensor_reduce(logit[:, t % 2, 0:n], logit[:, t % 2, 0:n], SC[t % 2][:, 0:n],
                                                    1.0, TAKEN, ALU.add, ALU.max, smax[:, t:t + 1]), logit_ok)
                    me.settle()
                    r = i * 2 * H + h
                    me.did(dve.tensor_scalar(sbias[:, t:t + 1], smax[:, t:t + 1], stat[:, 2, r:r + 1], -1.0,
                                             ALU.mult, ALU.mult), bias_ok)
                if 1 <= t < STEPS + 1:
                    n = (step_of(t - 1)[1] + 1) * P
                    dve.wait_ge(exp_ok, t)
                    me.did(dve.reciprocal(sinv[:, t - 1:t], ssum[:, t - 1:t]))
                    me.settle()
                    me.did(dve.tensor_scalar(prob[:, (t - 1) % 2, 0:n], prob[:, (t - 1) % 2, 0:n],
                                             sinv[:, t - 1:t], None, ALU.mult), prob_ok)
                if 2 <= t < STEPS + 2:
                    n = (step_of(t - 2)[1] + 1) * P
                    dve.wait_ge(pt_hi, t - 1)
                    low_of(pT[:, t % 2, 1, 0:n], PT[t % 2][:, 0:n], pT[:, t % 2, 0, 0:n], pt_lo)
                if t >= 11 and t % (2 * NT) == 3:
                    m = t // (2 * NT) - 1
                    dve.wait_ge(pair_hi, m + 1)
                    low_of(qT[:, 1, m, :], HEADS[m % 2][:, :], qT[:, 0, m, :], pair_lo)
                if t and filler(t - 1)[1] == "low" and filler(t - 1)[0][0] == "pb":
                    name = filler(t - 1)[0]
                    m = name[1]
                    await_chunk(dve, name)
                    dve.wait_ge(drained["act"], drained_count[sch.chunk["gp", m]][1])
                    me.did(dve.scalar_tensor_tensor(out=ypool[:, m, :], in0=ypool[:, m, :], scalar=1.0,
                                                    in1=bank(name)[:, :], op0=ALU.add, op1=ALU.mult),
                           drained["dve"])
            mod_vector(2)

            def merged_low(m):
                dve.wait_ge(m_hi, m + 1)
                me.did(dve.scalar_tensor_tensor(out=merged[:, 1, m, :], in0=msum[:, m % 2, :], scalar=0.5,
                                                in1=merged[:, 0, m, :].bitcast(F32), op0=ALU.mult, op1=ALU.subtract),
                       m_lo)

            for m in range(KD):
                if m:
                    merged_low(m - 1)
                await_chunk(dve, ("ab", m))
                dve.wait_ge(drained["act"], drained_count[sch.chunk["ga", m]][1])
                if m >= 2:
                    dve.wait_ge(m_lo, m - 1)
                me.did(dve.scalar_tensor_tensor(out=msum[:, m % 2, :], in0=tga[:, m % 4, :], scalar=1.0,
                                                in1=bank(("ab", m))[:, :], op0=ALU.add, op1=ALU.mult), drained["dve"])
                me.settle()
                me.did(dve.tensor_tensor(msum[:, m % 2, :], msum[:, m % 2, :], ypool[:, m, :], ALU.add), m_ok)
                if m in (1, 3):
                    mod_rows(3, m // 2)
            merged_low(KD - 1)
            mod_rows(3, 2)

            for m in range(KD):
                await_chunk(dve, ("wo", m))
                me.did(dve.scalar_tensor_tensor(out=xT[:, m, :], in0=bank(("wo", m))[:, :],
                                                scalar=mod[:, 2 * KD + m:2 * KD + m + 1], in1=xT[:, m, :],
                                                op0=ALU.mult, op1=ALU.add), drained["dve"])
                if m == 0:
                    mod_rows(3, 3)
                if m == 1:
                    mod_vector(3)
                if m in (1, 2, 4, 5):
                    mod_rows(4, (1, 2, 4, 5).index(m))
            mod_vector(4)
            dve.wait_ge(x2_sum, 2)
            me.did(dve.tensor_reduce(tstat[:, 0, :], OB[:, 0:2 * NT].rearrange("p (m t) -> p t m", t=NT), AX_X,
                                     ALU.add))
            me.settle()
            roots(1)
            norm(1, 3)

            def first_taps(kind, m, y):
                col = m if kind == "ua" else KF + m
                dve.wait_ge(y_tap, 2 * m + (1 if kind == "ua" else 2))
                for back in (1, 2):
                    if back == 2:
                        me.settle()
                    w = conv[:, (TAPS - 1 - back) * 2 * KF + col:(TAPS - 1 - back) * 2 * KF + col + 1]
                    me.did(dve.scalar_tensor_tensor(out=y[:, m % 2, back:], in0=bank((kind, m))[:, 0:S - back],
                                                    scalar=w, in1=y[:, m % 2, back:], op0=ALU.mult, op1=ALU.add),
                           drained["dve"] if back == 2 else None)

            def gu_low(m):
                dve.wait_ge(gu_hi, m + 1)
                low_of(guT[:, 1, m, :], ya[:, m % 2, :], guT[:, 0, m, :], gu_lo)

            for m in range(KF):
                first_taps("ua", m, ya)
                if m:
                    gu_low(m - 1)
                first_taps("ub", m, yb)
                dve.wait_ge(silu_ok, m + 1)
                me.settle()
                me.did(dve.tensor_tensor(ya[:, m % 2, :], ya[:, m % 2, :], yb[:, m % 2, :], ALU.mult), g_ok)
                if 4 <= m < 4 + KD:
                    mod_row_of(5, m - 4)
                if m == 4 + KD:
                    mod_vector(5)
            gu_low(KF - 1)
            for m in range(KD):
                await_chunk(dve, ("dn", m))
                me.did(dve.scalar_tensor_tensor(out=xT[:, m, :], in0=bank(("dn", m))[:, :],
                                                scalar=mod[:, 5 * KD + m:5 * KD + m + 1], in1=xT[:, m, :],
                                                op0=ALU.mult, op1=ALU.add), drained["dve"])

        @block.tensor
        def _(pe):
            def high_products(n, out_bank, rhs, k0=0, first=True, ks=None):
                hi = unit_split(n, 0)
                pe.wait_ge(high, n + 1)
                for k in ks or range(sch.units[n][0]):
                    for part in range(2):
                        pe.matmul(out_bank[:, :], hi[:, k, :], rhs[:, part, k0 + k, :],
                                  start=first and k == 0 and part == 0, stop=False)

            def low_products(n, out_bank, rhs, k0=0, last=True, ks=None):
                nk = sch.units[n][0]
                lo = unit_split(n, 1)
                pe.wait_ge(low, n + 1)
                for k in ks or range(nk):
                    mm = pe.matmul(out_bank[:, :], lo[:, k, :], rhs[:, 0, k0 + k, :], start=False,
                                   stop=last and k == nk - 1)
                    if k == nk - 1:
                        mm.then_inc(used, 1)

            def product(name, rhs):
                await_bank(pe, name)
                high_products(sch.unit[name], bank(name), rhs)
                low_products(sch.unit[name], bank(name), rhs)

            def first_products(names, which, lag):
                for name in names:
                    await_bank(pe, name)
                    pe.wait_ge(high, sch.unit[name] + 1)
                for k in range(KD + lag):
                    if k < KD:
                        for part, made in enumerate((h_hi, h_lo)):
                            pe.wait_ge(made, which * KD + k + 1)
                            for name in names:
                                pe.matmul(bank(name)[:, :], unit_split(sch.unit[name], 0)[:, k, :], hT[:, part, k, :],
                                          start=k == 0 and part == 0, stop=False)
                    if k >= lag:
                        for name in names:
                            pe.wait_ge(low, sch.unit[name] + 1)
                            mm = pe.matmul(bank(name)[:, :], unit_split(sch.unit[name], 1)[:, k - lag, :],
                                           hT[:, 0, k - lag, :], start=False, stop=k == KD + lag - 1)
                            if k == KD + lag - 1:
                                mm.then_inc(used, 1)

            pe.wait_ge(consts, 11)
            pe.wait_ge(c_in, 16)
            pe.transpose(banks[2][:, 0:KD], crow[:, :], ident[0:KD, 0:KD]).then_inc(c_t, 1)
            pe.wait_ge(x_in, 16 * NT)
            for k in range(KD):
                if k >= 4:
                    pe.wait_ge(x_kept[k % 2], (k - 4) // 2 + 1)
                for t in range(NT):
                    mm = pe.transpose((SC + PT)[k % 4][:, t * P:(t + 1) * P], xn[:, t, k * P:(k + 1) * P],
                                      ident[:, :])
                mm.then_inc(x_t, 1)

            def spread_roots(which):
                pe.wait_ge(diag_ok, NT * (which + 1))
                for t in range(NT):
                    mm = pe.matmul(SC[0][:, t * P:(t + 1) * P], ones[:, :], diag[:, t, :], start=True, stop=True)
                mm.then_inc(root_b, 1)

            def keep_clock(n, weights, moving):
                for _ in range(n):
                    pe.matmul(PT[1][:, :], weights, moving, start=True, stop=True)

            def row_products(q, rows_q, out_banks):
                for k in (2 * q, 2 * q + 1):
                    for half in range(2):
                        mm = pe.matmul(out_banks[half][0:1, :], csil[:, k:k + 1],
                                       rows_q[:, k % 2, half * S:(half + 1) * S], start=k == 0, stop=k == KD - 1)
                if q == KD // 2 - 1:
                    mm.then_inc(mod_first, 1)

            def row_turn(row, out_bank, n):
                pe.wait_ge(mod_row, 2 * n)
                for k in range(KD):
                    mm = pe.matmul(out_bank[:, k:k + 1], row[:, k * P:(k + 1) * P], ones[0:1, 0:1],
                                   start=True, stop=True)
                mm.then_inc(mod_turn, 1)

            def mod_columns(j):
                pe.wait_ge(mod_sum, KD * j)
                out_bank = OB if j == 1 else PT[0]
                if j == 1:
                    pe.wait_ge(vecs, 1)
                else:
                    pe.wait_ge(mod_ok, j)
                for k in range(KD):
                    mm = pe.matmul(out_bank[:, MC + k:MC + k + 1], macc[:, k * P:(k + 1) * P], ones[:, 0:1],
                                   start=True, stop=True)
                mm.then_inc(mod_col, 1)

            pe.wait_ge(x_kept[0], KD // 2)
            pe.wait_ge(c_silu, 1)
            pe.wait_ge(ada_in[0][0], 16)
            row_products(0, ada_first[0][0], banks[0:2])
            pe.wait_ge(rows_in, 16 * ROW_LOADS)
            pe.transpose(OB[:, 0:V_END], rows[0:V_END, 0, :], ident[0:V_END, 0:V_END])
            pe.transpose(OB[:, P:2 * P], rows[:, 1, :], ident[:, :])
            left = (TAPS + 1) * 2 * KF - P
            pe.transpose(OB[:, 2 * P:2 * P + left], rows[0:left, 2, :], ident[0:left, 0:left]).then_inc(rows_t, 1)
            spread_roots(0)
            for q in range(1, KD // 2):
                pe.wait_ge(ada_in[q][0], 16)
                row_products(q, ada_first[q][0], banks[0:2])
            mod_columns(1)
            row_turn(mrow, banks[2], 1)
            pe.wait_ge(mod_ok, 2)
            first_products((("qi", 0), ("qi", 1)), 0, 2)
            product(("kw", 0), hT)
            def wi_turn():
                pe.wait_ge(wi_row, 1)
                for t in range(NT):
                    mm = pe.transpose(OB[:, WC + t * IH:WC + (t + 1) * IH], wiT[0:IH, t * P:(t + 1) * P],
                                      ident[0:IH, 0:IH])
                mm.then_inc(wi_t, 1)

            THREE = ((0, 0), (0, 1), (1, 0))

            def index_dot(n):
                i, h = n // IH + 1, n % IH
                if n == 0:
                    await_drained(pe, ("kw", 0))
                if n >= 2:
                    pe.wait_ge(i_relu, n - 1)
                r = slice((h % 2) * HD, (h % 2 + 1) * HD)
                for a, b in THREE:
                    mm = pe.matmul(SC[n % 2][:, 0:(i + 1) * P], qiT[r, a, h // 2, i * P:(i + 1) * P],
                                   kiT[r, b, 0:(i + 1) * P], start=(a, b) == (0, 0), stop=a == 1)
                mm.then_inc(i_dot, 1)

            def squares(n):
                pe.wait_ge(sq_ok, n + 1)
                if n == 0:
                    pe.wait_ge(wi_ok, 1)
                for t in range(NT):
                    mm = pe.matmul(OB[:, t * 2 * H + 2 * n:t * 2 * H + 2 * n + 2], sq[:, n % 2, t * P:(t + 1) * P],
                                   halves[:, :], start=True, stop=True)
                mm.then_inc(sq_used, 1)

            def halves_of(products, name, steps):
                for n in range(2):
                    products(sch.unit[name], bank(name), hT, ks=range(n * KD // 2, (n + 1) * KD // 2))
                    index_dot(steps[n])

            for n in range(KA):
                if n == 0:
                    product(("q", n), hT)
                    wi_turn()
                else:
                    await_bank(pe, ("q", n))
                    halves_of(high_products, ("q", n), index_steps(n)[:2])
                    halves_of(low_products, ("q", n), index_steps(n)[2:])
                    squares(n - 1)

            def v_turn(m):
                pe.wait_ge(drained["act"], drained_count[sch.chunk["v", m]][1])
                if m >= 2:
                    pe.wait_ge(v_lo, m - 1)
                for t in range(NT):
                    mm = pe.transpose(PT[m % 2][:, t * P:(t + 1) * P], vraw[:, m % 2, t * P:(t + 1) * P], ident[:, :])
                mm.then_inc(v_t, 1)

            def k_turn(m):
                pe.wait_ge(kroot_ok, m + 1)
                if m >= 2:
                    pe.wait_ge(v_lo, m + 1)
                for t in range(NT):
                    mm = pe.transpose((SC + PT)[m][:, t * P:(t + 1) * P], kroot[:, m, t * P:(t + 1) * P], ident[:, :])
                mm.then_inc(kroot_t, 1)

            def group(g):
                pe.wait_ge(p_lo, g + 1)
                product(("mg", g), pooled[g % 2][:, :, :].rearrange("p a (k n) -> p a k n", k=1))

            product(("u", 0), hT)
            squares(KA - 1)
            for g in range(1, KA):
                product(("u", g), hT)
            product(("v", 0), hT)
            for m in range(1, KA):
                product(("v", m), hT)
                v_turn(m - 1)
            product(("k", 0), hT)
            v_turn(KA - 1)
            for m in range(1, KA):
                group(m - 1)
                product(("k", m), hT)
                squares(KA + m - 1)
            await_bank(pe, ("gp", 0))
            high_products(sch.unit["gp", 0], bank(("gp", 0)), hT)
            squares(2 * KA - 1)
            low_products(sch.unit["gp", 0], bank(("gp", 0)), hT)
            group(KA - 1)
            k_turn(0)
            k_turn(1)
            await_bank(pe, ("gp", 1))
            high_products(sch.unit["gp", 1], bank(("gp", 1)), hT)
            k_turn(2)
            k_turn(3)
            low_products(sch.unit["gp", 1], bank(("gp", 1)), hT)

            for t in range(SLOTS):
                if t < STEPS:
                    h, i = step_of(t)
                    r = slice((h % 2) * HD, (h % 2 + 1) * HD)
                    if t % (2 * NT) == 0:
                        pe.wait_ge(k_lo, h // 2 + 1)
                    if t < 2:
                        pe.wait_ge(kn_ok, t + 1)
                    else:
                        pe.wait_ge(logit_ok, t - 1)
                    for a, b in THREE:
                        mm = pe.matmul(SC[t % 2][:, 0:(i + 1) * P], qT[r, a, h // 2, i * P:(i + 1) * P],
                                       kT[r, b, h // 2, 0:(i + 1) * P], start=(a, b) == (0, 0), stop=a == 1)
                    mm.then_inc(score, 1)
                if 2 <= t < STEPS + 2:
                    i = step_of(t - 2)[1]
                    pe.wait_ge(prob_ok, t - 1)
                    if t < 4:
                        pe.wait_ge(kn_ok, t + 1)
                    else:
                        pe.wait_ge(pt_lo, t - 3)
                    for j in range(i + 1):
                        mm = pe.transpose(PT[t % 2][:, j * P:(j + 1) * P], prob[:, t % 2, j * P:(j + 1) * P],
                                          ident[:, :])
                    mm.then_inc(prob_t, 1)
                if filler(t):
                    name, part = filler(t)
                    if part == "high":
                        await_bank(pe, name)
                    (high_products if part == "high" else low_products)(
                        sch.unit[name], bank(name), mix if name[0] == "pb" else hT)
                if 3 <= t < STEPS + 3:
                    h, i = step_of(t - 3)
                    pe.wait_ge(pt_lo, t - 2)
                    pair, m = h // 2, P if h % 2 else HD
                    if (t - 3) % (2 * NT) == 0:
                        if pair == 1:
                            who, n = drained_count[max(k for k in range(sch.chunk[FILLERS[0]]) if sch.bank[k] == 2)]
                            pe.wait_ge(drained[who], n)
                        if pair > 1:
                            pe.wait_ge(pair_lo, pair - 1)
                    for j in range(i + 1):
                        for a, b in THREE:
                            v = vS[:, j, a, 2 * pair:2 * pair + 2, :].rearrange("p h d -> p (h d)")
                            mm = pe.matmul(HEADS[pair % 2][0:m, i * P:(i + 1) * P], v[:, 0:m],
                                           pT[:, (t - 1) % 2, b, j * P:(j + 1) * P],
                                           start=j == 0 and (a, b) == (0, 0), stop=j == i and a == 1)
                    mm.then_inc(pv_ok, 1)
            mod_columns(2)
            pe.wait_ge(pair_lo, NPAIR)
            for m in range(0, KD, 2):
                for n in (m, m + 1):
                    product(("ab", n), qT)
                if m + 4 < KD:
                    for n in (m + 4, m + 5):
                        product(("ga", n), hT)

            def token_squares(part):
                if part == 0:
                    pe.wait_ge(x2_add, KD - 2)
                    src = sqsum[:, :]
                else:
                    pe.wait_ge(x2_sq, KD)
                    src = sq2[:, (KD - 1) % 2, :]
                for t in range(NT):
                    mm = pe.matmul(OB[:, part * NT + t:part * NT + t + 1], src[:, t * P:(t + 1) * P], ones[:, 0:1],
                                   start=True, stop=True)
                mm.then_inc(x2_sum, 1)

            first = ("wo", 0)
            await_bank(pe, first)
            for ks in (range(KD - 1), range(KD - 1, KD)):
                pe.wait_ge(m_lo, ks.stop)
                high_products(sch.unit[first], bank(first), merged, ks=ks)
                low_products(sch.unit[first], bank(first), merged, ks=ks)
            for m in range(1, KD - 1):
                product(("wo", m), merged)
                if m == 1:
                    mod_columns(3)
            mod_columns(4)
            final = ("wo", KD - 1)
            await_bank(pe, final)
            high_products(sch.unit[final], bank(final), merged)
            token_squares(0)
            low_products(sch.unit[final], bank(final), merged)
            keep_clock(6, qT[:, 0, 0, 0:P], qT[:, 0, 1, :])
            token_squares(1)
            keep_clock(6, qT[:, 0, 0, 0:P], qT[:, 0, 1, :])
            spread_roots(1)
            keep_clock(6, qT[:, 0, 0, 0:P], qT[:, 0, 1, :])

            for m in range(KF):
                if m == 0:
                    first_products((("ua", 0), ("ub", 0)), 1, 0)
                else:
                    product(("ua", m), hT)
                    product(("ub", m), hT)
                if m == 4 + KD:
                    mod_columns(5)

            def out_turn(m):
                pe.wait_ge(drained["dve"], drained_count[sch.chunk["dn", m]][1])
                if m >= 2:
                    pe.wait_ge(out_ok, m - 1)
                for t in range(NT):
                    mm = pe.transpose(PT[m % 2][:, t * P:(t + 1) * P], xT[:, m, t * P:(t + 1) * P], ident[:, :])
                mm.then_inc(out_t, 1)

            for m in range(0, KD, 2):
                n = sch.unit["dn", m] - 4
                for k0 in range(0, KF, KD):
                    pe.wait_ge(gu_lo, min(k0 + KD, KF))
                    for half in range(2):
                        if k0 == 0:
                            await_bank(pe, ("dn", m + half))
                        high_products(n, bank(("dn", m + half)), guT, k0, k0 == 0)
                        low_products(n, bank(("dn", m + half)), guT, k0, k0 + KD >= KF)
                        n += 1
                    if m and k0 == 0:
                        out_turn(m - 2)
                        out_turn(m - 1)
            out_turn(KD - 2)
            out_turn(KD - 1)


_INS = ['x', 'c', 'w_ada', 'b_ada', 'norm1_g', 'w_in', 'q_norm_g', 'k_norm_g', 'w_attn_br', 'w_pool_grp', 'pool_scale',
        'w_pool_br', 'w_out', 'norm2_g', 'w_up', 'conv_w', 'conv_b', 'w_down']
_OUTS = [((1, 512, 1024), 'float32')]


def kernel(**inputs):
    import numpy as _np
    import concourse.bacc as _bacc
    from concourse import mybir as _mybir
    from concourse.bass_utils import run_bass_kernel_spmd as _run

    nc = _bacc.Bacc("TRN2", target_bir_lowering=False, num_devices=1)
    arrays, args = {}, []
    for name in _INS:
        a = _np.ascontiguousarray(inputs[name])
        arrays[f"in_{name}_dram"] = a
        args.append(nc.dram_tensor(f"in_{name}_dram", a.shape, _mybir.dt.from_np(a.dtype), kind="ExternalInput").ap())
    for i, (shape, dtype) in enumerate(_OUTS):
        dt = _mybir.dt.from_np(_np.dtype(dtype))
        args.append(nc.dram_tensor(f"out_{i}_dram", shape, dt, kind="ExternalOutput").ap())
    build_layer(nc, *args)
    r = _run(nc, [arrays], core_ids=[0])
    got = tuple(r.results[0][f"out_{i}_dram"] for i in range(len(_OUTS)))
    return got[0]
```
